# Optimizing a Trainium2 kernel written in Bass

```python
import jax, jax.numpy as jnp
from jax import lax
import numpy as np

"""Hybrid streaming encoder trunk: one inference step of DEPTH layers for two request groups.

Per layer (post-norm with DeepNorm residual scaling alpha = (2*DEPTH)^(1/4)):
  z = x @ w_in, columns = [rnn stream | q | k | v | rnn gate | attn gate]
  branch A: causal depthwise conv (width 4) -> RG-LRU (per-token linear recurrence)
  branch B: rotary GQA over a chunk-banded sliding window (own chunk + 2 previous chunks) with per-head sinks
  m = sigmoid(g_rnn) * (A @ w_br_rnn) + sigmoid(g_attn) * (B @ w_br_attn)
  x = LayerNorm(alpha * x + m @ w_out)
  x = LayerNorm(alpha * x + shared_expert(x) + sum_{top-k} gate_e * expert_e(x))

Inputs:
  x_prompt   (BATCH, SEQ, D_MODEL)          first SEQ frames of new streams, positions 0..SEQ-1
  x_sample   (DEC_BATCH, DEC_SEQ, D_MODEL)  next frames, positions PAST_LEN..PAST_LEN+DEC_SEQ-1
  cache_k, cache_v (DEPTH, DEC_BATCH, min(WINDOW, PAST_LEN), N_KV_HEADS, HEAD_DIM)  rotated keys / values of newest rows
  state_h    (DEPTH, DEC_BATCH, D_RNN)               RG-LRU hidden state
  state_conv (DEPTH, DEC_BATCH, CONV_W - 1, D_RNN)   last conv input rows
  weights stacked on a leading DEPTH axis.
Returns (y_prompt, y_sample, k_prompt, v_prompt, h_prompt, conv_prompt, k_sample, v_sample, h_sample, conv_sample):
  y_prompt (BATCH, SEQ, D_MODEL); y_sample (DEC_BATCH, DEC_SEQ, D_MODEL)
  k_prompt, v_prompt (DEPTH, BATCH, min(WINDOW, SEQ), N_KV_HEADS, HEAD_DIM)
  h_prompt (DEPTH, BATCH, D_RNN); conv_prompt (DEPTH, BATCH, CONV_W - 1, D_RNN)
  k_sample, v_sample (DEPTH, DEC_BATCH, DEC_SEQ, N_KV_HEADS, HEAD_DIM)  new rows
  h_sample (DEPTH, DEC_BATCH, D_RNN); conv_sample (DEPTH, DEC_BATCH, CONV_W - 1, D_RNN)
"""

D_MODEL = 1024
BATCH = 1
SEQ = 256
DEPTH = 2
DEC_BATCH = 1
DEC_SEQ = 32
PAST_LEN = 256

CHUNK = 64
D_RNN = D_MODEL
RNN_BLOCKS = 16
RNN_BW = D_RNN // RNN_BLOCKS
CONV_W = 4
RG_C = 8.0
HEAD_DIM = 64
N_Q_HEADS = D_MODEL // HEAD_DIM
N_KV_HEADS = 2
GQA = N_Q_HEADS // N_KV_HEADS
WINDOW = 128
WIN_CHUNKS = WINDOW // CHUNK
ROPE_THETA = 10000.0
N_EXPERTS = 64
TOP_K = 8
N_GROUPS = 8
TOPK_GROUPS = 4
D_EXPERT = 256
D_SHARED = 256
ROUTED_SCALE = 2.5
MOE_BLOCK = 128
DN_ALPHA = (2 * DEPTH) ** 0.25
DN_BETA = (8 * DEPTH) ** -0.25
LN_EPS = 1e-5
Q_OFF = D_RNN
K_OFF = Q_OFF + N_Q_HEADS * HEAD_DIM
V_OFF = K_OFF + N_KV_HEADS * HEAD_DIM
GR_OFF = V_OFF + N_KV_HEADS * HEAD_DIM
GA_OFF = GR_OFF + D_MODEL
IN_COLS = GA_OFF + D_MODEL

kernel_name = 'hawk_swa_moe_streaming_step'

def _layernorm(x, g, b):
    xf = x.astype(jnp.float32)
    mu = jnp.mean(xf, -1, keepdims=True)
    var = jnp.mean(jnp.square(xf - mu), -1, keepdims=True)
    return ((xf - mu) * lax.rsqrt(var + LN_EPS) * g.astype(jnp.float32) + b.astype(jnp.float32)).astype(x.dtype)

def _rope(t, pos):
    half = HEAD_DIM // 2
    inv = jnp.power(ROPE_THETA, -jnp.arange(half, dtype=jnp.float32) / half)
    ang = pos.astype(jnp.float32)[:, None] * inv[None, :]
    cos = jnp.cos(ang)[None, :, None, :]
    sin = jnp.sin(ang)[None, :, None, :]
    tf = t.astype(jnp.float32)
    t1, t2 = tf[..., :half], tf[..., half:]
    return jnp.concatenate([t1 * cos - t2 * sin, t2 * cos + t1 * sin], -1).astype(t.dtype)

def _lin_combine(left, right):
    a1, b1 = left
    a2, b2 = right
    return a1 * a2, a2 * b1 + b2

def _rglru(xr, conv_buf, h0, conv_w, conv_b, w_a, b_a, w_x, b_x, a_param, first_reset):
    B, T, _ = xr.shape
    xc = jnp.concatenate([conv_buf.astype(xr.dtype), xr], axis=1)
    u = sum((xc[:, j:j + T] * conv_w[j] for j in range(CONV_W)), conv_b)
    new_buf = xc[:, T:]
    ub = u.reshape(B, T, RNN_BLOCKS, RNN_BW)
    gx = jax.nn.sigmoid((jnp.einsum('btnc,ncd->btnd', ub, w_x).reshape(B, T, D_RNN) + b_x).astype(jnp.float32))
    ga = jax.nn.sigmoid((jnp.einsum('btnc,ncd->btnd', ub, w_a).reshape(B, T, D_RNN) + b_a).astype(jnp.float32))
    log_a = -RG_C * ga * jax.nn.softplus(-a_param.astype(jnp.float32))
    a = jnp.exp(log_a)
    mult = jnp.sqrt(-jnp.expm1(2.0 * log_a))
    if first_reset:
        mult = mult.at[:, 0].set(1.0)
    b = mult * gx * u.astype(jnp.float32)
    b = b.at[:, 0].add(a[:, 0] * h0.astype(jnp.float32))
    _, h = lax.associative_scan(_lin_combine, (a, b), axis=1)
    return h.astype(xr.dtype), h[:, -1].astype(h0.dtype), new_buf

def _sink_softmax(s, sinks):
    sk = jnp.broadcast_to(sinks.astype(jnp.float32).reshape(N_KV_HEADS, GQA, 1, 1), s.shape[:-1] + (1,))
    p = jax.nn.softmax(jnp.concatenate([s, sk], -1), axis=-1)
    return p[..., :-1]

def _attn_prompt(q, k, v, sinks):
    B, S = q.shape[:2]
    NC = S // CHUNK
    pad = WIN_CHUNKS * CHUNK
    KB = (WIN_CHUNKS + 1) * CHUNK
    qc = q.reshape(B, NC, CHUNK, N_KV_HEADS, GQA, HEAD_DIM)

    def band(t):
        tp = jnp.concatenate([jnp.zeros((B, pad) + t.shape[2:], t.dtype), t], 1)
        tp = tp.reshape(B, NC + WIN_CHUNKS, CHUNK, N_KV_HEADS, HEAD_DIM)
        return jnp.concatenate([tp[:, j:j + NC] for j in range(WIN_CHUNKS + 1)], axis=2)

    kb, vb = band(k), band(v)
    kpos = jnp.arange(NC)[:, None] * CHUNK + jnp.arange(KB)[None, :] - pad
    valid = (kpos >= 0)[None, :, None, None, None, :]
    s = jnp.einsum('bnqkgd,bnskd->bnkgqs', qc, kb).astype(jnp.float32) * (HEAD_DIM ** -0.5)
    s = jnp.where(valid, s, -jnp.inf)
    p = _sink_softmax(s, sinks).astype(v.dtype)
    o = jnp.einsum('bnkgqs,bnskd->bnqkgd', p, vb)
    return o.reshape(B, S, N_Q_HEADS * HEAD_DIM)

def _attn_sample(q, k_all, v_all, sinks):
    B, T = q.shape[:2]
    qg = q.reshape(B, T, N_KV_HEADS, GQA, HEAD_DIM)
    s = jnp.einsum('btkgd,bskd->bkgts', qg, k_all).astype(jnp.float32) * (HEAD_DIM ** -0.5)
    p = _sink_softmax(s, sinks).astype(v_all.dtype)
    o = jnp.einsum('bkgts,bskd->btkgd', p, v_all)
    return o.reshape(B, T, N_Q_HEADS * HEAD_DIM)

def _route(x2, w_router, e_bias):
    N = x2.shape[0]
    scores = jax.nn.sigmoid(jnp.dot(x2, w_router).astype(jnp.float32))
    biased = scores + e_bias.astype(jnp.float32)
    grp = biased.reshape(N, N_GROUPS, N_EXPERTS // N_GROUPS)
    grp_score = lax.top_k(grp, 2)[0].sum(-1)
    _, gidx = lax.top_k(grp_score, TOPK_GROUPS)
    gmask = jnp.any(gidx[..., None] == jnp.arange(N_GROUPS), axis=-2)
    emask = jnp.repeat(gmask, N_EXPERTS // N_GROUPS, axis=-1)
    _, eidx = lax.top_k(jnp.where(emask, biased, -jnp.inf), TOP_K)
    w = jnp.take_along_axis(scores, eidx, -1)
    gate = w / jnp.sum(w, -1, keepdims=True) * ROUTED_SCALE
    return eidx, gate

def _moe_routed(x2, eidx, gate, w1, w3, w2):
    N = x2.shape[0]
    NK = N * TOP_K
    e_flat = eidx.reshape(-1)
    tok_flat = jnp.repeat(jnp.arange(N, dtype=jnp.int32), TOP_K)
    g_flat = gate.reshape(-1)
    order = jnp.argsort(e_flat, stable=True)
    e_s, tok_s, g_s = e_flat[order], tok_flat[order], g_flat[order]
    counts = jnp.zeros((N_EXPERTS,), jnp.int32).at[e_flat].add(1)
    start = jnp.cumsum(counts) - counts
    pcounts = (counts + MOE_BLOCK - 1) // MOE_BLOCK * MOE_BLOCK
    pend = jnp.cumsum(pcounts)
    pstart = pend - pcounts
    dest = pstart[e_s] + (jnp.arange(NK, dtype=jnp.int32) - start[e_s])
    n_blocks = -(-NK // MOE_BLOCK) + N_EXPERTS
    P = n_blocks * MOE_BLOCK
    ptok = jnp.full((P,), N, jnp.int32).at[dest].set(tok_s)
    pgate = jnp.zeros((P,), jnp.float32).at[dest].set(g_s)
    blk_start = jnp.arange(n_blocks, dtype=jnp.int32) * MOE_BLOCK
    blk_e = jnp.minimum(jnp.sum(pend[None, :] <= blk_start[:, None], axis=1), N_EXPERTS - 1).astype(jnp.int32)
    xpad = jnp.concatenate([x2, jnp.zeros((1, x2.shape[1]), x2.dtype)], 0)

    def run_block(args):
        tok, e = args
        xb = xpad[tok]
        hdn = jax.nn.silu(xb @ w1[e]) * (xb @ w3[e])
        return hdn @ w2[e]

    yb = lax.map(run_block, (ptok.reshape(n_blocks, MOE_BLOCK), blk_e))
    yb = yb.reshape(P, -1).astype(jnp.float32) * pgate[:, None]
    return jax.ops.segment_sum(yb, ptok, num_segments=N + 1)[:N].astype(x2.dtype)

def _layer(x, pos, first_reset, conv_buf, h0, past_k, past_v, lw):
    (w_in, conv_w, conv_b, w_a, b_a, w_x, b_x, a_param, sinks, w_br_rnn, w_br_attn, w_out,
     ln1_g, ln1_b, w_router, e_bias, w1, w3, w2, ws1, ws3, ws2, ln2_g, ln2_b) = lw
    B, T, D = x.shape
    z = jnp.einsum('btd,dc->btc', x, w_in)
    xr = z[..., :Q_OFF]
    q = _rope(z[..., Q_OFF:K_OFF].reshape(B, T, N_Q_HEADS, HEAD_DIM), pos)
    k = _rope(z[..., K_OFF:V_OFF].reshape(B, T, N_KV_HEADS, HEAD_DIM), pos)
    v = z[..., V_OFF:GR_OFF].reshape(B, T, N_KV_HEADS, HEAD_DIM)
    g_rnn = jax.nn.sigmoid(z[..., GR_OFF:GA_OFF])
    g_attn = jax.nn.sigmoid(z[..., GA_OFF:])
    y_rnn, h_last, new_buf = _rglru(xr, conv_buf, h0, conv_w, conv_b, w_a, b_a, w_x, b_x, a_param, first_reset)
    if past_k is None:
        o = _attn_prompt(q, k, v, sinks)
        keep = min(WINDOW, T)
        new_k, new_v = k[:, T - keep:], v[:, T - keep:]
    else:
        o = _attn_sample(q, jnp.concatenate([past_k.astype(k.dtype), k], 1),
                         jnp.concatenate([past_v.astype(v.dtype), v], 1), sinks)
        new_k, new_v = k, v
    merged = g_rnn * (y_rnn @ w_br_rnn) + g_attn * (o @ w_br_attn)
    x = _layernorm(DN_ALPHA * x + merged @ w_out, ln1_g, ln1_b)
    x2 = x.reshape(B * T, D)
    eidx, gate = _route(x2, w_router, e_bias)
    shared = (jax.nn.silu(x2 @ ws1) * (x2 @ ws3)) @ ws2
    ff = shared + _moe_routed(x2, eidx, gate, w1, w3, w2)
    x = _layernorm(DN_ALPHA * x + ff.reshape(B, T, D), ln2_g, ln2_b)
    return x, new_k, new_v, h_last, new_buf

def setup_inputs(seed: int = 0) -> dict:
    key = jax.random.key(seed)
    ks = iter(jax.random.split(key, 40))

    def nrm(shape, scale):
        return jax.random.normal(next(ks), shape, jnp.float32) * scale

    win_rows = min(WINDOW, PAST_LEN)
    u = jax.random.uniform(next(ks), (DEPTH, D_RNN), jnp.float32, minval=0.81, maxval=0.998)
    a_param = -jnp.log(jnp.expm1(-0.5 * jnp.log(u)))
    return {
        'x_prompt': nrm((BATCH, SEQ, D_MODEL), 1.0),
        'x_sample': nrm((DEC_BATCH, DEC_SEQ, D_MODEL), 1.0),
        'cache_k': nrm((DEPTH, DEC_BATCH, win_rows, N_KV_HEADS, HEAD_DIM), 1.0),
        'cache_v': nrm((DEPTH, DEC_BATCH, win_rows, N_KV_HEADS, HEAD_DIM), 1.0),
        'state_h': nrm((DEPTH, DEC_BATCH, D_RNN), 0.5),
        'state_conv': nrm((DEPTH, DEC_BATCH, CONV_W - 1, D_RNN), 1.0),
        'w_in': nrm((DEPTH, D_MODEL, IN_COLS), D_MODEL ** -0.5),
        'conv_w': nrm((DEPTH, CONV_W, D_RNN), CONV_W ** -0.5),
        'conv_b': nrm((DEPTH, D_RNN), 0.02),
        'w_a': nrm((DEPTH, RNN_BLOCKS, RNN_BW, RNN_BW), RNN_BW ** -0.5),
        'b_a': nrm((DEPTH, D_RNN), 0.02),
        'w_x': nrm((DEPTH, RNN_BLOCKS, RNN_BW, RNN_BW), RNN_BW ** -0.5),
        'b_x': nrm((DEPTH, D_RNN), 0.02),
        'a_param': a_param,
        'sinks': nrm((DEPTH, N_Q_HEADS), 0.5),
        'w_br_rnn': nrm((DEPTH, D_RNN, D_MODEL), D_RNN ** -0.5 * DN_BETA),
        'w_br_attn': nrm((DEPTH, N_Q_HEADS * HEAD_DIM, D_MODEL), (N_Q_HEADS * HEAD_DIM) ** -0.5 * DN_BETA),
        'w_out': nrm((DEPTH, D_MODEL, D_MODEL), D_MODEL ** -0.5 * DN_BETA),
        'ln1_g': 1.0 + nrm((DEPTH, D_MODEL), 0.02),
        'ln1_b': nrm((DEPTH, D_MODEL), 0.02),
        'w_router': nrm((DEPTH, D_MODEL, N_EXPERTS), D_MODEL ** -0.5),
        'e_bias': nrm((DEPTH, N_EXPERTS), 0.01),
        'w1': nrm((DEPTH, N_EXPERTS, D_MODEL, D_EXPERT), D_MODEL ** -0.5),
        'w3': nrm((DEPTH, N_EXPERTS, D_MODEL, D_EXPERT), D_MODEL ** -0.5),
        'w2': nrm((DEPTH, N_EXPERTS, D_EXPERT, D_MODEL), D_EXPERT ** -0.5 * DN_BETA),
        'ws1': nrm((DEPTH, D_MODEL, D_SHARED), D_MODEL ** -0.5),
        'ws3': nrm((DEPTH, D_MODEL, D_SHARED), D_MODEL ** -0.5),
        'ws2': nrm((DEPTH, D_SHARED, D_MODEL), D_SHARED ** -0.5 * DN_BETA),
        'ln2_g': 1.0 + nrm((DEPTH, D_MODEL), 0.02),
        'ln2_b': nrm((DEPTH, D_MODEL), 0.02),
    }

def reference(x_prompt, x_sample, cache_k, cache_v, state_h, state_conv,
              w_in, conv_w, conv_b, w_a, b_a, w_x, b_x, a_param, sinks,
              w_br_rnn, w_br_attn, w_out, ln1_g, ln1_b, w_router, e_bias,
              w1, w3, w2, ws1, ws3, ws2, ln2_g, ln2_b):
    Bp, Tp, _ = x_prompt.shape
    Ts = x_sample.shape[1]
    pos_p = jnp.arange(Tp, dtype=jnp.int32)
    pos_s = PAST_LEN + jnp.arange(Ts, dtype=jnp.int32)
    xp, xs = x_prompt, x_sample
    kp_l, vp_l, hp_l, cp_l = [], [], [], []
    ks_l, vs_l, hs_l, cs_l = [], [], [], []
    for l in range(DEPTH):
        lw = (w_in[l], conv_w[l], conv_b[l], w_a[l], b_a[l], w_x[l], b_x[l], a_param[l], sinks[l],
              w_br_rnn[l], w_br_attn[l], w_out[l], ln1_g[l], ln1_b[l], w_router[l], e_bias[l],
              w1[l], w3[l], w2[l], ws1[l], ws3[l], ws2[l], ln2_g[l], ln2_b[l])
        conv0 = jnp.zeros((Bp, CONV_W - 1, D_RNN), xp.dtype)
        h0 = jnp.zeros((Bp, D_RNN), xp.dtype)
        xp, kp, vp, hp, cp = _layer(xp, pos_p, True, conv0, h0, None, None, lw)
        xs, kn, vn, hn, cn = _layer(xs, pos_s, False, state_conv[l], state_h[l], cache_k[l], cache_v[l], lw)
        kp_l.append(kp); vp_l.append(vp); hp_l.append(hp); cp_l.append(cp)
        ks_l.append(kn); vs_l.append(vn); hs_l.append(hn); cs_l.append(cn)
    return (xp, xs,
            jnp.stack(kp_l), jnp.stack(vp_l), jnp.stack(hp_l), jnp.stack(cp_l),
            jnp.stack(ks_l), jnp.stack(vs_l), jnp.stack(hs_l), jnp.stack(cs_l))


_drawn_inputs = setup_inputs


def setup_inputs(seed=0):
    import zlib

    import numpy as np

    out = dict(_drawn_inputs(seed))
    spreads = {}
    factors = {'b_a': 8.0, 'b_x': 7.134, 'sinks': 24.662}
    for name, (base, spread) in spreads.items():
        noise = np.random.default_rng([zlib.crc32(name.encode()), seed]).standard_normal(out[name].shape)
        drawn = base * np.exp(spread * noise) if base else spread * noise
        out[name] = __import__('jax').numpy.asarray(drawn.astype(out[name].dtype))
    for name, factor in factors.items():
        out[name] = (out[name] * factor).astype(out[name].dtype)
    return out
```

```python
from contextlib import ExitStack

import concourse.bass as bass
from concourse import mybir

F32 = mybir.dt.float32
F32R = mybir.dt.float32r
I32 = mybir.dt.int32
ALU = mybir.AluOpType
ACT = mybir.ActivationFunctionType
AX_X = mybir.AxisListType.X

P = 128
D = 1024
KC = D // P
TP, TS = 256, 32
T = TP + TS
TOK = [(0, 128), (128, 128), (256, 32)]
NT = len(TOK)
HD = 64
NQ = D // HD
NKV = 2
CONV_W = 4
RG_C = 8.0
NE, TOPK, NG, TOPG = 64, 8, 8, 4
EPG = NE // NG
DE = 256
ME = DE // P
ROUTED_SCALE = 2.5
SCALE = HD ** -0.5
WIN = 128
PAST = 256
CHUNK = 64
LN_EPS = 1e-5
Q_OFF, K_OFF = D, 2 * D
V_OFF = K_OFF + NKV * HD
GR_OFF = V_OFF + NKV * HD
GA_OFF = GR_OFF + D

CAP = 64
QUAD = 4
NQUAD = NE // QUAD
MAX_ROUNDS = -(-T // CAP)

XC = (CONV_W - 1) + TP + (CONV_W - 1) + TS
US = TP + (CONV_W - 1)
U = US + TS

V_CW, V_CB, V_BA, V_BX, V_AP, V_G1, V_B1, V_G2, V_B2, V_H0, V_CS = 0, 4, 5, 6, 7, 8, 9, 10, 11, 12, 13
NV = 16

CONSTS = dict(ident=P, upper=P, ones=P, mask=3 * P, cos=T, sin=T, iota=QUAD * CAP, pads=4, thr=MAX_ROUNDS - 1, valid=NT, blank=NT)
C_AT, _n = {}, 0
for _k, _w in CONSTS.items():
    C_AT[_k] = _n
    _n += _w
NCONST = _n

BIG = 1.0e30
MARK = -3.0e38

Z_RNN, Z_Q, Z_K, Z_V, Z_LRU, Z_GATE, Z_OUT, Z_FILL1, Z_SH2, Z_FILL2, Z_N = 0, 8, 16, 17, 18, 34, 50, 58, 66, 74, 82
Z_HALF = Z_N // 2
Z_FIRST = KC // 2

PIECES = ([("in", 256 * j) for j in range(4)] + [("q", j) for j in range(4)] + [("in", K_OFF)]
          + [("in", GR_OFF + 256 * j) for j in range(8)]
          + [(n, 256 * j) for j in range(4) for n in ("br_rnn", "br_attn")]
          + [("out", 256 * j) for j in range(4)] + [("router", 0), ("s1", 0), ("s3", 0), ("s2", 0)])
ND = len(PIECES)
D_IN, D_Q, D_KV, D_G, D_BR, D_OUT, D_ROUTER = 0, 4, 8, 9, 17, 25, 29
RING = 3
DMAS = {"q": 4, "br_attn": 2}
SLOT_INC = [sum(16 * DMAS.get(PIECES[d][0], 1) for d in range(s, ND, RING)) for s in range(RING)]

PARAM_DMAS = 2 * 17
CH = 144


def piece_landed(L, d):
    return L * SLOT_INC[d % RING] + sum(16 * DMAS.get(PIECES[x][0], 1) for x in range(d % RING, d + 1, RING))


def z_count(L, i):
    return Z_FIRST + L * Z_HALF + i // 2


def build(nc, inp, out, depth, alpha):
    with ExitStack() as ctx:
        def sb(name, shape, dt=F32, scope=ctx):
            return scope.enter_context(nc.sbuf_tensor(name, shape, dt))

        def sem(name):
            return ctx.enter_context(nc.semaphore(name))

        ps = ctx.enter_context(nc.psum_tensor("ps", [P, 8, 512], F32))

        cst = sb("cst", [P, NCONST])
        C = {k: cst[:, C_AT[k]:C_AT[k] + w] for k, w in CONSTS.items()}
        ident = C["ident"]
        experts = sb("experts", [P, QUAD, 3, KC * DE])
        dense = sb("dense", [P, RING, KC * 256])
        xT = sb("xT", [P, KC, T])
        prm_all = sb("prm_all", [P, depth, NV * KC])
        prm = sb("prm", [P, NV * KC])
        gperm_all = sb("gperm_all", [P, depth, 2, KC])
        gperm = sb("gperm", [P, 2, KC])
        ebias_all = sb("ebias_all", [P, depth, NE])
        ebias = sb("ebias", [P, NE])
        sink_all = sb("sink_all", [P, depth, NQ])
        kcT_all = sb("kcT_all", [P, depth, WIN])
        kcT = sb("kcT", [P, WIN])
        vc_all = sb("vc_all", [P, depth, NKV * HD])
        vc = sb("vc", [P, NKV * HD])
        sinkP = sb("sinkP", [P, KC, 2, 2])
        sinkS = sb("sinkS", [P, 2, 2])
        c8 = sb("c8", [P, 2, KC])
        stat = sb("stat", [P, NT, 2, 6])
        mv = sb("mv", [P, NT, 2])
        gate = sb("gate", [P, NT, NE])
        rank = sb("rank", [P, NT, NE])
        rounds = sb("rounds", [P, 2], I32)
        small = sb("small", [P, 64])
        st_rows = sb("st_rows", [P, P])
        k_rows = sb("k_rows", [P, 2, P])

        s1 = ExitStack()
        B1 = sb("B1", [P, KC, XC], scope=s1)
        B3 = sb("B3", [P, KC, XC], scope=s1)
        qT = sb("qT", [P, KC, T], scope=s1)
        s1a = ExitStack()
        wax = sb("wax", [P, 2, KC, P], scope=s1a)
        s1a.close()
        S = sb("S", [P, 2, 2, 3 * P], scope=s1)
        PTa = sb("PTa", [P, 2, 2, 3 * P], scope=s1)
        kT = sb("kT", [P, T], scope=s1)
        v = sb("v", [P, NT, NKV * HD], scope=s1)
        tmp = sb("tmp", [P, 2, U], scope=s1)
        st = sb("st", [P, 8, KC], scope=s1)
        ats = sb("ats", [P, 2, 5, 4], scope=s1)
        B4 = sb("B4", [P, KC, XC], scope=s1)
        B2 = sb("B2", [P, KC, XC], scope=s1)
        s1.close()
        B1f, B2f, B3f, B4f = (b[:, :, :].rearrange("p c t -> p (c t)") for b in (B1, B2, B3, B4))
        gr_s = B1f[:, 0:KC * T].rearrange("p (c t) -> p c t", c=KC)
        ga_s = B3f[:, 0:KC * T].rearrange("p (c t) -> p c t", c=KC)
        hT = B2f[:, 0:KC * T].rearrange("p (c t) -> p c t", c=KC)
        mT = B4f[:, 0:KC * T].rearrange("p (c t) -> p c t", c=KC)
        yP = hT
        u_, a_, gx_, gl_ = (f[:, 0:KC * U].rearrange("p (c t) -> p c t", c=KC) for f in (B2f, B2f, B3f, B4f))
        uF, aF, gxF, glF = (f[:, 0:KC * U] for f in (B2f, B2f, B3f, B4f))

        s2 = ExitStack()
        xh = sb("xh", [P, NT, D], F32R, scope=s2)
        xl = sb("xl", [P, NT, D], F32R, scope=s2)
        s2a = ExitStack()
        tok = sb("tok", [P, NT, D], scope=s2a)
        s2a.close()
        xg = sb("xg", [P, KC, QUAD * CAP], scope=s2)
        yT = sb("yT", [P, KC, 2 * CAP], scope=s2)
        oh = sb("oh", [P, NT, QUAD * CAP], F32R, scope=s2)
        ohT = sb("ohT", [P, 2, T], F32R, scope=s2)
        sil = sb("sil", [P, QUAD, CAP], scope=s2)
        hid = sb("hid", [P, QUAD, CAP], scope=s2)
        s2b = ExitStack()
        rt = sb("rt", [P, NT, NE], scope=s2b)
        rt2 = sb("rt2", [P, NT, NE], scope=s2b)
        m8 = sb("m8", [P, NT, NG, 8], scope=s2b)
        gsp = sb("gsp", [P, NT, 12], scope=s2b)
        gs2 = sb("gs2", [P, NT, 12], scope=s2b)
        g8 = sb("g8", [P, NT, 8], scope=s2b)
        gm = sb("gm", [P, NT, NG], scope=s2b)
        t8 = sb("t8", [P, NT, 8], scope=s2b)
        sel = sb("sel", [P, NT, NE], scope=s2b)
        score = sb("score", [P, NT, NE], scope=s2b)
        tr = sb("tr", [P, NT, 8], scope=s2b)
        rs = sb("rs", [P, 8], scope=s2b)
        s2b.close()
        yh = sb("yh", [P, D], F32R, scope=s2)
        yl = sb("yl", [P, D], F32R, scope=s2)
        iota = sb("iota_w", [P, QUAD * CAP], scope=s2)
        gsl = sb("gsl", [P, 2], scope=s2)
        ffT = sb("ffT", [P, KC, T], scope=s2)
        s2.close()
        raw = B1f[:, 0:2 * depth * P].rearrange("p (k l c) -> p k l c", k=2, l=depth)
        hs = yT[:, :, :].rearrange("p a b -> p (a b)")[:, 0:ME * T].rearrange("p (m t) -> p m t", m=ME)

        consts_in = sem("consts_in")
        params_in = sem("params_in")
        x_in = sem("x_in")
        rows_ready = sem("rows_ready")
        rows_kept = sem("rows_kept")
        dense_in = [sem(f"dense_in{s}") for s in range(RING)]
        w13_in = [sem(f"w13_in{e}") for e in range(QUAD)]
        w2_in = [sem(f"w2_in{e}") for e in range(QUAD)]
        wax_zero = sem("wax_zero")
        wax_in = sem("wax_in")
        z_ready = [sem(f"z_ready{b}") for b in range(2)]
        z_free = [sem(f"z_free{b}") for b in range(2)]
        neg_abs = sem("neg_abs")
        exp_abs = sem("exp_abs")
        stat_own = sem("stat_own")
        xc_used = sem("xc_used")
        own = sem("dve_own")
        act_own = sem("act_own")
        layer_prm = sem("layer_prm")
        xc_ready = sem("xc_ready")
        u_ready = sem("u_ready")
        q_ready = sem("q_ready")
        lru_gates = sem("lru_gates")
        gxu = sem("gxu")
        a_and_t = sem("a_and_t")
        m2_ready = sem("m2_ready")
        mult_ready = sem("mult_ready")
        h_scan = sem("h_scan")
        h_ready = sem("h_ready")
        st_ready = sem("st_ready")
        out_rows = sem("out_rows")
        out_kept = sem("out_kept")
        kv_stored = sem("kv_stored")
        states_stored = sem("states_stored")
        y_stored = sem("y_stored")
        s_scores = sem("s_scores")
        s_masked = sem("s_masked")
        s_max = sem("s_max")
        s_exp = sem("s_exp")
        s_norm = sem("s_norm")
        sam_pT = sem("sam_pT")
        s_pT = sem("s_pT")
        s_pT_kept = sem("s_pT_kept")
        s_o = sem("s_o")
        o_ready = sem("o_ready")
        gates_ready = sem("gates_ready")
        br_ready = sem("br_ready")
        br_used = sem("br_used")

        tok_ps = sem("tok_ps")
        tok_act = sem("tok_act")
        tok_dve = sem("tok_dve")
        y_rows = sem("y_rows")
        var_ready = sem("var_ready")
        dev_ready = sem("dev_ready")
        norm_set = sem("norm_set")
        xh_ready = sem("xh_ready")
        xl_ready = sem("xl_ready")
        logits = sem("logits")
        score_clear = sem("score_clear")
        score_ready = sem("score_ready")
        sel_ready = sem("sel_ready")
        ranks = sem("ranks")
        rounds_set = sem("rounds_set")
        gate_ready = sem("gate_ready")
        sh_ready = sem("sh_ready")
        sh_silu = sem("sh_silu")
        sh_hid = sem("sh_hid")
        oh_ready = sem("oh_ready")
        xg_full = sem("xg_full")
        xg_kept = sem("xg_kept")
        w13_done = sem("w13_done")
        silu_done = sem("silu_done")
        hid_ready = sem("hid_ready")
        w2_done = sem("w2_done")
        yT_ready = sem("yT_ready")
        y_tok = sem("y_tok")
        yh_ready = sem("yh_ready")
        yl_ready = sem("yl_ready")
        ohT_full = sem("ohT_full")
        ohT_ready = sem("ohT_ready")
        c_full = sem("c_full")
        c_added = sem("c_added")
        next_round = sem("next_round")

        wait_carried = {e.engine: sem(f"wait_carried{i}") for i, e in enumerate((nc.sync, nc.gpsimd, nc.tensor, nc.scalar, nc.vector))}

        block = ctx.enter_context(nc.Block())

        def carry_wait(eng):
            eng.sem_inc(wait_carried[eng.engine], 1)

        @block.sync
        def _(sp):
            sp.dma_start(cst[:, :], inp["consts"]).then_inc(consts_in, 16)
            xp = inp["x_prompt"].rearrange("b (t p) d -> p (b t) d", p=P)
            sp.dma_start(tok[:, 0:2, :], xp).then_inc(x_in, 16)
            sp.dma_start(tok[0:TS, 2, :], inp["x_sample"].rearrange("b t d -> (b t) d")).then_inc(x_in, 16)

            def wait_piece_used(L, d):
                kind, at = PIECES[d]
                j = {D_IN: d, D_Q: d - D_Q, D_G: d - D_G}
                if d < D_Q:
                    i = Z_RNN + 2 * d + 1
                elif d < D_KV:
                    i = Z_Q + 2 * (d - D_Q) + 1
                elif d == D_KV:
                    i = Z_V
                elif d < D_BR:
                    i = Z_GATE + 2 * (d - D_G) + 1
                elif d < D_OUT:
                    sp.wait_ge(br_ready, L * KC + 2 * ((d - D_BR) // 2) + 2)
                    return
                elif d < D_ROUTER:
                    i = Z_OUT + 2 * (d - D_OUT) + 1
                elif kind == "router":
                    sp.wait_ge(logits, L + 1)
                    return
                else:
                    sp.wait_ge(sh_ready, L * 2 + (1 if kind == "s1" else 2))
                    return
                sp.wait_ge(z_ready[i % 2], z_count(L, i) + 1)

            def load_piece(L, d):
                kind, at = PIECES[d]
                slot = dense[:, d % RING, :]
                full = slot.rearrange("p (k c) -> p k c", k=KC)
                s = dense_in[d % RING]
                rows = lambda w: w[bass.ds(L, 1)].rearrange("l (k p) c -> p (l k) c", p=P)
                if d >= RING:
                    wait_piece_used(L, d - RING)
                else:
                    sp.wait_ge(z_ready[1], Z_FIRST + L * Z_HALF - (Z_N - Z_SH2 - KC) // 2)
                if kind == "q":
                    for c in range(2):
                        for g in range(2):
                            x = Q_OFF + (g * KC + 2 * at + c) * HD
                            sp.dma_start(full[:, :, c * P + g * HD:c * P + g * HD + HD], rows(inp["w_in"])[:, :, x:x + HD])\
                                .then_inc(s, 16)
                elif kind == "br_attn":
                    w = inp["w_br_attn"][bass.ds(L, 1)].rearrange("l (g k p) c -> g p (l k) c", g=2, p=HD)
                    for g in range(2):
                        sp.dma_start(full[g * HD:g * HD + HD, :, :], w[g, :, :, at:at + 256]).then_inc(s, 16)
                elif kind == "router":
                    dst = slot[:, 0:KC * NE].rearrange("p (k c) -> p k c", k=KC)
                    sp.dma_start(dst, rows(inp["w_router"])).then_inc(s, 16)
                elif kind == "s2":
                    dst = slot.rearrange("p (m c) -> p m c", m=ME)
                    sp.dma_start(dst, rows(inp["ws2"])).then_inc(s, 16)
                else:
                    w = {"in": "w_in", "br_rnn": "w_br_rnn", "out": "w_out", "s1": "ws1", "s3": "ws3"}[kind]
                    sp.dma_start(full, rows(inp[w])[:, :, at:at + 256]).then_inc(s, 16)

            def load_pair(L, i, u):
                for e in (2 * u, 2 * u + 1):
                    at = L * NE + i * QUAD + e
                    for j, w in enumerate(("w1", "w3")):
                        src = inp[w].rearrange("l e (p k) c -> (l e) p (k c)", k=KC)[bass.ds(at, 1)]
                        sp.dma_start(experts[:, e, j, :], src.rearrange("o p x -> p (o x)")).then_inc(w13_in[e], 16)
                    src = inp["w2"].rearrange("l e (m p) c -> (l e) p m c", p=P)[bass.ds(at, 1)]
                    dst = experts[:, e, 2, :].rearrange("p (m c) -> p m c", m=ME)
                    sp.dma_start(dst, src.rearrange("o p m c -> p (o m) c")).then_inc(w2_in[e], 16)

            done = sp.alloc_register("quads_done")
            sp.reg_mov(done, 0)
            with sp.Fori(0, depth) as L:
                for d in range(RING):
                    load_piece(L, d)
                q0 = sp.snap(done)
                sp.wait_ge(w2_done, q0 * 4)
                for u in range(2):
                    load_pair(L, 0, u)
                for d in range(RING, ND):
                    load_piece(L, d)
                sp.wait_ge(rounds_set, L + 1)
                carry_wait(sp)
                nr = sp.value_load(rounds[0:1, 0:1], min_val=1, max_val=MAX_ROUNDS)
                with sp.Fori(1, nr * NQUAD) as t:
                    for u in range(2):
                        sp.wait_ge(w2_done, (q0 + t) * 4 + (2 * u - 2))
                        load_pair(L, t % NQUAD, u)
                sp.reg_add(done, done, nr * NQUAD)

        @block.gpsimd
        def _(pool):
            with pool.Fori(0, depth) as L:
                for b in range(2):
                    pool.wait_ge(z_free[b], Z_FIRST + L * Z_HALF)
                carry_wait(pool)
                nc.gpsimd.memset(wax[:, :, :, :], 0.0).then_inc(wax_zero, 1)
                pool.wait_ge(wax_zero, L + 1)
                carry_wait(pool)
                for j, w in enumerate(("w_x", "w_a")):
                    src = inp[w][bass.ds(L, 1)].rearrange("l (c g) i o -> g i (l c) o", g=2)
                    for g in range(2):
                        pool.dma_start(wax[g * HD:g * HD + HD, j, :, g * HD:g * HD + HD], src[g]).then_inc(wax_in, 16)
                pool.wait_ge(z_free[Z_V % 2], z_count(L, Z_V) + 1)
                carry_wait(pool)
                rows = lambda o: o[bass.ds(L, 1)].rearrange("l b t g d -> (l b t) (g d)")
                pool.dma_start(rows(out["v_prompt"]), v[:, 1, :]).then_inc(kv_stored, 16)
                pool.dma_start(rows(out["v_sample"]), v[0:TS, 2, :]).then_inc(kv_stored, 16)
                pool.wait_ge(out_kept, 2 * L + 1)
                carry_wait(pool)
                pool.dma_start(rows(out["k_prompt"]), k_rows[:, 0, :]).then_inc(kv_stored, 16)
                pool.dma_start(rows(out["k_sample"]), k_rows[0:TS, 1, :]).then_inc(kv_stored, 16)
                pool.wait_ge(out_kept, 2 * L + 2)
                carry_wait(pool)
                hrow = lambda o: o[bass.ds(L, 1)].rearrange("l b (c p) -> (l b c) p", p=P)
                crow = lambda o: o[bass.ds(L, 1)].rearrange("l b j (c p) -> (l b j c) p", p=P)
                pool.dma_start(hrow(out["h_prompt"]), st_rows[0:KC, :]).then_inc(states_stored, 16)
                pool.dma_start(hrow(out["h_sample"]), st_rows[KC:2 * KC, :]).then_inc(states_stored, 16)
                pool.dma_start(crow(out["conv_prompt"]), st_rows[2 * KC:5 * KC, :]).then_inc(states_stored, 16)
                pool.dma_start(crow(out["conv_sample"]), st_rows[5 * KC:8 * KC, :]).then_inc(states_stored, 16)
                pool.wait_ge(kv_stored, (L + 1) * 64)
                pool.wait_ge(states_stored, (L + 1) * 64)
            pool.wait_ge(y_rows, 2 * NT)
            yp = out["y_prompt"].rearrange("b (t p) d -> p (b t) d", p=P)
            pool.dma_start(yp, tok[:, 0:2, :]).then_inc(y_stored, 16)
            pool.dma_start(out["y_sample"].rearrange("b t d -> (b t) d"), tok[0:TS, 2, :]).then_inc(y_stored, 16)
            pool.wait_ge(y_stored, 32)

        @block.tensor
        def _(pe):
            mm, transpose = nc.tensor.matmul, nc.tensor.transpose

            def bank_of(L, i):
                pe.wait_ge(z_free[i % 2], z_count(L, i))
                return ps[:, i % 2, :]

            def over_features(bank, d, col, rhs, n):
                w = dense[:, d % RING, :].rearrange("p (k c) -> p k c", k=KC)
                for k in range(KC):
                    last = mm(bank[:, 0:n], w[:, k, col:col + P], rhs(k), start=k == 0, stop=k == KC - 1)
                return last

            def piece(L, d):
                pe.wait_ge(dense_in[d % RING], piece_landed(L, d))

            def fill_xT(wait):
                for c in range(KC):
                    wait(c)
                    for t, (at, n) in enumerate(TOK):
                        last = transpose(ps[:, c % 2, at:at + n], tok[0:n, t, c * P:c * P + P], ident[0:n, 0:n])
                    last.then_inc(z_ready[c % 2], 1)

            def to_tokens(src):
                for t, (at, n) in enumerate(TOK):
                    for h in range(2):
                        for c in range(4):
                            last = transpose(ps[0:n, 2 + 2 * t + h, c * P:c * P + P], src[:, 4 * h + c, at:at + n], ident)
                        last.then_inc(tok_ps, 1)

            pe.wait_ge(consts_in, 16)
            pe.wait_ge(params_in, PARAM_DMAS * 16)
            for l in range(depth):
                transpose(ps[:, 2, l * P:l * P + P], raw[:, 0, l, :], ident)
                last = transpose(ps[:, 3, l * P:l * P + P], raw[:, 1, l, :], ident)
            last.then_inc(rows_ready, 1)
            pe.wait_ge(x_in, 32)
            fill_xT(lambda c: pe.wait_ge(z_free[c % 2], c // 2) if c >= 2 else None)
            pe.wait_ge(rows_kept, 2)

            done = pe.alloc_register("quads_done")
            pe.reg_mov(done, 0)
            with pe.Fori(0, depth) as L:
                xk = lambda k: xT[:, k, :]
                for b in range(2):
                    pe.wait_ge(z_free[b], Z_FIRST + L * Z_HALF)

                for m in range(KC):
                    if m % 2 == 0:
                        piece(L, D_IN + m // 2)
                    over_features(bank_of(L, Z_RNN + m), D_IN + m // 2, m % 2 * P, xk, T).then_inc(z_ready[m % 2], 1)
                for c in range(KC):
                    d = D_Q + c // 2
                    if c % 2 == 0:
                        piece(L, d)
                    bank = bank_of(L, Z_Q + c)
                    over_features(bank, d, c % 2 * P, xk, T).then_inc(z_ready[c % 2], 1)
                piece(L, D_KV)
                over_features(bank_of(L, Z_K), D_KV, 0, xk, T).then_inc(z_ready[Z_K % 2], 1)
                bank = bank_of(L, Z_V)
                w = dense[:, D_KV % RING, :].rearrange("p (k c) -> p k c", k=KC)
                for t, (at, n) in enumerate(TOK):
                    for k in range(KC):
                        last = mm(bank[0:n, t * P:t * P + P], xT[:, k, at:at + n], w[:, k, P:2 * P], start=k == 0, stop=k == KC - 1)
                last.then_inc(z_ready[Z_V % 2], 1)
                pe.wait_ge(wax_in, (L + 1) * 64)
                for c in range(KC):
                    pe.wait_ge(u_ready, L * KC + c + 1)
                    for j in range(2):
                        bank = bank_of(L, Z_LRU + 2 * c + j)
                        mm(bank[:, 0:U], wax[:, j, c, :], u_[:, c, :], start=True, stop=True).then_inc(z_ready[j], 1)
                pe.wait_ge(q_ready, L * (KC + 1) + KC + 1)
                transpose(ps[:, 7, 0:P], kT[:, TP - WIN:TP], ident)
                transpose(ps[0:TS, 7, P:2 * P], kT[:, TP:T], ident).then_inc(out_rows, 1)

                for h in range(2):
                    lo, hi = h * HD, h * HD + HD
                    for a in range(2):
                        for i in range(4):
                            q = qT[lo:hi, 4 * a + i, TP:T]
                            o = ps[32 * i:32 * i + 32, 2 + h, a * 160:a * 160 + 160]
                            mm(o[:, 0:WIN], q, kcT[lo:hi, :], start=True, stop=True)
                            last = mm(o[:, WIN:WIN + TS], q, kT[lo:hi, TP:T], start=True, stop=True)
                last.then_inc(s_scores, 1)
                pe.wait_ge(s_norm, L * (KC + 1) + 1)
                for h in range(2):
                    for a in range(2):
                        p = S[:, 0, h, a * 160:a * 160 + 160]
                        transpose(ps[:, 4 + h, a * P:a * P + P], p[:, 0:WIN], ident)
                        last = transpose(ps[0:TS, 4 + h, (2 + a) * P:(3 + a) * P], p[:, WIN:WIN + TS], ident)
                last.then_inc(s_pT, 1)
                pe.wait_ge(z_free[Z_V % 2], z_count(L, Z_V) + 1)
                pe.wait_ge(s_pT_kept, L * (KC + 1) + 1)
                for h in range(2):
                    lo, hi = h * HD, h * HD + HD
                    pt = PTa[:, 0, :, :].rearrange("p h x -> p (h x)")[:, h * 256:h * 256 + 256]
                    ptn = PTa[:, 1, :, :].rearrange("p h x -> p (h x)")[:, h * 256:h * 256 + 256]
                    for a in range(2):
                        o = ps[lo:hi, 6, a * P:a * P + P]
                        mm(o, vc[:, lo:hi], pt[:, a * P:a * P + P], start=True, stop=False)
                        last = mm(o, v[0:TS, 2, lo:hi], ptn[0:TS, a * P:a * P + P], start=False, stop=True)
                last.then_inc(s_o, 1)

                for c in range(KC):
                    n = L * (KC + 1) + c + 1
                    if c == 0:
                        pe.wait_ge(s_exp, n)
                    else:
                        pe.wait_ge(s_masked, L * KC + c)
                    for h in range(2):
                        lo, hi = h * HD, h * HD + HD
                        mm(ps[:, 2 + h, 0:TP], qT[lo:hi, c, P:TP], kT[lo:hi, 0:TP], start=True, stop=True)
                        last = mm(ps[:, 2 + h, TP:TP + P], qT[lo:hi, c, 0:P], kT[lo:hi, 0:P], start=True, stop=True)
                    last.then_inc(s_scores, 1)
                    for m in (2 * c, 2 * c + 1):
                        d = D_G + m // 2
                        if m % 2 == 0:
                            piece(L, d)
                        over_features(bank_of(L, Z_GATE + m), d, m % 2 * P, xk, T).then_inc(z_ready[m % 2], 1)
                    pe.wait_ge(s_norm, n + 1)
                    pe.wait_ge(s_pT_kept, n)
                    for h in range(2):
                        for k in range(3):
                            last = transpose(ps[:, 4 + h, k * P:k * P + P], S[:, c % 2, h, k * P:k * P + P], ident)
                    last.then_inc(s_pT, 1)
                    pe.wait_ge(s_pT_kept, n + 1)
                    pe.wait_ge(o_ready, n)
                    for h in range(2):
                        lo, hi = h * HD, h * HD + HD
                        pt = PTa[:, c % 2, h, :]
                        mm(ps[lo:hi, 6, P:2 * P], v[:, 0, lo:hi], pt[:, 0:P], start=True, stop=False)
                        mm(ps[lo:hi, 6, P:2 * P], v[:, 1, lo:hi], pt[:, P:2 * P], start=False, stop=True)
                        last = mm(ps[lo:hi, 6, 0:P], v[:, 0, lo:hi], pt[:, 2 * P:3 * P], start=True, stop=True)
                    last.then_inc(s_o, 1)

                pe.wait_ge(st_ready, L + 1)
                pe.wait_ge(out_kept, 2 * L + 1)
                carry_wait(pe)
                transpose(ps[0:8 * KC, 7, 0:P], st[:, :, :].rearrange("p v c -> p (v c)"), ident).then_inc(out_rows, 1)

                pe.wait_ge(h_ready, L + 1)
                pe.wait_ge(o_ready, (L + 1) * (KC + 1))
                for m in range(KC):
                    d = D_BR + m // 2 * 2
                    if m % 2 == 0:
                        piece(L, d)
                        piece(L, d + 1)
                    if m >= 2:
                        pe.wait_ge(br_used, L * KC + m - 1)
                    over_features(ps[:, 2 + m % 2, :], d, m % 2 * P, lambda k: hT[:, k, :], T)
                    over_features(ps[:, 4 + m % 2, :], d + 1, m % 2 * P, lambda k: qT[:, k, :], T).then_inc(br_ready, 1)
                pe.wait_ge(br_used, (L + 1) * KC)
                for m in range(KC):
                    if m % 2 == 0:
                        piece(L, D_OUT + m // 2)
                    over_features(bank_of(L, Z_OUT + m), D_OUT + m // 2, m % 2 * P, lambda k: mT[:, k, :], T)\
                        .then_inc(z_ready[m % 2], 1)
                for b in range(2):
                    pe.wait_ge(z_free[b], z_count(L, Z_OUT + KC))
                pe.wait_ge(out_kept, 2 * L + 2)
                to_tokens(yP)
                pe.wait_ge(tok_act, (2 * L + 1) * NT)
                pe.wait_ge(tok_dve, (2 * L + 1) * NT)
                fill_xT(lambda c: bank_of(L, Z_FILL1 + c))

                piece(L, D_ROUTER)
                for b in range(2):
                    pe.wait_ge(z_free[b], z_count(L, Z_FILL1 + KC))
                w = dense[:, D_ROUTER % RING, 0:KC * NE].rearrange("p (k c) -> p k c", k=KC)
                for t, (at, n) in enumerate(TOK):
                    for k in range(KC):
                        last = mm(ps[0:n, 2, t * NE:t * NE + NE], xT[:, k, at:at + n], w[:, k, :], start=k == 0, stop=k == KC - 1)
                last.then_inc(logits, 1)
                for j in range(2):
                    piece(L, D_ROUTER + 1 + j)
                    for m in range(ME):
                        last = over_features(ps[:, 4 + 2 * j + m, :], D_ROUTER + 1 + j, m * P, xk, T)
                    last.then_inc(sh_ready, 1)
                pe.wait_ge(sel_ready, L + 1)
                for t in range(NT):
                    o = ps[:, 3, t * NE:t * NE + NE]
                    for x in range(t):
                        mm(o, C["ones"], sel[:, x, :], start=x == 0, stop=False)
                    mm(o, C["upper"], sel[:, t, :], start=t == 0, stop=True)
                for t in range(NT):
                    last = mm(ps[:, 3, NT * NE:(NT + 1) * NE], C["ones"], sel[:, t, :], start=t == 0, stop=t == NT - 1)
                last.then_inc(ranks, 1)
                d = D_ROUTER + 3
                piece(L, d)
                pe.wait_ge(sh_hid, (L + 1) * 2)
                w = dense[:, d % RING, :].rearrange("p (m c) -> p m c", m=ME)
                for c in range(KC):
                    bank = bank_of(L, Z_SH2 + c)
                    for m in range(ME):
                        last = mm(bank[:, 0:T], w[:, m, c * P:c * P + P], hs[:, m, :], start=m == 0, stop=m == ME - 1)
                    last.then_inc(z_ready[c % 2], 1)

                def gather(n):
                    pe.wait_ge(oh_ready, n + 1)
                    for j in range(4):
                        if j >= 2:
                            pe.wait_ge(xg_kept, n * 4 + (j - 1))
                        for k in (2 * j, 2 * j + 1):
                            o = ps[:, j % 2, k % 2 * 256:k % 2 * 256 + 256]
                            if k == 0:
                                pe.wait_ge(xh_ready, (L + 1) * NT)
                                pe.wait_ge(xl_ready, (L + 1) * NT)
                            for t in range(NT):
                                r = TOK[t][1]
                                mm(o, xh[0:r, t, k * P:k * P + P], oh[0:r, t, :], start=t == 0, stop=False)
                                last = mm(o, xl[0:r, t, k * P:k * P + P], oh[0:r, t, :], start=False, stop=t == NT - 1)
                        last.then_inc(xg_full, 1)

                def up(n, u):
                    pe.wait_ge(xg_kept, n * 4 + 4)
                    pe.wait_ge(hid_ready, n * 2 + u)
                    for e in (2 * u, 2 * u + 1):
                        pe.wait_ge(w13_in[e], (n + 1) * 32)
                        for j in range(2):
                            w = experts[:, e, j, :].rearrange("p (k c) -> p k c", k=KC)
                            for m in range(ME):
                                x = j * 4 + (e % 2) * 2 + m
                                for k in range(KC):
                                    last = mm(ps[:, 2, x * CAP:x * CAP + CAP], w[:, k, m * P:m * P + P],
                                              xg[:, k, e * CAP:e * CAP + CAP], start=k == 0, stop=k == KC - 1)
                    last.then_inc(w13_done, 1)

                def down(n, u):
                    pe.wait_ge(hid_ready, n * 2 + u + 1)
                    pe.wait_ge(yl_ready, (n * 2 + u) * 2)
                    for e in (2 * u, 2 * u + 1):
                        pe.wait_ge(w2_in[e], (n + 1) * 16)
                    for c in range(KC):
                        for e in (2 * u, 2 * u + 1):
                            w = experts[:, e, 2, :].rearrange("p (m c) -> p m c", m=ME)
                            x = c % 4 * 2 + e % 2
                            for m in range(ME):
                                last = mm(ps[:, 3 + c // 4, x * CAP:x * CAP + CAP], w[:, m, c * P:c * P + P],
                                          hid[:, e % 2 * 2 + m, :], start=m == 0, stop=m == ME - 1)
                        if c % 4 == 3:
                            last.then_inc(w2_done, 1)

                def turn(n, u):
                    for b in range(2):
                        pe.wait_ge(yT_ready, (n * 2 + u) * 2 + (b + 1))
                        for c in range(4):
                            last = transpose(ps[:, 3 + b, c * P:c * P + P], yT[:, 4 * b + c, :], ident)
                        last.then_inc(y_tok, 1)

                def slots_to_tokens(n, i, u):
                    pe.wait_ge(ohT_ready, n * 2 + u)
                    o = oh[:, :, u * P:u * P + P].bitcast(F32)
                    for t, (at, r) in enumerate(TOK):
                        transpose(ps[:, 7, at:at + r], o[0:r, t, :], ident[0:r, 0:r])
                    for t in range(NT):
                        g = gate[:, t, bass.ds(i * QUAD + 2 * u, 2)]
                        last = mm(ps[:, 7, T:T + 2], o[:, t, :], g, start=t == 0, stop=t == NT - 1)
                    last.then_inc(ohT_full, 1)

                def combine(n, u):
                    p = n * 2 + u
                    pe.wait_ge(ohT_ready, p + 1)
                    pe.wait_ge(yl_ready, p * 2 + 2)
                    for c in range(KC):
                        pe.wait_ge(c_added, p * KC + max(c - 1, 0))
                        o = ps[:, 5 + c % 2, 0:T]
                        mm(o, yh[:, c * P:c * P + P], ohT[:, u, :], start=True, stop=False)
                        mm(o, yl[:, c * P:c * P + P], ohT[:, u, :], start=False, stop=True).then_inc(c_full, 1)

                def quad(n, i, first=False, last=False):
                    up(n, 0)
                    if not first:
                        combine(n - 1, 1)
                    slots_to_tokens(n, i, 0)
                    down(n, 0)
                    slots_to_tokens(n, i, 1)
                    up(n, 1)
                    turn(n, 0)
                    if not last:
                        gather(n + 1)
                    down(n, 1)
                    combine(n, 0)
                    turn(n, 1)

                for b in range(2):
                    pe.wait_ge(z_free[b], z_count(L, Z_SH2 + KC))
                pe.wait_ge(rounds_set, L + 1)
                carry_wait(pe)
                nr = pe.value_load(rounds[0:1, 0:1], min_val=1, max_val=MAX_ROUNDS)
                with pe.Fori(0, nr) as r:
                    q = pe.snap(done)
                    gather(q)
                    quad(q, 0, first=True)
                    with pe.Fori(1, NQUAD - 1) as i:
                        quad(q + i, i)
                    quad(q + (NQUAD - 1), NQUAD - 1, last=True)
                    combine(q + (NQUAD - 1), 1)
                    pe.reg_add(done, done, NQUAD)

                pe.wait_ge(c_added, pe.snap(done) * (2 * KC))
                to_tokens(ffT)
                pe.wait_ge(tok_act, (2 * L + 2) * NT)
                pe.wait_ge(tok_dve, (2 * L + 2) * NT)
                fill_xT(lambda c: bank_of(L, Z_FILL2 + c))

            for b in range(2):
                pe.wait_ge(z_free[b], Z_FIRST + depth * Z_HALF)
            to_tokens(xT)

        @block.scalar
        def _(act):
            activation = nc.scalar.activation

            def rows_of(w, at, n, l):
                act.dma_start(raw[at * KC:(at + n) * KC, 0, l, :], w).then_inc(params_in, 16)
            for l in range(depth):
                rows_of(inp["conv_w"][l].rearrange("j (c p) -> (j c) p", p=P), V_CW, CONV_W, l)
                for at, name in ((V_CB, "conv_b"), (V_BA, "b_a"), (V_BX, "b_x"), (V_AP, "a_param"), (V_G1, "ln1_g"),
                                 (V_B1, "ln1_b"), (V_G2, "ln2_g"), (V_B2, "ln2_b")):
                    rows_of(inp[name][l].rearrange("(c p) -> c p", p=P), at, 1, l)
                rows_of(inp["state_h"][l].rearrange("b (c p) -> (b c) p", p=P), V_H0, 1, l)
                rows_of(inp["state_conv"][l].rearrange("b j (c p) -> (b j c) p", p=P), V_CS, CONV_W - 1, l)
                act.dma_start(raw[:, 1, l, :], inp["cache_k"][l].rearrange("b t g d -> (b t) (g d)")).then_inc(params_in, 16)
                act.dma_start(vc_all[:, l, :], inp["cache_v"][l].rearrange("b t g d -> (b t) (g d)")).then_inc(params_in, 16)
                for j, name in enumerate(("ln1_g", "ln1_b")):
                    act.dma_start(gperm_all[:, l, j, :], inp[name][l].rearrange("(p k) -> p k", k=KC)).then_inc(params_in, 16)
                wide = lambda w: w[l].rearrange("(o n) -> o n", o=1).to_broadcast((P, w.shape[1]))
                act.dma_start(ebias_all[:, l, :], wide(inp["e_bias"])).then_inc(params_in, 16)
                act.dma_start(sink_all[:, l, :], wide(inp["sinks"])).then_inc(params_in, 16)

            def z_item(L, i):
                act.wait_ge(z_ready[i % 2], z_count(L, i) + 1)
                return ps[:, i % 2, :]

            for c in range(0, KC, 2):
                act.wait_ge(z_ready[0], c // 2 + 1)
                activation(xT[:, c, :], ps[:, 0, 0:T], ACT.Copy).then_inc(z_free[0], 1)

            def norm_rows(L, k):
                for t, (at, n) in enumerate(TOK):
                    act.wait_ge(var_ready, (2 * L + k) * NT + (t + 1))
                    activation(mv[0:n, t, 1:2], mv[0:n, t, 1:2], ACT.Sqrt).then_inc(dev_ready, 1)
                for t, (at, n) in enumerate(TOK):
                    act.wait_ge(norm_set, (2 * L + k) * NT + (t + 1))
                    activation(tok[0:n, t, 512:D], ps[0:n, 3 + 2 * t, :], ACT.Identity, bias=mv[0:n, t, 0:1],
                               scale=mv[0:n, t, 1:2]).then_inc(tok_act, 1)

            def norm_back(L, g, b, first):
                for c in range(0, KC, 2):
                    bank = z_item(L, first + c)
                    activation(xT[:, c, :], bank[:, 0:T], ACT.Identity, bias=prm[:, b * KC + c:b * KC + c + 1],
                               scale=prm[:, g * KC + c:g * KC + c + 1]).then_inc(z_free[0], 1)

            done = act.alloc_register("quads_done")
            act.reg_mov(done, 0)
            with act.Fori(0, depth) as L:
                act.wait_ge(neg_abs, L + 1)
                activation(small[:, 0:KC], small[:, 0:KC], ACT.Exp).then_inc(exp_abs, 1)
                act.wait_ge(rows_kept, 2)
                for m in range(KC):
                    bank = z_item(L, Z_RNN + m)
                    activation(B1[:, m, CONV_W - 1:CONV_W - 1 + TP], bank[:, 0:TP], ACT.Copy)
                    activation(B1[:, m, XC - TS:XC], bank[:, TP:T], ACT.Copy).then_inc(z_free[m % 2], 1)
                bank = z_item(L, Z_V)
                activation(v[:, 0:2, :], bank[:, 0:2 * P].rearrange("p (t c) -> p t c", t=2), ACT.Copy)
                activation(v[0:TS, 2, :], bank[0:TS, 2 * P:3 * P], ACT.Copy).then_inc(z_free[Z_V % 2], 1)
                act.wait_ge(layer_prm, L + 1)
                for c in range(KC):
                    for j, (dst, b) in enumerate(((gx_, V_BX), (gl_, V_BA))):
                        bank = z_item(L, Z_LRU + 2 * c + j)
                        activation(dst[:, c, :], bank[:, 0:U], ACT.Sigmoid, bias=prm[:, b * KC + c:b * KC + c + 1])\
                            .then_inc(z_free[j], 1)
                act.wait_ge(gxu, L + 1)
                act.wait_ge(z_free[1], z_count(L, Z_LRU + 2 * KC))
                for c in range(KC):
                    activation(a_[:, c, :], gl_[:, c, :], ACT.Exp, scale=c8[:, 0, c:c + 1]).then_inc(act_own, 1)
                act.wait_ge(act_own, (L + 1) * KC)
                for c in range(KC):
                    activation(gl_[:, c, :], gl_[:, c, :], ACT.Tanh, scale=c8[:, 1, c:c + 1]).then_inc(a_and_t, 1)
                act.wait_ge(s_max, L * (KC + 1) + 1)
                for h in range(2):
                    for a in range(2):
                        x = 2 * h + a
                        activation(S[:, 0, h, a * 160:a * 160 + 160], ps[:, 2 + h, a * 160:a * 160 + 160], ACT.Exp,
                                   bias=ats[:, 0, 1, x:x + 1], scale=SCALE, accum_out=ats[:, 0, 2, x:x + 1])
                activation(ats[:, 0, 4, :], ats[:, 0, 3, :], ACT.Exp).then_inc(s_exp, 1)
                act.wait_ge(s_pT, L * (KC + 1) + 1)
                ptc = PTa[:, 0, :, :].rearrange("p h x -> p (h x)")
                ptn = PTa[0:TS, 1, :, :].rearrange("p h x -> p (h x)")
                for h in range(2):
                    activation(ptc[:, h * 256:h * 256 + 256], ps[:, 4 + h, 0:256], ACT.Copy)
                    last = activation(ptn[:, h * 256:h * 256 + 256], ps[0:TS, 4 + h, 256:512], ACT.Copy)
                last.then_inc(s_pT_kept, 1)
                act.wait_ge(m2_ready, (L + 1) * KC)
                activation(glF, glF, ACT.Sqrt).then_inc(mult_ready, 1)

                act.wait_ge(xc_used, L + 1)
                for c in range(KC):
                    n = L * (KC + 1) + c + 1
                    w = c % 2
                    act.wait_ge(s_max, n + 1)
                    for b, (lo, hi) in enumerate(((0, TP), (TP, TP + P))):
                        for h in range(2):
                            x = 2 * b + h
                            activation(S[:, w, h, lo:hi], S[:, w, h, lo:hi], ACT.Exp, bias=ats[:, w, 1, x:x + 1],
                                       scale=SCALE, accum_out=ats[:, w, 2, x:x + 1])
                    activation(ats[:, w, 4, :], ats[:, w, 3, :], ACT.Exp).then_inc(s_exp, 1)
                    if c == KC // 2:
                        act.wait_ge(h_scan, L + 1)
                        activation(hT[:, :, 0:TP], gl_[:, :, 0:TP], ACT.Copy)
                        activation(hT[:, :, TP:T], gl_[:, :, US:U], ACT.Copy).then_inc(h_ready, 1)
                    for m in (2 * c, 2 * c + 1):
                        bank = z_item(L, Z_GATE + m)
                        dst = gr_s[:, m, :] if m < KC else ga_s[:, m - KC, :]
                        activation(dst, bank[:, 0:T], ACT.Sigmoid).then_inc(z_free[m % 2], 1)
                    act.wait_ge(s_pT, n + 1)
                    act.wait_ge(s_o, L * (KC + 1) + max(c, 1))
                    activation(PTa[:, w, 0, :], ps[:, 4, 0:3 * P], ACT.Copy)
                    activation(PTa[:, w, 1, :], ps[:, 5, 0:3 * P], ACT.Copy).then_inc(s_pT_kept, 1)

                norm_rows(L, 0)
                for t, (at, n) in enumerate(TOK):
                    act.wait_ge(tok_act, (2 * L) * NT + (t + 1))
                    act.wait_ge(tok_dve, (2 * L) * NT + (t + 1))
                    activation(xh[0:n, t, :].rearrange("p (k f) -> p f k", k=KC),
                               tok[0:n, t, :].rearrange("p (f k) -> p f k", k=KC), ACT.Copy).then_inc(xh_ready, 1)
                norm_back(L, V_G1, V_B1, Z_FILL1)
                act.wait_ge(logits, L + 1)
                act.wait_ge(score_clear, L + 1)
                activation(score[:, 0:2, :], ps[:, 2, 0:2 * NE].rearrange("p (t e) -> p t e", t=2), ACT.Sigmoid)
                activation(score[0:TS, 2, :], ps[0:TS, 2, 2 * NE:3 * NE], ACT.Sigmoid).then_inc(score_ready, 1)
                act.wait_ge(sh_ready, L * 2 + 1)
                for m in range(ME):
                    activation(hs[:, m, :], ps[:, 4 + m, 0:T], ACT.Silu).then_inc(sh_silu, 1)

                def keep_gathered(n):
                    act.wait_ge(w13_done, n * 2)
                    for j in range(4):
                        act.wait_ge(xg_full, n * 4 + (j + 1))
                        for k in (2 * j, 2 * j + 1):
                            last = activation(xg[:, k, :], ps[:, j % 2, k % 2 * 256:k % 2 * 256 + 256], ACT.Identity,
                                              bias=gperm[:, 1, k:k + 1], scale=gperm[:, 0, k:k + 1])
                        last.then_inc(xg_kept, 1)

                def silu(n, u):
                    p = n * 2 + u
                    act.wait_ge(w13_done, p + 1)
                    act.wait_ge(hid_ready, p)
                    activation(sil[:, :, :].rearrange("p a s -> p (a s)"), ps[:, 2, 0:4 * CAP], ACT.Silu)\
                        .then_inc(silu_done, 1)

                def keep_yT(n, u):
                    p = n * 2 + u
                    act.wait_ge(y_tok, p * 2)
                    for b in range(2):
                        act.wait_ge(w2_done, p * 2 + (b + 1))
                        activation(yT[:, 4 * b:4 * b + 4, :].rearrange("p c s -> p (c s)"), ps[:, 3 + b, :], ACT.Copy)\
                            .then_inc(yT_ready, 1)

                def high_part(n, u):
                    p = n * 2 + u
                    act.wait_ge(ohT_ready, p + 1)
                    act.wait_ge(c_full, p * KC)
                    for b in range(2):
                        act.wait_ge(y_tok, p * 2 + (b + 1))
                        activation(yh[:, 512 * b:512 * b + 512], ps[:, 3 + b, :], ACT.Identity, scale=gsl[:, u:u + 1])\
                            .then_inc(yh_ready, 1)

                def quad(n, last=False):
                    silu(n, 0)
                    keep_yT(n, 0)
                    silu(n, 1)
                    high_part(n, 0)
                    if not last:
                        keep_gathered(n + 1)
                    keep_yT(n, 1)
                    high_part(n, 1)

                act.wait_ge(rounds_set, L + 1)
                carry_wait(act)
                nr = act.value_load(rounds[0:1, 0:1], min_val=1, max_val=MAX_ROUNDS)
                with act.Fori(0, nr) as r:
                    q = act.snap(done)
                    keep_gathered(q)
                    with act.Fori(0, NQUAD - 1) as i:
                        quad(q + i)
                    quad(q + (NQUAD - 1), last=True)
                    act.reg_add(done, done, NQUAD)

                norm_rows(L, 1)
                norm_back(L, V_G2, V_B2, Z_FILL2)

            for t, (at, n) in enumerate(TOK):
                act.wait_ge(tok_ps, (2 * depth + 0) * 2 * NT + 2 * t + 2)
                activation(tok[0:n, t, 512:D], ps[0:n, 3 + 2 * t, :], ACT.Copy).then_inc(y_rows, 1)

        @block.vector
        def _(dve):
            V = nc.vector
            steps = [0]
            before = [0]

            def link(ins, plain=False):
                steps[0] += 1
                ins.then_inc(own, 1)
                dve.wait_ge(own, before[0] + steps[0])
                if plain:
                    carry_wait(dve)

            def z_item(L, i):
                dve.wait_ge(z_ready[i % 2], z_count(L, i) + 1)
                return ps[:, i % 2, :]

            dve.wait_ge(rows_ready, 1)
            V.tensor_copy(prm_all[:, :, :], ps[:, 2, 0:depth * P].rearrange("p (l c) -> p l c", l=depth)).then_inc(rows_kept, 1)
            V.tensor_copy(kcT_all[:, :, :], ps[:, 3, 0:depth * P].rearrange("p (l c) -> p l c", l=depth)).then_inc(rows_kept, 1)
            dve.wait_ge(rows_kept, 2)
            for c in range(1, KC, 2):
                dve.wait_ge(z_ready[1], c // 2 + 1)
                V.tensor_copy(xT[:, c, :], ps[:, 1, 0:T]).then_inc(z_free[1], 1)

            def stats(L, k):
                base = (2 * L + k) * 4 * NT
                for t, (at, n) in enumerate(TOK):
                    for h in range(2):
                        dve.wait_ge(tok_ps, (2 * L + k) * 2 * NT + (2 * t + h + 1))
                        V.bn_stats(stat[0:n, t, h, :], ps[0:n, 2 + 2 * t + h, :]).then_inc(stat_own, 1)
                    dve.wait_ge(stat_own, base + (3 * t + 2))
                    carry_wait(dve)
                    V.bn_aggr(mv[0:n, t, :], stat[0:n, t, :, :]).then_inc(stat_own, 1)
                    dve.wait_ge(stat_own, base + (3 * t + 3))
                    V.tensor_scalar(mv[0:n, t, 1:2], mv[0:n, t, 1:2], LN_EPS, None, ALU.add).then_inc(var_ready, 1)
                for t, (at, n) in enumerate(TOK):
                    dve.wait_ge(dev_ready, (2 * L + k) * NT + (t + 1))
                    V.reciprocal(mv[0:n, t, 1:2], mv[0:n, t, 1:2]).then_inc(stat_own, 1)
                    dve.wait_ge(stat_own, base + (3 * NT + t + 1))
                    V.scalar_tensor_tensor(mv[0:n, t, 0:1], mv[0:n, t, 0:1], -1.0, mv[0:n, t, 1:2], ALU.mult, ALU.mult)\
                        .then_inc(norm_set, 1)
                    dve.wait_ge(norm_set, (2 * L + k) * NT + (t + 1))
                    V.tensor_scalar(tok[0:n, t, 0:512], ps[0:n, 2 + 2 * t, :], mv[0:n, t, 1:2], mv[0:n, t, 0:1],
                                    ALU.mult, ALU.add).then_inc(tok_dve, 1)

            def norm_back(L, g, b, first):
                for c in range(1, KC, 2):
                    bank = z_item(L, first + c)
                    V.tensor_scalar(xT[:, c, :], bank[:, 0:T], prm[:, g * KC + c:g * KC + c + 1],
                                    prm[:, b * KC + c:b * KC + c + 1], ALU.mult, ALU.add).then_inc(z_free[1], 1)

            done = dve.alloc_register("quads_done")
            dve.reg_mov(done, 0)
            with dve.Fori(0, depth) as L:
                before[0] = L * CH
                for b in range(2):
                    dve.wait_ge(z_free[b], Z_FIRST + L * Z_HALF)
                dve.wait_ge(params_in, PARAM_DMAS * 16)
                V.tensor_copy(prm[:, :], prm_all[:, bass.ds(L, 1), :].rearrange("p o c -> p (o c)"))
                V.tensor_copy(gperm[:, :, :], gperm_all[:, bass.ds(L, 1), :, :].rearrange("p o j k -> p (o j) k"))
                V.tensor_copy(ebias[:, :], ebias_all[:, bass.ds(L, 1), :].rearrange("p o c -> p (o c)"))
                V.tensor_copy(kcT[:, :], kcT_all[:, bass.ds(L, 1), :].rearrange("p o c -> p (o c)"))
                V.tensor_copy(vc[:, :], vc_all[:, bass.ds(L, 1), :].rearrange("p o c -> p (o c)"))
                sk = sink_all[:, bass.ds(L, 1), :].rearrange("p o (h c) -> p (o c) h", h=2)
                V.tensor_copy(sinkP[:, :, 0, :], sk)
                link(V.tensor_copy(sinkP[:, :, 1, :], sk))
                for i in range(4):
                    x = slice(32 * i, 32 * i + 32)
                    last = V.tensor_copy(sinkS[x, :, :], sinkP[x, i:KC:4, 0, :].rearrange("p a h -> p h a"))
                link(last)
                ap = prm[:, V_AP * KC:V_AP * KC + KC]
                e, s_, s2_, p_ = (small[:, 8 * j:8 * j + 8] for j in range(4))
                link(V.tensor_scalar(e, ap, -1.0, None, ALU.mult))
                V.tensor_tensor(e, e, ap, ALU.min).then_inc(neg_abs, 1)
                dve.wait_ge(exp_abs, L + 1)
                link(V.tensor_scalar(s2_, e, 2.0, None, ALU.add))
                link(V.reciprocal(s2_, s2_))
                link(V.tensor_tensor(s_, e, s2_, ALU.mult))
                link(V.tensor_tensor(s2_, s_, s_, ALU.mult))
                link(V.tensor_scalar(p_, s2_, 1.0 / 17, 1.0 / 15, ALU.mult, ALU.add))
                for k in (13, 11, 9, 7, 5, 3, 1):
                    link(V.tensor_tensor(p_, p_, s2_, ALU.mult))
                    link(V.tensor_scalar(p_, p_, 1.0 / k, None, ALU.add))
                link(V.scalar_tensor_tensor(p_, p_, 2.0, s_, ALU.mult, ALU.mult))
                link(V.tensor_scalar(s_, ap, -1.0, 0.0, ALU.mult, ALU.max))
                link(V.tensor_tensor(p_, p_, s_, ALU.add))
                V.tensor_scalar(c8[:, 0, :], p_, -RG_C, None, ALU.mult)
                V.tensor_scalar(c8[:, 1, :], p_, RG_C, None, ALU.mult).then_inc(layer_prm, 1)

                V.memset(B1[:, :, 0:CONV_W - 1], 0.0)
                cs = prm[:, V_CS * KC:(V_CS + CONV_W - 1) * KC].rearrange("p (j c) -> p c j", c=KC)
                link(V.tensor_copy(B1[:, :, CONV_W - 1 + TP:US + CONV_W - 1], cs))
                for c in range(KC):
                    dve.wait_ge(z_free[c % 2], z_count(L, Z_RNN + c) + 1)
                    w = lambda j: prm[:, (V_CW + j) * KC + c:(V_CW + j) * KC + c + 1]
                    link(V.tensor_scalar(u_[:, c, :], B1[:, c, 0:U], w(0), prm[:, V_CB * KC + c:V_CB * KC + c + 1],
                                         ALU.mult, ALU.add))
                    for j in range(1, CONV_W):
                        last = V.scalar_tensor_tensor(u_[:, c, :], B1[:, c, j:j + U], w(j), u_[:, c, :], ALU.mult, ALU.add)
                        if j < CONV_W - 1:
                            link(last)
                    last.then_inc(u_ready, 1)
                V.tensor_copy(st[:, 2:5, :], B1[:, :, TP:TP + 3].rearrange("p c j -> p j c"))
                V.tensor_copy(st[:, 5:8, :], B1[:, :, XC - 3:XC].rearrange("p c j -> p j c")).then_inc(xc_used, 1)

                rot = tmp[:, :, :].rearrange("p a t -> p (a t)")[:, 0:T]
                for c in range(KC + 1):
                    i = Z_Q + c
                    dst = qT[:, c, :] if c < KC else kT[:, :]
                    bank = z_item(L, i)
                    V.tensor_tensor(dst, bank[:, 0:T], C["cos"], ALU.mult)
                    for x in range(4):
                        a, b = 32 * x, 32 * (x ^ 1)
                        last = V.tensor_tensor(rot[a:a + 32, :], bank[b:b + 32, 0:T], C["sin"][b:b + 32, :], ALU.mult)
                    last.then_inc(z_free[i % 2], 1)
                    dve.wait_ge(z_free[i % 2], z_count(L, i) + 1)
                    V.tensor_tensor(dst, dst, rot, ALU.add).then_inc(q_ready, 1)
                    dve.wait_ge(q_ready, L * (KC + 1) + c + 1)
                for b in range(2):
                    dve.wait_ge(z_free[b], z_count(L, Z_LRU + 2 * KC))
                V.tensor_tensor(gxF, gxF, uF, ALU.mult).then_inc(gxu, 1)
                dve.wait_ge(kv_stored, L * 64)
                dve.wait_ge(out_rows, 2 * L + 1)
                V.tensor_copy(k_rows[:, 0, :], ps[:, 7, 0:P])
                V.tensor_copy(k_rows[0:TS, 1, :], ps[0:TS, 7, P:2 * P]).then_inc(out_kept, 1)

                def soften(w, sinks, n):
                    m, nm, dif = ats[:, w, 0, :], ats[:, w, 1, :], ats[:, w, 3, :]
                    link(V.scalar_tensor_tensor(m, m, SCALE, sinks, ALU.mult, ALU.max))
                    link(V.tensor_scalar(nm, m, -1.0, None, ALU.mult))
                    V.tensor_tensor(dif, sinks, nm, ALU.add).then_inc(s_max, 1)

                def normalise(w, parts, n):
                    dve.wait_ge(s_exp, n)
                    den, rd = ats[:, w, 2, :], ats[:, w, 0, :]
                    link(V.tensor_tensor(den, den, ats[:, w, 4, :], ALU.add))
                    link(V.reciprocal(rd, den))
                    for x, s in enumerate(parts):
                        last = V.tensor_scalar(s, s, rd[:, x:x + 1], None, ALU.mult)
                    last.then_inc(s_norm, 1)

                n = L * (KC + 1) + 1
                dve.wait_ge(s_scores, n)
                for h in range(2):
                    last = V.tensor_reduce(ats[:, 0, 0, 2 * h:2 * h + 2], ps[:, 2 + h, 0:320].rearrange("p (a s) -> p a s", a=2),
                                           AX_X, ALU.max)
                link(last)
                soften(0, sinkS[:, :, :].rearrange("p h a -> p (h a)"), n)
                normalise(0, [S[:, 0, h, a * 160:a * 160 + 160] for h in range(2) for a in range(2)], n)
                for c in range(KC):
                    dve.wait_ge(a_and_t, L * KC + c + 1)
                    t_ = tmp[:, c % 2, :]
                    link(V.tensor_scalar(t_, gl_[:, c, :], 1.0, None, ALU.add))
                    link(V.reciprocal(t_, t_))
                    V.scalar_tensor_tensor(gl_[:, c, :], gl_[:, c, :], 2.0, t_, ALU.mult, ALU.mult).then_inc(m2_ready, 1)
                dve.wait_ge(s_o, n)
                V.tensor_copy(qT[:, :, TP:T], ps[:, 6, 0:KC * TS].rearrange("p (c t) -> p c t", c=KC)).then_inc(o_ready, 1)
                dve.wait_ge(mult_ready, L + 1)
                link(V.memset(gl_[:, :, 0:1], 1.0))
                V.memset(a_[:, :, 0:1], 0.0)
                V.memset(a_[:, :, US - 1:US], 0.0)
                link(V.tensor_tensor(gxF, gxF, glF, ALU.mult))
                h0 = prm[:, V_H0 * KC:V_H0 * KC + KC].rearrange("p (c o) -> p c o", o=1)
                link(V.tensor_copy(gx_[:, :, US - 1:US], h0))
                V.tensor_tensor_scan(glF, aF, gxF, 0.0, ALU.mult, ALU.add).then_inc(h_scan, 1)
                dve.wait_ge(h_scan, L + 1)
                V.tensor_copy(st[:, 0, :], gl_[:, :, TP - 1])
                V.tensor_copy(st[:, 1, :], gl_[:, :, U - 1]).then_inc(st_ready, 1)

                for c in range(KC):
                    n = L * (KC + 1) + c + 1
                    w = c % 2
                    dve.wait_ge(s_scores, n + 1)
                    dve.wait_ge(s_pT, L * (KC + 1) + max(c, 1))
                    for h in range(2):
                        last = V.tensor_tensor(S[:, w, h, :], ps[:, 2 + h, 0:3 * P], C["mask"], ALU.add)
                    last.then_inc(s_masked, 1)
                    dve.wait_ge(s_masked, L * KC + c + 1)
                    V.tensor_reduce(ats[:, w, 0, 0:2], S[:, w, :, 0:TP], AX_X, ALU.max)
                    link(V.tensor_reduce(ats[:, w, 0, 2:4], S[:, w, :, TP:TP + P], AX_X, ALU.max))
                    soften(w, sinkP[:, c, :, :].rearrange("p b h -> p (b h)"), n)
                    if c > 0:
                        dve.wait_ge(s_o, n)
                        V.tensor_copy(qT[:, c - 1, 0:TP], ps[:, 6, 0:TP]).then_inc(o_ready, 1)
                    normalise(w, [S[:, w, h, lo:hi] for lo, hi in ((0, TP), (TP, TP + P)) for h in range(2)], n + 1)
                dve.wait_ge(s_o, n + 1)
                V.tensor_copy(qT[:, KC - 1, 0:TP], ps[:, 6, 0:TP]).then_inc(o_ready, 1)
                dve.wait_ge(out_rows, 2 * L + 2)
                V.tensor_copy(st_rows[0:8 * KC, :], ps[0:8 * KC, 7, 0:P]).then_inc(out_kept, 1)

                dve.wait_ge(z_free[0], z_count(L, Z_OUT))
                dve.wait_ge(z_free[1], z_count(L, Z_OUT))
                for m in range(KC):
                    dve.wait_ge(br_ready, L * KC + m + 1)
                    V.tensor_tensor(gr_s[:, m, :], ps[:, 2 + m % 2, 0:T], gr_s[:, m, :], ALU.mult)
                    link(V.tensor_tensor(ga_s[:, m, :], ps[:, 4 + m % 2, 0:T], ga_s[:, m, :], ALU.mult))
                    V.tensor_tensor(mT[:, m, :], gr_s[:, m, :], ga_s[:, m, :], ALU.add).then_inc(br_used, 1)
                for m in range(KC):
                    bank = z_item(L, Z_OUT + m)
                    V.scalar_tensor_tensor(yP[:, m, :], xT[:, m, :], alpha, bank[:, 0:T], ALU.mult, ALU.add)\
                        .then_inc(z_free[m % 2], 1)

                stats(L, 0)
                V.memset(score[:, 2, :], 0.0).then_inc(score_clear, 1)
                for t, (at, n) in enumerate(TOK):
                    dve.wait_ge(xh_ready, L * NT + t + 1)
                    V.tensor_tensor(xl[0:n, t, :].rearrange("p (k f) -> p f k", k=KC),
                                    tok[0:n, t, :].rearrange("p (f k) -> p f k", k=KC),
                                    xh[0:n, t, :].bitcast(F32).rearrange("p (k f) -> p f k", k=KC), ALU.subtract)\
                        .then_inc(xl_ready, 1)
                norm_back(L, V_G1, V_B1, Z_FILL1)

                dve.wait_ge(kv_stored, (L + 1) * 64)
                b3 = lambda x, k: x.rearrange("p (o k) -> p o k", o=1).to_broadcast((P, NT, k))
                V.tensor_copy(gsp[:, :, 8:12], b3(C["pads"], 4))
                V.tensor_copy(tr[:, :, 4:8], b3(C["pads"], 4))
                dve.wait_ge(score_ready, L + 1)
                link(V.tensor_tensor(rt[:, :, :], score[:, :, :], b3(ebias[:, :], NE), ALU.add), plain=True)
                for t in range(NT):
                    for g in range(NG):
                        last = V.max(m8[:, t, g, :], rt[:, t, g * EPG:(g + 1) * EPG])
                link(last)
                link(V.tensor_tensor(gsp[:, :, 0:NG], m8[:, :, :, 0], m8[:, :, :, 1], ALU.add), plain=True)
                for t in range(NT):
                    last = V.max(g8[:, t, :], gsp[:, t, 0:NG])
                link(last)
                link(V.tensor_copy(tr[:, :, 0:TOPG], g8[:, :, 0:TOPG]), plain=True)
                for t in range(NT):
                    last = V.match_replace(gs2[:, t, :], tr[:, t, :], gsp[:, t, :], MARK)
                link(last)
                link(V.tensor_scalar(gm[:, :, :], gs2[:, :, 0:NG], MARK, None, ALU.is_equal))
                r4 = lambda x: x.rearrange("p t (g e) -> p t g e", g=NG)
                gb = gm[:, :, :].rearrange("p t (g o) -> p t g o", o=1).to_broadcast((P, NT, NG, EPG))
                link(V.tensor_tensor(r4(rt[:, :, :]), r4(rt[:, :, :]), gb, ALU.mult))
                link(V.tensor_scalar(gm[:, :, :], gm[:, :, :], BIG, -BIG, ALU.mult, ALU.add))
                link(V.tensor_tensor(r4(rt[:, :, :]), r4(rt[:, :, :]), gb, ALU.add), plain=True)
                for t in range(NT):
                    last = V.max(t8[:, t, :], rt[:, t, :])
                link(last, plain=True)
                for t in range(NT):
                    last = V.match_replace(rt2[:, t, :], t8[:, t, :], rt[:, t, :], MARK)
                link(last)
                link(V.tensor_scalar(rt2[:, :, :], rt2[:, :, :], MARK, None, ALU.is_equal))
                valid = C["valid"].rearrange("p (t o) -> p t o", o=1)
                V.tensor_tensor(sel[:, :, :], rt2[:, :, :], valid.to_broadcast((P, NT, NE)), ALU.mult).then_inc(sel_ready, 1)
                dve.wait_ge(sel_ready, L + 1)
                link(V.tensor_tensor(gate[:, :, :], score[:, :, :], sel[:, :, :], ALU.mult))
                link(V.tensor_reduce(rs[:, 0:NT], gate[:, :, :], AX_X, ALU.add))
                link(V.tensor_tensor(rs[:, 0:NT], rs[:, 0:NT], C["blank"], ALU.add))
                link(V.reciprocal(rs[:, 0:NT], rs[:, 0:NT]))
                dve.wait_ge(sh_ready, L * 2 + 2)
                for m in range(ME):
                    dve.wait_ge(sh_silu, L * ME + m + 1)
                    V.tensor_tensor(hs[:, m, :], ps[:, 6 + m, 0:T], hs[:, m, :], ALU.mult).then_inc(sh_hid, 1)
                rb = rs[:, 0:NT].rearrange("p (t o) -> p t o", o=1).to_broadcast((P, NT, NE))
                V.scalar_tensor_tensor(gate[:, :, :], gate[:, :, :], ROUTED_SCALE, rb, ALU.mult, ALU.mult).then_inc(gate_ready, 1)
                dve.wait_ge(ranks, L + 1)
                link(V.scalar_tensor_tensor(rank[:, :, :], ps[:, 3, 0:NT * NE].rearrange("p (t e) -> p t e", t=NT), 1.0,
                                            sel[:, :, :], ALU.add, ALU.mult))
                V.tensor_scalar(rank[:, :, :], rank[:, :, :], -1.0, None, ALU.add)
                link(V.tensor_reduce(rs[:, 4:5], ps[:, 3, NT * NE:(NT + 1) * NE], AX_X, ALU.max))
                link(V.tensor_scalar(rt[:, 0, 0:MAX_ROUNDS - 1], C["thr"], rs[:, 4:5], None, ALU.is_lt))
                link(V.tensor_reduce(rs[:, 5:6], rt[:, 0, 0:MAX_ROUNDS - 1], AX_X, ALU.add))
                link(V.tensor_copy(iota[:, :], C["iota"]))
                V.tensor_scalar(rounds[:, 0:1], rs[:, 5:6], 1.0, None, ALU.add).then_inc(rounds_set, 1)
                dve.wait_ge(rounds_set, L + 1)
                for c in range(KC):
                    bank = z_item(L, Z_SH2 + c)
                    V.scalar_tensor_tensor(ffT[:, c, :], xT[:, c, :], alpha, bank[:, 0:T], ALU.mult, ALU.add)\
                        .then_inc(z_free[c % 2], 1)
                for b in range(2):
                    dve.wait_ge(z_free[b], z_count(L, Z_SH2 + KC))

                def one_hot(n, i):
                    dve.wait_ge(ohT_full, n * 2)
                    shape = (P, NT, QUAD, CAP)
                    a = iota[:, :].rearrange("p (o e s) -> p o e s", o=1, e=QUAD).to_broadcast(shape)
                    b = rank[:, :, bass.ds(i * QUAD, QUAD)].rearrange("p t (e o) -> p t e o", o=1).to_broadcast(shape)
                    V.tensor_tensor(oh[:, :, :].rearrange("p t (e s) -> p t e s", e=QUAD), a, b, ALU.is_equal)\
                        .then_inc(oh_ready, 1)

                def hidden(n, u):
                    p = n * 2 + u
                    dve.wait_ge(silu_done, p + 1)
                    dve.wait_ge(w2_done, p * 2)
                    V.tensor_tensor(hid[:, :, :].rearrange("p a s -> p (a s)"), ps[:, 2, 4 * CAP:8 * CAP],
                                    sil[:, :, :].rearrange("p a s -> p (a s)"), ALU.mult).then_inc(hid_ready, 1)

                def keep_turned(n, u):
                    dve.wait_ge(ohT_full, n * 2 + (u + 1))
                    V.tensor_copy(gsl[0:CAP, u:u + 1], ps[0:CAP, 7, T:T + 1])
                    V.tensor_copy(gsl[CAP:P, u:u + 1], ps[CAP:P, 7, T + 1:T + 2])
                    V.tensor_copy(ohT[:, u, :], ps[:, 7, 0:T]).then_inc(ohT_ready, 1)

                def low_part(n, u):
                    p = n * 2 + u
                    dve.wait_ge(ohT_ready, p + 1)
                    for b in range(2):
                        dve.wait_ge(yh_ready, p * 2 + (b + 1))
                        x = slice(512 * b, 512 * b + 512)
                        V.scalar_tensor_tensor(yl[:, x], ps[:, 3 + b, :], gsl[:, u:u + 1], yh[:, x].bitcast(F32),
                                               ALU.mult, ALU.subtract).then_inc(yl_ready, 1)

                def add_output(n, u):
                    p = n * 2 + u
                    dve.wait_ge(c_added, p * KC)
                    for c in range(KC):
                        dve.wait_ge(c_full, p * KC + (c + 1))
                        V.tensor_tensor(ffT[:, c, :], ps[:, 5 + c % 2, 0:T], ffT[:, c, :], ALU.add).then_inc(c_added, 1)

                def quad(n, i, first=False, last=False):
                    hidden(n, 0)
                    if not first:
                        add_output(n - 1, 1)
                    keep_turned(n, 0)
                    keep_turned(n, 1)
                    if not last:
                        one_hot(n + 1, i + 1)
                    hidden(n, 1)
                    low_part(n, 0)
                    add_output(n, 0)
                    low_part(n, 1)

                carry_wait(dve)
                nr = dve.value_load(rounds[0:1, 0:1], min_val=1, max_val=MAX_ROUNDS)
                with dve.Fori(0, nr) as r:
                    q = dve.snap(done)
                    one_hot(q, 0)
                    quad(q, 0, first=True)
                    with dve.Fori(1, NQUAD - 1) as i:
                        quad(q + i, i)
                    quad(q + (NQUAD - 1), NQUAD - 1, last=True)
                    add_output(q + (NQUAD - 1), 1)
                    V.tensor_scalar(iota[:, :], iota[:, :], float(CAP), None, ALU.add).then_inc(next_round, NQUAD)
                    dve.wait_ge(next_round, q + NQUAD)
                    dve.reg_add(done, done, NQUAD)

                stats(L, 1)
                norm_back(L, V_G2, V_B2, Z_FILL2)
            assert steps[0] == CH, steps[0]

            for t, (at, n) in enumerate(TOK):
                dve.wait_ge(tok_ps, 2 * depth * 2 * NT + 2 * t + 1)
                V.tensor_copy(tok[0:n, t, 0:512], ps[0:n, 2 + 2 * t, :]).then_inc(y_rows, 1)



def _constants():
    import numpy as np

    f = np.float32
    c = np.zeros((P, NCONST), f)
    put = lambda k, x: c.__setitem__((slice(None), slice(C_AT[k], C_AT[k] + CONSTS[k])), x)
    row, col = np.arange(P)[:, None], np.arange(P)[None, :]
    put("ident", row == col)
    put("upper", row < col)
    put("ones", 1.0)
    q, kw = row // CHUNK, np.arange(TP)[None, :] // CHUNK
    wide = np.where((kw <= q + 2) & (kw >= q), 0.0, -BIG)
    narrow = np.where(col // CHUNK <= q, 0.0, -BIG)
    put("mask", np.concatenate([wide, narrow], 1))
    half = HD // 2
    inv = np.power(f(10000.0), -np.arange(half, dtype=f) / f(half)).astype(f)
    pos = np.concatenate([np.arange(TP), PAST + np.arange(TS)]).astype(f)
    ang = (pos[None, :] * inv[np.arange(P) % half][:, None]).astype(f)
    put("cos", np.cos(ang))
    put("sin", np.where(row % HD < half, 1.0, -1.0) * np.sin(ang))
    put("iota", np.arange(QUAD * CAP)[None, :] % CAP)
    put("pads", np.array([[4e30, 3e30, 2e30, 1e30]]))
    put("thr", CAP * np.arange(1, MAX_ROUNDS)[None, :])
    rows = np.stack([np.arange(P) < n for _, n in TOK], 1)
    put("valid", rows)
    put("blank", ~rows)
    return c


def kernel(**inputs):
    import numpy as np
    import concourse.bacc as bacc
    from concourse.bass_utils import run_bass_kernel_spmd as run

    arrays = {k: np.ascontiguousarray(a) for k, a in inputs.items()}
    arrays["consts"] = _constants()
    depth = arrays["w_in"].shape[0]
    nc = bacc.Bacc("TRN2", target_bir_lowering=False, num_devices=1)
    inp = {k: nc.dram_tensor("in_" + k, a.shape, mybir.dt.from_np(a.dtype), kind="ExternalInput").ap() for k, a in arrays.items()}
    kv = lambda t: (depth, 1, t, NKV, HD)
    shapes = {"y_prompt": (1, TP, D), "y_sample": (1, TS, D), "k_prompt": kv(WIN), "v_prompt": kv(WIN), "h_prompt": (depth, 1, D),
              "conv_prompt": (depth, 1, CONV_W - 1, D), "k_sample": kv(TS), "v_sample": kv(TS), "h_sample": (depth, 1, D),
              "conv_sample": (depth, 1, CONV_W - 1, D)}
    out = {k: nc.dram_tensor("out_" + k, s, F32, kind="ExternalOutput").ap() for k, s in shapes.items()}
    build(nc, inp, out, depth, float((2 * depth) ** 0.25))
    r = run(nc, [{"in_" + k: a for k, a in arrays.items()}], core_ids=[0])
    return tuple(r.results[0]["out_" + k] for k in shapes)
```

```python
from contextlib import ExitStack

import concourse.bass as bass
from concourse import mybir

F32 = mybir.dt.float32
F32R = mybir.dt.float32r
I32 = mybir.dt.int32
ALU = mybir.AluOpType
ACT = mybir.ActivationFunctionType
AX_X = mybir.AxisListType.X

P = 128
D = 1024
KC = D // P
TP, TS = 256, 32
T = TP + TS
TOK = [(0, 128), (128, 128), (256, 32)]
NT = len(TOK)
HD = 64
NQ = D // HD
NKV = 2
CONV_W = 4
RG_C = 8.0
NE, TOPK, NG, TOPG = 64, 8, 8, 4
EPG = NE // NG
DE = 256
ME = DE // P
ROUTED_SCALE = 2.5
SCALE = HD ** -0.5
WIN = 128
PAST = 256
CHUNK = 64
LN_EPS = 1e-5
Q_OFF, K_OFF = D, 2 * D
V_OFF = K_OFF + NKV * HD
GR_OFF = V_OFF + NKV * HD
GA_OFF = GR_OFF + D

CAP = 64
QUAD = 4
NQUAD = NE // QUAD
MAX_ROUNDS = -(-T // CAP)

XC = (CONV_W - 1) + TP + (CONV_W - 1) + TS
US = TP + (CONV_W - 1)
U = US + TS

V_CW, V_CB, V_BA, V_BX, V_AP, V_G1, V_B1, V_G2, V_B2, V_H0, V_CS = 0, 4, 5, 6, 7, 8, 9, 10, 11, 12, 13
NV = 16

CONSTS = dict(ident=P, upper=P, ones=P, mask=3 * P, cos=T, sin=T, iota=QUAD * CAP, pads=4, thr=MAX_ROUNDS - 1, valid=NT, blank=NT)
C_AT, _n = {}, 0
for _k, _w in CONSTS.items():
    C_AT[_k] = _n
    _n += _w
NCONST = _n

BIG = 1.0e30
MARK = -3.0e38

Z_RNN, Z_Q, Z_K, Z_V, Z_LRU, Z_GATE, Z_OUT, Z_FILL1, Z_SH2, Z_FILL2, Z_N = 0, 8, 16, 17, 18, 34, 50, 58, 66, 74, 82
Z_HALF = Z_N // 2
Z_FIRST = KC // 2

PIECES = ([("in", 256 * j) for j in range(4)] + [("q", j) for j in range(4)] + [("in", K_OFF)]
          + [("in", GR_OFF + 256 * j) for j in range(8)]
          + [(n, 256 * j) for j in range(4) for n in ("br_rnn", "br_attn")]
          + [("out", 256 * j) for j in range(4)] + [("router", 0), ("s1", 0), ("s3", 0), ("s2", 0)])
ND = len(PIECES)
D_IN, D_Q, D_KV, D_G, D_BR, D_OUT, D_ROUTER = 0, 4, 8, 9, 17, 25, 29
RING = 3
DMAS = {"q": 4, "br_attn": 2}
SLOT_INC = [sum(16 * DMAS.get(PIECES[d][0], 1) for d in range(s, ND, RING)) for s in range(RING)]

VECTOR_DMAS, CACHED_DMAS = 11, 6
EXPERTS_AFTER = (D_KV + 1, D_G + 1, D_G + 3, D_G + 4)
GATES_AHEAD = ((0, 1), (2, 3), (4,))
GATES_WITH = ((5,), (6, 7), (8,), (9, 10), (11,), (12, 13), (14,), (15,))
H_WITH = 2
CH = 133


FREE = 1


def piece_landed(L, d):
    return L * SLOT_INC[d % RING] + sum(16 * DMAS.get(PIECES[x][0], 1) for x in range(d % RING, d + 1, RING))


def z_count(L, i):
    return Z_FIRST + L * Z_HALF + i // 2


def build(nc, inp, out, depth, alpha):
    with ExitStack() as ctx:
        def sb(name, shape, dt=F32, scope=ctx):
            return scope.enter_context(nc.sbuf_tensor(name, shape, dt))

        def sem(name):
            return ctx.enter_context(nc.semaphore(name))

        ps = ctx.enter_context(nc.psum_tensor("ps", [P, 8, 512], F32))

        cst = sb("cst", [P, NCONST])
        C = {k: cst[:, C_AT[k]:C_AT[k] + w] for k, w in CONSTS.items()}
        ident = C["ident"]
        experts = sb("experts", [P, QUAD, 3, KC * DE])
        dense = sb("dense", [P, RING, KC * 256])
        xT = sb("xT", [P, KC, T])
        prm_all = sb("prm_all", [P, depth, NV * KC])
        prm = sb("prm", [P, NV * KC])
        gperm_all = sb("gperm_all", [P, depth, 2, KC])
        gperm = sb("gperm", [P, 2, KC])
        ebias_all = sb("ebias_all", [P, depth, NE])
        ebias = sb("ebias", [P, NE])
        sink_all = sb("sink_all", [P, depth, NQ])
        kcT_all = sb("kcT_all", [P, depth, WIN])
        kcT = sb("kcT", [P, WIN])
        vc_all = sb("vc_all", [P, depth, NKV * HD])
        vc = sb("vc", [P, NKV * HD])
        sinkP = sb("sinkP", [P, KC, 2, 2])
        sinkS = sb("sinkS", [P, 2, 2])
        c8 = sb("c8", [P, 2, KC])
        stat = sb("stat", [P, NT, 2, 6])
        mv = sb("mv", [P, NT, 2])
        gate = sb("gate", [P, NT, NE])
        rank = sb("rank", [P, NT, NE])
        rounds = sb("rounds", [P, 2], I32)
        small = sb("small", [P, 64])
        st_rows = sb("st_rows", [P, P])
        k_rows = sb("k_rows", [P, 2, P])

        s1 = ExitStack()
        B1 = sb("B1", [P, KC, XC], scope=s1)
        B3 = sb("B3", [P, KC, XC], scope=s1)
        qT = sb("qT", [P, KC, T], scope=s1)
        s1a = ExitStack()
        wax = sb("wax", [P, 2, KC, P], scope=s1a)
        s1a.close()
        S = sb("S", [P, 2, 2, 3 * P], scope=s1)
        PTa = sb("PTa", [P, 2, 2, 3 * P], scope=s1)
        kT = sb("kT", [P, T], scope=s1)
        v = sb("v", [P, NT, NKV * HD], scope=s1)
        tmp = sb("tmp", [P, 2, U], scope=s1)
        st = sb("st", [P, 8, KC], scope=s1)
        ats = sb("ats", [P, 2, 5, 4], scope=s1)
        B4 = sb("B4", [P, KC, XC], scope=s1)
        B2 = sb("B2", [P, KC, XC], scope=s1)
        s1.close()
        B1f, B2f, B3f, B4f = (b[:, :, :].rearrange("p c t -> p (c t)") for b in (B1, B2, B3, B4))
        gr_s = B1f[:, 0:KC * T].rearrange("p (c t) -> p c t", c=KC)
        ga_s = B3f[:, 0:KC * T].rearrange("p (c t) -> p c t", c=KC)
        hT = B2f[:, 0:KC * T].rearrange("p (c t) -> p c t", c=KC)
        mT = B4f[:, 0:KC * T].rearrange("p (c t) -> p c t", c=KC)
        yP = hT
        u_, a_, gx_, gl_ = (f[:, 0:KC * U].rearrange("p (c t) -> p c t", c=KC) for f in (B2f, B2f, B3f, B4f))
        uF, aF, gxF, glF = (f[:, 0:KC * U] for f in (B2f, B2f, B3f, B4f))

        s2 = ExitStack()
        xh = sb("xh", [P, NT, D], F32R, scope=s2)
        xl = sb("xl", [P, NT - 1, D], F32R, scope=s2)
        s2a = ExitStack()
        tok = sb("tok", [P, NT, D], scope=s2a)
        s2a.close()
        xg = sb("xg", [P, KC, QUAD * CAP], scope=s2)
        oh = sb("oh", [P, NT, QUAD * CAP], F32R, scope=s2)
        ohT = sb("ohT", [P, 2, T], F32R, scope=s2)
        sil = sb("sil", [P, DE], scope=s2)
        hid = sb("hid", [P, DE], scope=s2)
        hidT = sb("hidT", [P, ME, 2 * CAP], scope=s2)
        s2b = ExitStack()
        rt = sb("rt", [P, NT, NE], scope=s2b)
        rt2 = sb("rt2", [P, NT, NE], scope=s2b)
        m8 = sb("m8", [P, NT, NG, 8], scope=s2b)
        gsp = sb("gsp", [P, NT, 12], scope=s2b)
        gs2 = sb("gs2", [P, NT, 12], scope=s2b)
        g8 = sb("g8", [P, NT, 8], scope=s2b)
        gm = sb("gm", [P, NT, NG], scope=s2b)
        t8 = sb("t8", [P, NT, 8], scope=s2b)
        sel = sb("sel", [P, NT, NE], scope=s2b)
        score = sb("score", [P, NT, NE], scope=s2b)
        tr = sb("tr", [P, NT, 8], scope=s2b)
        rs = sb("rs", [P, 8], scope=s2b)
        hs = sb("hs", [P, ME, T], scope=s2b)
        s2b.close()
        yh = sb("yh", [P, 2, D], F32R, scope=s2)
        yl = sb("yl", [P, 2, D], F32R, scope=s2)
        iota = sb("iota_w", [P, QUAD * CAP], scope=s2)
        gsl = sb("gsl", [P, 2], scope=s2)
        ffT = sb("ffT", [P, KC, T], scope=s2)
        s2.close()
        raw = B1f[:, 0:2 * depth * P].rearrange("p (k l c) -> p k l c", k=2, l=depth)


        consts_in = sem("consts_in")
        vectors_in = sem("vectors_in")
        cached_in = sem("cached_in")
        x_in = sem("x_in")
        rows_ready = sem("rows_ready")
        rows_kept = sem("rows_kept")
        dense_in = [sem(f"dense_in{s}") for s in range(RING)]
        w13_in = [sem(f"w13_in{e}") for e in range(QUAD)]
        w2_in = [sem(f"w2_in{e}") for e in range(QUAD)]
        wax_zero = sem("wax_zero")
        wax_in = sem("wax_in")
        z_ready = [sem(f"z_ready{b}") for b in range(2)]
        z_free = [sem(f"z_free{b}") for b in range(2)]
        neg_abs = sem("neg_abs")
        exp_abs = sem("exp_abs")
        stat_own = sem("stat_own")
        xc_used = sem("xc_used")
        own = sem("dve_own")
        act_own = sem("act_own")
        layer_prm = sem("layer_prm")
        xc_ready = sem("xc_ready")
        u_ready = sem("u_ready")
        q_ready = sem("q_ready")
        lru_gates = sem("lru_gates")
        gxu = sem("gxu")
        a_and_t = sem("a_and_t")
        m2_ready = sem("m2_ready")
        mult_ready = sem("mult_ready")
        h_scan = sem("h_scan")
        h_ready = sem("h_ready")
        st_ready = sem("st_ready")
        out_rows = sem("out_rows")
        out_kept = sem("out_kept")
        kv_stored = sem("kv_stored")
        states_stored = sem("states_stored")
        y_stored = sem("y_stored")
        s_scores = sem("s_scores")
        s_masked = sem("s_masked")
        s_max = sem("s_max")
        s_exp = sem("s_exp")
        s_norm = sem("s_norm")
        sam_pT = sem("sam_pT")
        s_pT = sem("s_pT")
        s_pT_kept = sem("s_pT_kept")
        s_o = sem("s_o")
        o_ready = sem("o_ready")
        gates_ready = sem("gates_ready")
        br_rnn_ready = sem("br_rnn_ready")
        br_ready = sem("br_ready")
        br_used = sem("br_used")

        tok_ps = sem("tok_ps")
        tok_act = sem("tok_act")
        tok_dve = sem("tok_dve")
        y_rows = sem("y_rows")
        var_ready = sem("var_ready")
        dev_ready = sem("dev_ready")
        norm_set = sem("norm_set")
        xh_ready = sem("xh_ready")
        xl_ready = sem("xl_ready")
        logits = sem("logits")
        score_clear = sem("score_clear")
        score_ready = sem("score_ready")
        sel_ready = sem("sel_ready")
        ranks = sem("ranks")
        rounds_set = sem("rounds_set")
        gate_ready = sem("gate_ready")
        sh_ready = sem("sh_ready")
        sh_silu = sem("sh_silu")
        sh_hid = sem("sh_hid")
        oh_ready = sem("oh_ready")
        xg_full = sem("xg_full")
        xg_kept = sem("xg_kept")
        w13_done = sem("w13_done")
        silu_done = sem("silu_done")
        hid_ready = sem("hid_ready")
        w2_done = sem("w2_done")
        hid_turned = sem("hid_turned")
        hidT_ready = sem("hidT_ready")
        yh_ready = sem("yh_ready")
        yl_ready = sem("yl_ready")
        ohT_full = sem("ohT_full")
        ohT_ready = sem("ohT_ready")
        c_full = sem("c_full")
        c_added = sem("c_added")
        next_round = sem("next_round")

        wait_carried = {e.engine: sem(f"wait_carried{i}") for i, e in enumerate((nc.sync, nc.gpsimd, nc.tensor, nc.scalar, nc.vector))}

        block = ctx.enter_context(nc.Block())

        def carry_wait(eng):
            eng.sem_inc(wait_carried[eng.engine], 1)

        @block.sync
        def _(sp):
            sp.dma_start(cst[:, :], inp["consts"]).then_inc(consts_in, 16)
            xp = inp["x_prompt"].rearrange("b (t p) d -> p (b t) d", p=P)
            sp.dma_start(tok[:, 0:2, :], xp).then_inc(x_in, 16)
            sp.dma_start(tok[0:TS, 2, :], inp["x_sample"].rearrange("b t d -> (b t) d")).then_inc(x_in, 16)

            def wait_piece_used(L, d):
                kind, at = PIECES[d]
                j = {D_IN: d, D_Q: d - D_Q, D_G: d - D_G}
                if d < D_Q:
                    i = Z_RNN + 2 * d + 1
                elif d < D_KV:
                    i = Z_Q + 2 * (d - D_Q) + 1
                elif d == D_KV:
                    i = Z_V
                elif d < D_BR:
                    i = Z_GATE + 2 * (d - D_G) + 1
                elif d < D_OUT:
                    sp.wait_ge(br_rnn_ready if kind == "br_rnn" else br_ready, L * KC + 2 * ((d - D_BR) // 2) + 2)
                    return
                elif d < D_ROUTER:
                    i = Z_OUT + 2 * (d - D_OUT) + 1
                elif kind == "router":
                    sp.wait_ge(logits, L + 1)
                    return
                else:
                    sp.wait_ge(sh_ready, L * 2 + (1 if kind == "s1" else 2))
                    return
                sp.wait_ge(z_ready[i % 2], z_count(L, i) + 1)

            def load_piece(L, d):
                kind, at = PIECES[d]
                slot = dense[:, d % RING, :]
                full = slot.rearrange("p (k c) -> p k c", k=KC)
                s = dense_in[d % RING]
                rows = lambda w: w[bass.ds(L, 1)].rearrange("l (k p) c -> p (l k) c", p=P)
                if d >= RING:
                    wait_piece_used(L, d - RING)
                else:
                    sp.wait_ge(z_ready[1], Z_FIRST + L * Z_HALF - (Z_N - Z_SH2 - KC) // 2)
                if kind == "q":
                    for c in range(2):
                        for g in range(2):
                            x = Q_OFF + (g * KC + 2 * at + c) * HD
                            sp.dma_start(full[:, :, c * P + g * HD:c * P + g * HD + HD], rows(inp["w_in"])[:, :, x:x + HD])\
                                .then_inc(s, 16)
                elif kind == "br_attn":
                    w = inp["w_br_attn"][bass.ds(L, 1)].rearrange("l (g k p) c -> g p (l k) c", g=2, p=HD)
                    for g in range(2):
                        sp.dma_start(full[g * HD:g * HD + HD, :, :], w[g, :, :, at:at + 256]).then_inc(s, 16)
                elif kind == "router":
                    dst = slot[:, 0:KC * NE].rearrange("p (k c) -> p k c", k=KC)
                    sp.dma_start(dst, rows(inp["w_router"])).then_inc(s, 16)
                elif kind == "s2":
                    dst = slot.rearrange("p (m c) -> p m c", m=ME)
                    sp.dma_start(dst, rows(inp["ws2"])).then_inc(s, 16)
                else:
                    w = {"in": "w_in", "br_rnn": "w_br_rnn", "out": "w_out", "s1": "ws1", "s3": "ws3"}[kind]
                    sp.dma_start(full, rows(inp[w])[:, :, at:at + 256]).then_inc(s, 16)

            def load_w13(L, i, u):
                for e in (2 * u, 2 * u + 1):
                    at = L * NE + i * QUAD + e
                    for j, w in enumerate(("w1", "w3")):
                        src = inp[w].rearrange("l e (p k) c -> (l e) p (k c)", k=KC)[bass.ds(at, 1)]
                        sp.dma_start(experts[:, e, j, :], src.rearrange("o p x -> p (o x)")).then_inc(w13_in[e], 16)

            def load_w2(L, i, u):
                for e in (2 * u, 2 * u + 1):
                    at = L * NE + i * QUAD + e
                    src = inp["w2"].rearrange("l e (m p) c -> (l e) p m c", p=P)[bass.ds(at, 1)]
                    dst = experts[:, e, 2, :].rearrange("p (m c) -> p m c", m=ME)
                    sp.dma_start(dst, src.rearrange("o p m c -> p (o m) c")).then_inc(w2_in[e], 16)

            done = sp.alloc_register("quads_done")
            sp.reg_mov(done, 0)
            with sp.Fori(0, depth) as L:
                for d in range(RING):
                    load_piece(L, d)
                q0 = sp.snap(done)
                for d in range(RING, ND):
                    load_piece(L, d)
                    if d == EXPERTS_AFTER[0]:
                        sp.wait_ge(w2_done, FREE + q0 * 4)
                    if d in EXPERTS_AFTER:
                        u, part = divmod(EXPERTS_AFTER.index(d), 2)
                        (load_w2 if part else load_w13)(L, 0, u)
                sp.wait_ge(rounds_set, L + 1)
                carry_wait(sp)
                nr = sp.value_load(rounds[0:1, 0:1], min_val=1, max_val=MAX_ROUNDS)
                with sp.Fori(1, nr * NQUAD) as t:
                    for u in range(2):
                        sp.wait_ge(w13_done, FREE + (q0 + t) * 2 + (u - 1))
                        load_w13(L, t % NQUAD, u)
                        sp.wait_ge(w2_done, FREE + (q0 + t) * 4 + (2 * u - 2))
                        load_w2(L, t % NQUAD, u)
                sp.reg_add(done, done, nr * NQUAD)

        @block.gpsimd
        def _(pool):
            pool.dma_start(raw[:, 1, :, :], inp["cache_k"].rearrange("l b t g d -> (b t) l (g d)")).then_inc(cached_in, 16)
            pool.dma_start(vc_all[:, :, :], inp["cache_v"].rearrange("l b t g d -> (b t) l (g d)")).then_inc(cached_in, 16)
            for j, name in enumerate(("ln1_g", "ln1_b")):
                pool.dma_start(gperm_all[:, :, j, :], inp[name].rearrange("l (p k) -> p l k", k=KC)).then_inc(cached_in, 16)
            wide = lambda w: w.rearrange("(o l) n -> o l n", o=1).to_broadcast((P, depth, w.shape[1]))
            pool.dma_start(ebias_all[:, :, :], wide(inp["e_bias"])).then_inc(cached_in, 16)
            pool.dma_start(sink_all[:, :, :], wide(inp["sinks"])).then_inc(cached_in, 16)
            with pool.Fori(0, depth) as L:
                for b in range(2):
                    pool.wait_ge(z_free[b], Z_FIRST + L * Z_HALF)
                carry_wait(pool)
                nc.gpsimd.memset(wax[:, :, :, :], 0.0).then_inc(wax_zero, 1)
                pool.wait_ge(wax_zero, L + 1)
                carry_wait(pool)
                for j, w in enumerate(("w_x", "w_a")):
                    src = inp[w][bass.ds(L, 1)].rearrange("l (c g) i o -> g i (l c) o", g=2)
                    for g in range(2):
                        pool.dma_start(wax[g * HD:g * HD + HD, j, :, g * HD:g * HD + HD], src[g]).then_inc(wax_in, 16)
                pool.wait_ge(z_free[Z_V % 2], z_count(L, Z_V) + 1)
                carry_wait(pool)
                rows = lambda o: o[bass.ds(L, 1)].rearrange("l b t g d -> (l b t) (g d)")
                pool.dma_start(rows(out["v_prompt"]), v[:, 1, :]).then_inc(kv_stored, 16)
                pool.dma_start(rows(out["v_sample"]), v[0:TS, 2, :]).then_inc(kv_stored, 16)
                pool.wait_ge(out_kept, 2 * L + 1)
                carry_wait(pool)
                pool.dma_start(rows(out["k_prompt"]), k_rows[:, 0, :]).then_inc(kv_stored, 16)
                pool.dma_start(rows(out["k_sample"]), k_rows[0:TS, 1, :]).then_inc(kv_stored, 16)
                pool.wait_ge(out_kept, 2 * L + 2)
                carry_wait(pool)
                hrow = lambda o: o[bass.ds(L, 1)].rearrange("l b (c p) -> (l b c) p", p=P)
                crow = lambda o: o[bass.ds(L, 1)].rearrange("l b j (c p) -> (l b j c) p", p=P)
                pool.dma_start(hrow(out["h_prompt"]), st_rows[0:KC, :]).then_inc(states_stored, 16)
                pool.dma_start(hrow(out["h_sample"]), st_rows[KC:2 * KC, :]).then_inc(states_stored, 16)
                pool.dma_start(crow(out["conv_prompt"]), st_rows[2 * KC:5 * KC, :]).then_inc(states_stored, 16)
                pool.dma_start(crow(out["conv_sample"]), st_rows[5 * KC:8 * KC, :]).then_inc(states_stored, 16)
                pool.wait_ge(kv_stored, (L + 1) * 64)
                pool.wait_ge(states_stored, (L + 1) * 64)
            pool.wait_ge(y_rows, 2 * NT)
            yp = out["y_prompt"].rearrange("b (t p) d -> p (b t) d", p=P)
            pool.dma_start(yp, tok[:, 0:2, :]).then_inc(y_stored, 16)
            pool.dma_start(out["y_sample"].rearrange("b t d -> (b t) d"), tok[0:TS, 2, :]).then_inc(y_stored, 16)
            pool.wait_ge(y_stored, 32)

        @block.tensor
        def _(pe):
            mm, transpose = nc.tensor.matmul, nc.tensor.transpose

            def bank_of(L, i):
                pe.wait_ge(z_free[i % 2], z_count(L, i))
                return ps[:, i % 2, :]

            def over_features(bank, d, col, rhs, n):
                w = dense[:, d % RING, :].rearrange("p (k c) -> p k c", k=KC)
                for k in range(KC):
                    last = mm(bank[:, 0:n], w[:, k, col:col + P], rhs(k), start=k == 0, stop=k == KC - 1)
                return last

            def piece(L, d):
                pe.wait_ge(dense_in[d % RING], piece_landed(L, d))

            def fill_xT(wait):
                for c in range(KC):
                    wait(c)
                    for t, (at, n) in enumerate(TOK):
                        last = transpose(ps[:, c % 2, at:at + n], tok[0:n, t, c * P:c * P + P], ident[0:n, 0:n])
                    last.then_inc(z_ready[c % 2], 1)

            def to_tokens(src):
                for t, (at, n) in enumerate(TOK):
                    for h in range(2):
                        for c in range(4):
                            last = transpose(ps[0:n, 2 + 2 * t + h, c * P:c * P + P], src[:, 4 * h + c, at:at + n], ident)
                        last.then_inc(tok_ps, 1)

            for s in (w13_done, w2_done, c_full, ohT_full, hid_turned):
                pe.sem_inc(s, FREE)
            pe.wait_ge(consts_in, 16)
            pe.wait_ge(x_in, 32)
            fill_xT(lambda c: pe.wait_ge(z_free[c % 2], c // 2) if c >= 2 else None)
            pe.wait_ge(vectors_in, VECTOR_DMAS * 16)
            pe.wait_ge(cached_in, CACHED_DMAS * 16)
            for l in range(depth):
                transpose(ps[:, 2, l * P:l * P + P], raw[:, 0, l, :], ident)
                last = transpose(ps[:, 3, l * P:l * P + P], raw[:, 1, l, :], ident)
            last.then_inc(rows_ready, 1)

            done = pe.alloc_register("quads_done")
            pe.reg_mov(done, 0)
            with pe.Fori(0, depth) as L:
                xk = lambda k: xT[:, k, :]
                for b in range(2):
                    pe.wait_ge(z_free[b], Z_FIRST + L * Z_HALF)

                for m in range(KC):
                    if m % 2 == 0:
                        piece(L, D_IN + m // 2)
                    over_features(bank_of(L, Z_RNN + m), D_IN + m // 2, m % 2 * P, xk, T).then_inc(z_ready[m % 2], 1)
                for c in range(KC):
                    d = D_Q + c // 2
                    if c % 2 == 0:
                        piece(L, d)
                    bank = bank_of(L, Z_Q + c)
                    over_features(bank, d, c % 2 * P, xk, T).then_inc(z_ready[c % 2], 1)
                piece(L, D_KV)
                over_features(bank_of(L, Z_K), D_KV, 0, xk, T).then_inc(z_ready[Z_K % 2], 1)
                bank = bank_of(L, Z_V)
                w = dense[:, D_KV % RING, :].rearrange("p (k c) -> p k c", k=KC)
                for t, (at, n) in enumerate(TOK):
                    for k in range(KC):
                        last = mm(bank[0:n, t * P:t * P + P], xT[:, k, at:at + n], w[:, k, P:2 * P], start=k == 0, stop=k == KC - 1)
                last.then_inc(z_ready[Z_V % 2], 1)
                pe.wait_ge(wax_in, (L + 1) * 64)
                for c in range(KC):
                    pe.wait_ge(u_ready, L * KC + c + 1)
                    for j in range(2):
                        bank = bank_of(L, Z_LRU + 2 * c + j)
                        mm(bank[:, 0:U], wax[:, j, c, :], u_[:, c, :], start=True, stop=True).then_inc(z_ready[j], 1)
                def gate_chunks(ms):
                    for m in ms:
                        d = D_G + m // 2
                        if m % 2 == 0:
                            piece(L, d)
                        over_features(bank_of(L, Z_GATE + m), d, m % 2 * P, xk, T).then_inc(z_ready[m % 2], 1)

                pe.wait_ge(q_ready, L * (KC + 1) + KC + 1)
                transpose(ps[:, 7, 0:P], kT[:, TP - WIN:TP], ident)
                transpose(ps[0:TS, 7, P:2 * P], kT[:, TP:T], ident).then_inc(out_rows, 1)

                for h in range(2):
                    lo, hi = h * HD, h * HD + HD
                    for a in range(2):
                        for i in range(4):
                            q = qT[lo:hi, 4 * a + i, TP:T]
                            o = ps[32 * i:32 * i + 32, 2 + h, a * 160:a * 160 + 160]
                            mm(o[:, 0:WIN], q, kcT[lo:hi, :], start=True, stop=True)
                            last = mm(o[:, WIN:WIN + TS], q, kT[lo:hi, TP:T], start=True, stop=True)
                last.then_inc(s_scores, 1)
                gate_chunks(GATES_AHEAD[0])
                pe.wait_ge(s_norm, L * (KC + 1) + 1)
                for h in range(2):
                    for a in range(2):
                        p = S[:, 0, h, a * 160:a * 160 + 160]
                        transpose(ps[:, 4 + h, a * P:a * P + P], p[:, 0:WIN], ident)
                        last = transpose(ps[0:TS, 4 + h, (2 + a) * P:(3 + a) * P], p[:, WIN:WIN + TS], ident)
                last.then_inc(s_pT, 1)
                gate_chunks(GATES_AHEAD[1])
                pe.wait_ge(z_free[Z_V % 2], z_count(L, Z_V) + 1)
                pe.wait_ge(s_pT_kept, L * (KC + 1) + 1)
                for h in range(2):
                    lo, hi = h * HD, h * HD + HD
                    pt = PTa[:, 0, :, :].rearrange("p h x -> p (h x)")[:, h * 256:h * 256 + 256]
                    ptn = PTa[:, 1, :, :].rearrange("p h x -> p (h x)")[:, h * 256:h * 256 + 256]
                    for a in range(2):
                        o = ps[lo:hi, 6, a * P:a * P + P]
                        mm(o, vc[:, lo:hi], pt[:, a * P:a * P + P], start=True, stop=False)
                        last = mm(o, v[0:TS, 2, lo:hi], ptn[0:TS, a * P:a * P + P], start=False, stop=True)
                last.then_inc(s_o, 1)

                gate_chunks(GATES_AHEAD[2])

                def pair_scores(c):
                    if c == 0:
                        pe.wait_ge(s_exp, L * (KC + 1) + 1)
                    else:
                        pe.wait_ge(s_masked, L * KC + c)
                    for h in range(2):
                        lo, hi = h * HD, h * HD + HD
                        mm(ps[:, 2 + h, 0:TP], qT[lo:hi, c, P:TP], kT[lo:hi, 0:TP], start=True, stop=True)
                        last = mm(ps[:, 2 + h, TP:TP + P], qT[lo:hi, c, 0:P], kT[lo:hi, 0:P], start=True, stop=True)
                    last.then_inc(s_scores, 1)

                def pair_output(c):
                    n = L * (KC + 1) + c + 1
                    pe.wait_ge(s_pT_kept, n + 1)
                    pe.wait_ge(o_ready, n)
                    for h in range(2):
                        lo, hi = h * HD, h * HD + HD
                        pt = PTa[:, c % 2, h, :]
                        mm(ps[lo:hi, 6, P:2 * P], v[:, 0, lo:hi], pt[:, 0:P], start=True, stop=False)
                        mm(ps[lo:hi, 6, P:2 * P], v[:, 1, lo:hi], pt[:, P:2 * P], start=False, stop=True)
                        last = mm(ps[lo:hi, 6, 0:P], v[:, 0, lo:hi], pt[:, 2 * P:3 * P], start=True, stop=True)
                    last.then_inc(s_o, 1)

                pair_scores(0)
                for c in range(KC):
                    n = L * (KC + 1) + c + 1
                    if c < KC - 1:
                        pair_scores(c + 1)
                    gate_chunks(GATES_WITH[c])
                    pe.wait_ge(s_norm, n + 1)
                    pe.wait_ge(s_pT_kept, n)
                    for h in range(2):
                        for k in range(3):
                            last = transpose(ps[:, 4 + h, k * P:k * P + P], S[:, c % 2, h, k * P:k * P + P], ident)
                    last.then_inc(s_pT, 1)
                    if c > 0:
                        pair_output(c - 1)
                pair_output(KC - 1)

                pe.wait_ge(st_ready, L + 1)
                pe.wait_ge(out_kept, 2 * L + 1)
                carry_wait(pe)
                transpose(ps[0:8 * KC, 7, 0:P], st[:, :, :].rearrange("p v c -> p (v c)"), ident).then_inc(out_rows, 1)

                pe.wait_ge(h_ready, L + 1)
                pe.wait_ge(o_ready, (L + 1) * (KC + 1))
                for j in range(KC // 2):
                    for i, (src, sig) in enumerate(((hT, br_rnn_ready), (qT, br_ready))):
                        d = D_BR + 2 * j + i
                        piece(L, d)
                        for m in (2 * j, 2 * j + 1):
                            if m >= 2 and i == 0:
                                pe.wait_ge(br_used, L * KC + m - 1)
                            over_features(ps[:, 2 + 2 * i + m % 2, :], d, m % 2 * P, lambda k: src[:, k, :], T).then_inc(sig, 1)
                pe.wait_ge(br_used, (L + 1) * KC)
                for m in range(KC):
                    if m % 2 == 0:
                        piece(L, D_OUT + m // 2)
                    over_features(bank_of(L, Z_OUT + m), D_OUT + m // 2, m % 2 * P, lambda k: mT[:, k, :], T)\
                        .then_inc(z_ready[m % 2], 1)
                for b in range(2):
                    pe.wait_ge(z_free[b], z_count(L, Z_OUT + KC))
                pe.wait_ge(out_kept, 2 * L + 2)
                to_tokens(yP)
                pe.wait_ge(tok_act, (2 * L + 1) * NT)
                pe.wait_ge(tok_dve, (2 * L + 1) * NT)
                fill_xT(lambda c: bank_of(L, Z_FILL1 + c))

                piece(L, D_ROUTER)
                for b in range(2):
                    pe.wait_ge(z_free[b], z_count(L, Z_FILL1 + KC))
                w = dense[:, D_ROUTER % RING, 0:KC * NE].rearrange("p (k c) -> p k c", k=KC)
                for t, (at, n) in enumerate(TOK):
                    for k in range(KC):
                        last = mm(ps[0:n, 2, t * NE:t * NE + NE], xT[:, k, at:at + n], w[:, k, :], start=k == 0, stop=k == KC - 1)
                last.then_inc(logits, 1)
                for j in range(2):
                    piece(L, D_ROUTER + 1 + j)
                    for m in range(ME):
                        last = over_features(ps[:, 4 + 2 * j + m, :], D_ROUTER + 1 + j, m * P, xk, T)
                    last.then_inc(sh_ready, 1)
                pe.wait_ge(sel_ready, L + 1)
                for t in range(NT):
                    o = ps[:, 3, t * NE:t * NE + NE]
                    for x in range(t):
                        mm(o, C["ones"], sel[:, x, :], start=x == 0, stop=False)
                    mm(o, C["upper"], sel[:, t, :], start=t == 0, stop=True)
                for t in range(NT):
                    last = mm(ps[:, 3, NT * NE:(NT + 1) * NE], C["ones"], sel[:, t, :], start=t == 0, stop=t == NT - 1)
                last.then_inc(ranks, 1)
                d = D_ROUTER + 3
                piece(L, d)
                pe.wait_ge(sh_hid, (L + 1) * 2)
                w = dense[:, d % RING, :].rearrange("p (m c) -> p m c", m=ME)
                for c in range(KC):
                    bank = bank_of(L, Z_SH2 + c)
                    for m in range(ME):
                        last = mm(bank[:, 0:T], w[:, m, c * P:c * P + P], hs[:, m, :], start=m == 0, stop=m == ME - 1)
                    last.then_inc(z_ready[c % 2], 1)

                def gather(n, js=range(4)):
                    pe.wait_ge(oh_ready, n + 1)
                    for j in js:
                        if j >= 2:
                            pe.wait_ge(xg_kept, n * 4 + (j - 1))
                        for k in (2 * j, 2 * j + 1):
                            o = ps[:, j % 2, k % 2 * 256:k % 2 * 256 + 256]
                            x = slice(k * P, k * P + P)
                            if k == 0:
                                pe.wait_ge(xh_ready, (L + 1) * NT)
                                pe.wait_ge(xl_ready, (L + 1) * NT)
                            for t in range(NT - 1):
                                mm(o, xh[:, t, x], oh[:, t, :], start=t == 0, stop=False)
                                mm(o, xl[:, t, x], oh[:, t, :], start=False, stop=False)
                            last = mm(o, xh[0:2 * TS, NT - 1, x], oh[0:2 * TS, NT - 1, :], start=False, stop=True)
                        last.then_inc(xg_full, 1)

                def up(n, u):
                    pe.wait_ge(xg_kept, n * 4 + 4)
                    pe.wait_ge(hidT_ready, FREE + n * 2 + u)
                    for e in (2 * u, 2 * u + 1):
                        pe.wait_ge(w13_in[e], (n + 1) * 32)
                    for k in range(KC):
                        for e in (2 * u, 2 * u + 1):
                            last = mm(ps[e % 2 * CAP:(e % 2 + 1) * CAP, 2, :], xg[:, k, e * CAP:e * CAP + CAP],
                                      experts[:, e, 0:2, k * DE:k * DE + DE], start=k == 0, stop=k == KC - 1)
                    last.then_inc(w13_done, 1)

                def turn(n, u):
                    pe.wait_ge(hid_ready, FREE + n * 2 + u + 1)
                    for m in range(ME):
                        last = transpose(ps[:, 2, m * P:m * P + P], hid[:, m * P:m * P + P], ident)
                    last.then_inc(hid_turned, 1)

                def down(n, u):
                    pe.wait_ge(hidT_ready, FREE + n * 2 + u + 1)
                    pe.wait_ge(yl_ready, FREE + (n * 2 + u) * 2)
                    for e in (2 * u, 2 * u + 1):
                        pe.wait_ge(w2_in[e], (n + 1) * 16)
                    for b in range(2):
                        for m in range(ME):
                            for e in (2 * u, 2 * u + 1):
                                last = mm(ps[e % 2 * CAP:(e % 2 + 1) * CAP, 3 + b, :], hidT[:, m, e % 2 * CAP:(e % 2 + 1) * CAP],
                                          experts[:, e, 2, m * D + b * 512:m * D + b * 512 + 512], start=m == 0, stop=m == ME - 1)
                        last.then_inc(w2_done, 1)

                def slots_to_tokens(n, i, u):
                    pe.wait_ge(ohT_ready, FREE + n * 2 + u)
                    o = oh[:, :, u * P:u * P + P].bitcast(F32)
                    for t, (at, r) in enumerate(TOK):
                        transpose(ps[:, 7, at:at + r], o[0:r, t, :], ident[0:r, 0:r])
                    for t in range(NT):
                        g = gate[:, t, bass.ds(i * QUAD + 2 * u, 2)]
                        last = mm(ps[:, 7, T:T + 2], o[:, t, :], g, start=t == 0, stop=t == NT - 1)
                    last.then_inc(ohT_full, 1)

                def combine(n):
                    pe.wait_ge(ohT_ready, FREE + n * 2 + 2)
                    pe.wait_ge(yl_ready, FREE + n * 4 + 4)
                    for c in range(KC):
                        pe.wait_ge(c_added, FREE + n * KC + max(c - 1, 0))
                        o = ps[:, 5 + c % 2, 0:T]
                        for u in range(2):
                            mm(o, yh[:, u, c * P:c * P + P], ohT[:, u, :], start=u == 0, stop=False)
                            last = mm(o, yl[:, u, c * P:c * P + P], ohT[:, u, :], start=False, stop=u == 1)
                        last.then_inc(c_full, 1)

                def quad(n, i, first=False, last=False):
                    up(n, 0)
                    if not first:
                        combine(n - 1)
                    slots_to_tokens(n, i, 0)
                    turn(n, 0)
                    slots_to_tokens(n, i, 1)
                    down(n, 0)
                    up(n, 1)
                    if not last:
                        gather(n + 1, range(2))
                    turn(n, 1)
                    if not last:
                        gather(n + 1, range(2, 4))
                    down(n, 1)

                for b in range(2):
                    pe.wait_ge(z_free[b], z_count(L, Z_SH2 + KC))
                pe.wait_ge(rounds_set, L + 1)
                carry_wait(pe)
                nr = pe.value_load(rounds[0:1, 0:1], min_val=1, max_val=MAX_ROUNDS)
                with pe.Fori(0, nr) as r:
                    q = pe.snap(done)
                    gather(q)
                    quad(q, 0, first=True)
                    with pe.Fori(1, NQUAD - 1) as i:
                        quad(q + i, i)
                    quad(q + (NQUAD - 1), NQUAD - 1, last=True)
                    combine(q + (NQUAD - 1))
                    pe.reg_add(done, done, NQUAD)

                pe.wait_ge(c_added, FREE + pe.snap(done) * KC)
                to_tokens(ffT)
                pe.wait_ge(tok_act, (2 * L + 2) * NT)
                pe.wait_ge(tok_dve, (2 * L + 2) * NT)
                fill_xT(lambda c: bank_of(L, Z_FILL2 + c))

            for b in range(2):
                pe.wait_ge(z_free[b], Z_FIRST + depth * Z_HALF)
            to_tokens(xT)

        @block.scalar
        def _(act):
            activation = nc.scalar.activation

            act.sem_inc(hidT_ready, FREE)
            def rows_of(w, at, n):
                act.dma_start(raw[at * KC:(at + n) * KC, 0, :, :], w).then_inc(vectors_in, 16)
            rows_of(inp["conv_w"].rearrange("l j (c p) -> (j c) l p", p=P), V_CW, CONV_W)
            for at, name in ((V_CB, "conv_b"), (V_BA, "b_a"), (V_BX, "b_x"), (V_AP, "a_param"), (V_G1, "ln1_g"),
                             (V_B1, "ln1_b"), (V_G2, "ln2_g"), (V_B2, "ln2_b")):
                rows_of(inp[name].rearrange("l (c p) -> c l p", p=P), at, 1)
            rows_of(inp["state_h"].rearrange("l b (c p) -> (b c) l p", p=P), V_H0, 1)
            rows_of(inp["state_conv"].rearrange("l b j (c p) -> (b j c) l p", p=P), V_CS, CONV_W - 1)

            def z_item(L, i):
                act.wait_ge(z_ready[i % 2], z_count(L, i) + 1)
                return ps[:, i % 2, :]

            for c in range(0, KC, 2):
                act.wait_ge(z_ready[0], c // 2 + 1)
                activation(xT[:, c, :], ps[:, 0, 0:T], ACT.Copy).then_inc(z_free[0], 1)

            def norm_rows(L, k):
                for t, (at, n) in enumerate(TOK):
                    act.wait_ge(var_ready, (2 * L + k) * NT + (t + 1))
                    activation(mv[0:n, t, 1:2], mv[0:n, t, 1:2], ACT.Sqrt).then_inc(dev_ready, 1)
                for t, (at, n) in enumerate(TOK):
                    act.wait_ge(norm_set, (2 * L + k) * NT + (t + 1))
                    activation(tok[0:n, t, 512:D], ps[0:n, 3 + 2 * t, :], ACT.Identity, bias=mv[0:n, t, 0:1],
                               scale=mv[0:n, t, 1:2]).then_inc(tok_act, 1)

            def norm_back(L, g, b, first):
                for c in range(0, KC, 2):
                    bank = z_item(L, first + c)
                    activation(xT[:, c, :], bank[:, 0:T], ACT.Identity, bias=prm[:, b * KC + c:b * KC + c + 1],
                               scale=prm[:, g * KC + c:g * KC + c + 1]).then_inc(z_free[0], 1)

            done = act.alloc_register("quads_done")
            act.reg_mov(done, 0)
            with act.Fori(0, depth) as L:
                act.wait_ge(neg_abs, L + 1)
                activation(small[:, 0:KC], small[:, 0:KC], ACT.Exp).then_inc(exp_abs, 1)
                act.wait_ge(rows_kept, 2)
                for m in range(KC):
                    bank = z_item(L, Z_RNN + m)
                    activation(B1[:, m, CONV_W - 1:CONV_W - 1 + TP], bank[:, 0:TP], ACT.Copy)
                    activation(B1[:, m, XC - TS:XC], bank[:, TP:T], ACT.Copy).then_inc(z_free[m % 2], 1)
                bank = z_item(L, Z_V)
                activation(v[:, 0:2, :], bank[:, 0:2 * P].rearrange("p (t c) -> p t c", t=2), ACT.Copy)
                activation(v[0:TS, 2, :], bank[0:TS, 2 * P:3 * P], ACT.Copy).then_inc(z_free[Z_V % 2], 1)
                act.wait_ge(layer_prm, L + 1)
                for c in range(KC):
                    for j, (dst, b) in enumerate(((gx_, V_BX), (gl_, V_BA))):
                        bank = z_item(L, Z_LRU + 2 * c + j)
                        activation(dst[:, c, :], bank[:, 0:U], ACT.Sigmoid, bias=prm[:, b * KC + c:b * KC + c + 1])\
                            .then_inc(z_free[j], 1)
                act.wait_ge(s_max, L * (KC + 1) + 1)
                for h in range(2):
                    for a in range(2):
                        x = 2 * h + a
                        activation(S[:, 0, h, a * 160:a * 160 + 160], ps[:, 2 + h, a * 160:a * 160 + 160], ACT.Exp,
                                   bias=ats[:, 0, 1, x:x + 1], scale=SCALE, accum_out=ats[:, 0, 2, x:x + 1])
                activation(ats[:, 0, 4, :], ats[:, 0, 3, :], ACT.Exp).then_inc(s_exp, 1)
                act.wait_ge(gxu, L + 1)
                act.wait_ge(z_free[1], z_count(L, Z_LRU + 2 * KC))
                for c in range(KC):
                    activation(a_[:, c, :], gl_[:, c, :], ACT.Exp, scale=c8[:, 0, c:c + 1]).then_inc(act_own, 1)
                act.wait_ge(act_own, (L + 1) * KC)
                for c in range(KC):
                    activation(gl_[:, c, :], gl_[:, c, :], ACT.Tanh, scale=c8[:, 1, c:c + 1]).then_inc(a_and_t, 1)

                def keep_gates(ms):
                    for m in ms:
                        bank = z_item(L, Z_GATE + m)
                        dst = gr_s[:, m, :] if m < KC else ga_s[:, m - KC, :]
                        activation(dst, bank[:, 0:T], ACT.Tanh, scale=0.5).then_inc(z_free[m % 2], 1)

                act.wait_ge(xc_used, L + 1)
                keep_gates(GATES_AHEAD[0])
                act.wait_ge(s_pT, L * (KC + 1) + 1)
                ptc = PTa[:, 0, :, :].rearrange("p h x -> p (h x)")
                ptn = PTa[0:TS, 1, :, :].rearrange("p h x -> p (h x)")
                for h in range(2):
                    activation(ptc[:, h * 256:h * 256 + 256], ps[:, 4 + h, 0:256], ACT.Copy)
                    last = activation(ptn[:, h * 256:h * 256 + 256], ps[0:TS, 4 + h, 256:512], ACT.Copy)
                last.then_inc(s_pT_kept, 1)
                keep_gates(GATES_AHEAD[1])
                act.wait_ge(m2_ready, (L + 1) * (KC // 2))
                activation(glF, glF, ACT.Sqrt).then_inc(mult_ready, 1)
                keep_gates(GATES_AHEAD[2])

                def exponentials(c):
                    w = c % 2
                    act.wait_ge(s_max, L * (KC + 1) + c + 2)
                    for b, (lo, hi) in enumerate(((0, TP), (TP, TP + P))):
                        for h in range(2):
                            x = 2 * b + h
                            activation(S[:, w, h, lo:hi], S[:, w, h, lo:hi], ACT.Exp, bias=ats[:, w, 1, x:x + 1],
                                       scale=SCALE, accum_out=ats[:, w, 2, x:x + 1])
                    activation(ats[:, w, 4, :], ats[:, w, 3, :], ACT.Exp).then_inc(s_exp, 1)

                exponentials(0)
                for c in range(KC):
                    n = L * (KC + 1) + c + 1
                    w = c % 2
                    if c == H_WITH:
                        act.wait_ge(h_scan, L + 1)
                        activation(hT[:, :, 0:TP], gl_[:, :, 0:TP], ACT.Copy)
                        activation(hT[:, :, TP:T], gl_[:, :, US:U], ACT.Copy).then_inc(h_ready, 1)
                    if c < KC - 1:
                        exponentials(c + 1)
                    keep_gates(GATES_WITH[c])
                    act.wait_ge(s_pT, n + 1)
                    act.wait_ge(s_o, L * (KC + 1) + max(c, 1))
                    activation(PTa[:, w, 0, :], ps[:, 4, 0:3 * P], ACT.Copy)
                    activation(PTa[:, w, 1, :], ps[:, 5, 0:3 * P], ACT.Copy).then_inc(s_pT_kept, 1)

                norm_rows(L, 0)
                for t, (at, n) in enumerate(TOK):
                    act.wait_ge(tok_act, (2 * L) * NT + (t + 1))
                    act.wait_ge(tok_dve, (2 * L) * NT + (t + 1))
                    activation(xh[0:n, t, :].rearrange("p (k f) -> p f k", k=KC),
                               tok[0:n, t, :].rearrange("p (f k) -> p f k", k=KC), ACT.Copy).then_inc(xh_ready, 1)
                norm_back(L, V_G1, V_B1, Z_FILL1)
                act.wait_ge(logits, L + 1)
                act.wait_ge(score_clear, L + 1)
                activation(score[:, 0:2, :], ps[:, 2, 0:2 * NE].rearrange("p (t e) -> p t e", t=2), ACT.Sigmoid)
                activation(score[0:TS, 2, :], ps[0:TS, 2, 2 * NE:3 * NE], ACT.Sigmoid).then_inc(score_ready, 1)
                act.wait_ge(kv_stored, (L + 1) * 64)
                act.wait_ge(sh_ready, L * 2 + 1)
                for m in range(ME):
                    activation(hs[:, m, :], ps[:, 4 + m, 0:T], ACT.Silu).then_inc(sh_silu, 1)

                def keep_gathered(n, js=range(4)):
                    act.wait_ge(w13_done, FREE + n * 2)
                    for j in js:
                        act.wait_ge(xg_full, n * 4 + (j + 1))
                        for k in (2 * j, 2 * j + 1):
                            last = activation(xg[:, k, :], ps[:, j % 2, k % 2 * 256:k % 2 * 256 + 256], ACT.Identity,
                                              bias=gperm[:, 1, k:k + 1], scale=gperm[:, 0, k:k + 1])
                        last.then_inc(xg_kept, 1)

                def silu(n, u):
                    p = n * 2 + u
                    act.wait_ge(w13_done, FREE + p + 1)
                    act.wait_ge(hid_ready, FREE + p)
                    activation(sil[:, :], ps[:, 2, 0:DE], ACT.Silu).then_inc(silu_done, 1)

                def keep_hidden(n, u):
                    p = n * 2 + u
                    act.wait_ge(w2_done, FREE + p * 2)
                    act.wait_ge(hid_turned, FREE + p + 1)
                    activation(hidT[:, :, :].rearrange("p m s -> p (m s)"), ps[:, 2, 0:ME * P], ACT.Copy).then_inc(hidT_ready, 1)

                def high_part(n, u):
                    p = n * 2 + u
                    act.wait_ge(ohT_ready, FREE + p + 1)
                    act.wait_ge(c_full, FREE + n * KC)
                    for b in range(2):
                        act.wait_ge(w2_done, FREE + p * 2 + (b + 1))
                        activation(yh[:, u, 512 * b:512 * b + 512], ps[:, 3 + b, :], ACT.Identity, scale=gsl[:, u:u + 1])\
                            .then_inc(yh_ready, 1)

                def quad(n, last=False):
                    silu(n, 0)
                    keep_hidden(n, 0)
                    high_part(n, 0)
                    silu(n, 1)
                    if not last:
                        keep_gathered(n + 1, range(2))
                    keep_hidden(n, 1)
                    if not last:
                        keep_gathered(n + 1, range(2, 4))
                    high_part(n, 1)

                act.wait_ge(rounds_set, L + 1)
                carry_wait(act)
                nr = act.value_load(rounds[0:1, 0:1], min_val=1, max_val=MAX_ROUNDS)
                with act.Fori(0, nr) as r:
                    q = act.snap(done)
                    keep_gathered(q)
                    with act.Fori(0, NQUAD - 1) as i:
                        quad(q + i)
                    quad(q + (NQUAD - 1), last=True)
                    act.reg_add(done, done, NQUAD)

                norm_rows(L, 1)
                norm_back(L, V_G2, V_B2, Z_FILL2)

            for t, (at, n) in enumerate(TOK):
                act.wait_ge(tok_ps, (2 * depth + 0) * 2 * NT + 2 * t + 2)
                activation(tok[0:n, t, 512:D], ps[0:n, 3 + 2 * t, :], ACT.Copy).then_inc(y_rows, 1)

        @block.vector
        def _(dve):
            V = nc.vector
            steps = [0]
            before = [0]

            def link(ins, plain=False):
                steps[0] += 1
                ins.then_inc(own, 1)
                dve.wait_ge(own, before[0] + steps[0])
                if plain:
                    carry_wait(dve)

            def z_item(L, i):
                dve.wait_ge(z_ready[i % 2], z_count(L, i) + 1)
                return ps[:, i % 2, :]

            for s in (hid_ready, yl_ready, ohT_ready, c_added):
                dve.sem_inc(s, FREE)
            for c in range(1, KC, 2):
                dve.wait_ge(z_ready[1], c // 2 + 1)
                V.tensor_copy(xT[:, c, :], ps[:, 1, 0:T]).then_inc(z_free[1], 1)
            dve.wait_ge(rows_ready, 1)
            V.tensor_copy(prm_all[:, :, :], ps[:, 2, 0:depth * P].rearrange("p (l c) -> p l c", l=depth)).then_inc(rows_kept, 1)
            V.tensor_copy(kcT_all[:, :, :], ps[:, 3, 0:depth * P].rearrange("p (l c) -> p l c", l=depth)).then_inc(rows_kept, 1)
            dve.wait_ge(rows_kept, 2)

            def stats(L, k, eps):
                base = (2 * L + k) * 4 * NT
                for t, (at, n) in enumerate(TOK):
                    for h in range(2):
                        dve.wait_ge(tok_ps, (2 * L + k) * 2 * NT + (2 * t + h + 1))
                        V.bn_stats(stat[0:n, t, h, :], ps[0:n, 2 + 2 * t + h, :]).then_inc(stat_own, 1)
                    dve.wait_ge(stat_own, base + (3 * t + 2))
                    carry_wait(dve)
                    V.bn_aggr(mv[0:n, t, :], stat[0:n, t, :, :]).then_inc(stat_own, 1)
                    dve.wait_ge(stat_own, base + (3 * t + 3))
                    V.tensor_scalar(mv[0:n, t, 1:2], mv[0:n, t, 1:2], eps, None, ALU.add).then_inc(var_ready, 1)
                for t, (at, n) in enumerate(TOK):
                    dve.wait_ge(dev_ready, (2 * L + k) * NT + (t + 1))
                    V.reciprocal(mv[0:n, t, 1:2], mv[0:n, t, 1:2]).then_inc(stat_own, 1)
                    dve.wait_ge(stat_own, base + (3 * NT + t + 1))
                    V.scalar_tensor_tensor(mv[0:n, t, 0:1], mv[0:n, t, 0:1], -1.0, mv[0:n, t, 1:2], ALU.mult, ALU.mult)\
                        .then_inc(norm_set, 1)
                    dve.wait_ge(norm_set, (2 * L + k) * NT + (t + 1))
                    V.tensor_scalar(tok[0:n, t, 0:512], ps[0:n, 2 + 2 * t, :], mv[0:n, t, 1:2], mv[0:n, t, 0:1],
                                    ALU.mult, ALU.add).then_inc(tok_dve, 1)

            def norm_back(L, g, b, first):
                for c in range(1, KC, 2):
                    bank = z_item(L, first + c)
                    V.tensor_scalar(xT[:, c, :], bank[:, 0:T], prm[:, g * KC + c:g * KC + c + 1],
                                    prm[:, b * KC + c:b * KC + c + 1], ALU.mult, ALU.add).then_inc(z_free[1], 1)

            done = dve.alloc_register("quads_done")
            dve.reg_mov(done, 0)
            with dve.Fori(0, depth) as L:
                before[0] = L * CH
                for b in range(2):
                    dve.wait_ge(z_free[b], Z_FIRST + L * Z_HALF)
                dve.wait_ge(cached_in, CACHED_DMAS * 16)
                V.tensor_copy(prm[:, :], prm_all[:, bass.ds(L, 1), :].rearrange("p o c -> p (o c)"))
                V.tensor_copy(gperm[:, :, :], gperm_all[:, bass.ds(L, 1), :, :].rearrange("p o j k -> p (o j) k"))
                V.tensor_copy(ebias[:, :], ebias_all[:, bass.ds(L, 1), :].rearrange("p o c -> p (o c)"))
                V.tensor_copy(kcT[:, :], kcT_all[:, bass.ds(L, 1), :].rearrange("p o c -> p (o c)"))
                V.tensor_copy(vc[:, :], vc_all[:, bass.ds(L, 1), :].rearrange("p o c -> p (o c)"))
                sk = sink_all[:, bass.ds(L, 1), :].rearrange("p o (h c) -> p (o c) h", h=2)
                V.tensor_copy(sinkP[:, :, 0, :], sk)
                link(V.tensor_copy(sinkP[:, :, 1, :], sk))
                for i in range(4):
                    x = slice(32 * i, 32 * i + 32)
                    last = V.tensor_copy(sinkS[x, :, :], sinkP[x, i:KC:4, 0, :].rearrange("p a h -> p h a"))
                link(last)
                ap = prm[:, V_AP * KC:V_AP * KC + KC]
                e, s_, s2_, p_ = (small[:, 8 * j:8 * j + 8] for j in range(4))
                link(V.tensor_scalar(e, ap, -1.0, None, ALU.mult))
                V.tensor_tensor(e, e, ap, ALU.min).then_inc(neg_abs, 1)
                dve.wait_ge(exp_abs, L + 1)
                link(V.tensor_scalar(s2_, e, 2.0, None, ALU.add))
                link(V.reciprocal(s2_, s2_))
                link(V.tensor_tensor(s_, e, s2_, ALU.mult))
                link(V.tensor_tensor(s2_, s_, s_, ALU.mult))
                link(V.tensor_scalar(p_, s2_, 1.0 / 17, 1.0 / 15, ALU.mult, ALU.add))
                for k in (13, 11, 9, 7, 5, 3, 1):
                    link(V.tensor_tensor(p_, p_, s2_, ALU.mult))
                    link(V.tensor_scalar(p_, p_, 1.0 / k, None, ALU.add))
                link(V.scalar_tensor_tensor(p_, p_, 2.0, s_, ALU.mult, ALU.mult))
                link(V.tensor_scalar(s_, ap, -1.0, 0.0, ALU.mult, ALU.max))
                link(V.tensor_tensor(p_, p_, s_, ALU.add))
                V.tensor_scalar(c8[:, 0, :], p_, -RG_C, None, ALU.mult)
                V.tensor_scalar(c8[:, 1, :], p_, RG_C, None, ALU.mult).then_inc(layer_prm, 1)

                V.memset(B1[:, :, 0:CONV_W - 1], 0.0)
                cs = prm[:, V_CS * KC:(V_CS + CONV_W - 1) * KC].rearrange("p (j c) -> p c j", c=KC)
                link(V.tensor_copy(B1[:, :, CONV_W - 1 + TP:US + CONV_W - 1], cs))
                for c in range(KC):
                    dve.wait_ge(z_free[c % 2], z_count(L, Z_RNN + c) + 1)
                    w = lambda j: prm[:, (V_CW + j) * KC + c:(V_CW + j) * KC + c + 1]
                    link(V.tensor_scalar(u_[:, c, :], B1[:, c, 0:U], w(0), prm[:, V_CB * KC + c:V_CB * KC + c + 1],
                                         ALU.mult, ALU.add))
                    for j in range(1, CONV_W):
                        last = V.scalar_tensor_tensor(u_[:, c, :], B1[:, c, j:j + U], w(j), u_[:, c, :], ALU.mult, ALU.add)
                        if j < CONV_W - 1:
                            link(last)
                    last.then_inc(u_ready, 1)
                V.tensor_copy(st[:, 2:5, :], B1[:, :, TP:TP + 3].rearrange("p c j -> p j c"))
                V.tensor_copy(st[:, 5:8, :], B1[:, :, XC - 3:XC].rearrange("p c j -> p j c")).then_inc(xc_used, 1)

                rot = tmp[:, :, :].rearrange("p a t -> p (a t)")[:, 0:T]
                for c in range(KC + 1):
                    i = Z_Q + c
                    dst = qT[:, c, :] if c < KC else kT[:, :]
                    bank = z_item(L, i)
                    V.tensor_tensor(dst, bank[:, 0:T], C["cos"], ALU.mult)
                    for x in range(4):
                        a, b = 32 * x, 32 * (x ^ 1)
                        last = V.tensor_tensor(rot[a:a + 32, :], bank[b:b + 32, 0:T], C["sin"][b:b + 32, :], ALU.mult)
                    last.then_inc(z_free[i % 2], 1)
                    dve.wait_ge(z_free[i % 2], z_count(L, i) + 1)
                    V.tensor_tensor(dst, dst, rot, ALU.add).then_inc(q_ready, 1)
                    dve.wait_ge(q_ready, L * (KC + 1) + c + 1)
                dve.wait_ge(out_rows, 2 * L + 1)
                V.tensor_copy(k_rows[:, 0, :], ps[:, 7, 0:P])
                V.tensor_copy(k_rows[0:TS, 1, :], ps[0:TS, 7, P:2 * P]).then_inc(out_kept, 1)

                def soften(w, sinks, n):
                    m, nm, dif = ats[:, w, 0, :], ats[:, w, 1, :], ats[:, w, 3, :]
                    link(V.scalar_tensor_tensor(m, m, SCALE, sinks, ALU.mult, ALU.max))
                    link(V.tensor_scalar(nm, m, -1.0, None, ALU.mult))
                    V.tensor_tensor(dif, sinks, nm, ALU.add).then_inc(s_max, 1)

                def normalise(w, parts, n):
                    dve.wait_ge(s_exp, n)
                    den, rd = ats[:, w, 2, :], ats[:, w, 0, :]
                    link(V.tensor_tensor(den, den, ats[:, w, 4, :], ALU.add))
                    link(V.reciprocal(rd, den))
                    for x, s in enumerate(parts):
                        last = V.tensor_scalar(s, s, rd[:, x:x + 1], None, ALU.mult)
                    last.then_inc(s_norm, 1)

                n = L * (KC + 1) + 1
                dve.wait_ge(s_scores, n)
                for h in range(2):
                    last = V.tensor_reduce(ats[:, 0, 0, 2 * h:2 * h + 2], ps[:, 2 + h, 0:320].rearrange("p (a s) -> p a s", a=2),
                                           AX_X, ALU.max)
                link(last)
                soften(0, sinkS[:, :, :].rearrange("p h a -> p (h a)"), n)
                for b in range(2):
                    dve.wait_ge(z_free[b], z_count(L, Z_LRU + 2 * KC))
                V.tensor_tensor(gxF, gxF, uF, ALU.mult).then_inc(gxu, 1)
                normalise(0, [S[:, 0, h, a * 160:a * 160 + 160] for h in range(2) for a in range(2)], n)
                for c in range(0, KC, 2):
                    dve.wait_ge(a_and_t, L * KC + c + 2)
                    link(V.tensor_tensor(tmp[:, :, :], a_[:, c:c + 2, :], a_[:, c:c + 2, :], ALU.mult))
                    V.scalar_tensor_tensor(gl_[:, c:c + 2, :], tmp[:, :, :], 1.0, gl_[:, c:c + 2, :], ALU.add, ALU.mult)\
                        .then_inc(m2_ready, 1)
                    dve.wait_ge(m2_ready, L * (KC // 2) + c // 2 + 1)
                dve.wait_ge(mult_ready, L + 1)
                link(V.memset(gl_[:, :, 0:1], 1.0))
                V.memset(a_[:, :, 0:1], 0.0)
                V.memset(a_[:, :, US - 1:US], 0.0)
                link(V.tensor_tensor(gxF, gxF, glF, ALU.mult))
                h0 = prm[:, V_H0 * KC:V_H0 * KC + KC].rearrange("p (c o) -> p c o", o=1)
                link(V.tensor_copy(gx_[:, :, US - 1:US], h0))
                V.tensor_tensor_scan(glF, aF, gxF, 0.0, ALU.mult, ALU.add).then_inc(h_scan, 1)
                dve.wait_ge(h_scan, L + 1)
                V.tensor_copy(st[:, 0, :], gl_[:, :, TP - 1])
                V.tensor_copy(st[:, 1, :], gl_[:, :, U - 1]).then_inc(st_ready, 1)

                def mask_and_max(c):
                    w = c % 2
                    dve.wait_ge(s_scores, L * (KC + 1) + c + 2)
                    dve.wait_ge(s_pT, L * (KC + 1) + max(c, 1))
                    for h in range(2):
                        last = V.tensor_tensor(S[:, w, h, :], ps[:, 2 + h, 0:3 * P], C["mask"], ALU.add)
                    last.then_inc(s_masked, 1)
                    dve.wait_ge(s_masked, L * KC + c + 1)
                    V.tensor_reduce(ats[:, w, 0, 0:2], S[:, w, :, 0:TP], AX_X, ALU.max)
                    link(V.tensor_reduce(ats[:, w, 0, 2:4], S[:, w, :, TP:TP + P], AX_X, ALU.max))
                    soften(w, sinkP[:, c, :, :].rearrange("p b h -> p (b h)"), n)

                def keep_output(c):
                    dve.wait_ge(s_o, L * (KC + 1) + c + 2)
                    V.tensor_copy(qT[:, c, 0:TP], ps[:, 6, 0:TP]).then_inc(o_ready, 1)

                mask_and_max(0)
                dve.wait_ge(s_o, L * (KC + 1) + 1)
                V.tensor_copy(qT[:, :, TP:T], ps[:, 6, 0:KC * TS].rearrange("p (c t) -> p c t", c=KC)).then_inc(o_ready, 1)
                for c in range(KC):
                    w = c % 2
                    if c < KC - 1:
                        mask_and_max(c + 1)
                    if c > 1:
                        keep_output(c - 2)
                    normalise(w, [S[:, w, h, lo:hi] for lo, hi in ((0, TP), (TP, TP + P)) for h in range(2)],
                              L * (KC + 1) + c + 2)
                keep_output(KC - 2)
                keep_output(KC - 1)
                dve.wait_ge(out_rows, 2 * L + 2)
                V.tensor_copy(st_rows[0:8 * KC, :], ps[0:8 * KC, 7, 0:P]).then_inc(out_kept, 1)

                dve.wait_ge(z_free[0], z_count(L, Z_OUT))
                dve.wait_ge(z_free[1], z_count(L, Z_OUT))
                for m in range(KC):
                    dve.wait_ge(br_rnn_ready, L * KC + m + 1)
                    V.scalar_tensor_tensor(gr_s[:, m, :], gr_s[:, m, :], 1.0, ps[:, 2 + m % 2, 0:T], ALU.add, ALU.mult)
                    dve.wait_ge(br_ready, L * KC + m + 1)
                    link(V.scalar_tensor_tensor(ga_s[:, m, :], ga_s[:, m, :], 1.0, ps[:, 4 + m % 2, 0:T], ALU.add, ALU.mult))
                    V.tensor_tensor(mT[:, m, :], gr_s[:, m, :], ga_s[:, m, :], ALU.add).then_inc(br_used, 1)
                for m in range(KC):
                    bank = z_item(L, Z_OUT + m)
                    V.scalar_tensor_tensor(yP[:, m, :], xT[:, m, :], 2.0 * alpha, bank[:, 0:T], ALU.mult, ALU.add)\
                        .then_inc(z_free[m % 2], 1)

                stats(L, 0, 4.0 * LN_EPS)
                V.memset(score[:, 2, :], 0.0).then_inc(score_clear, 1)
                for t, (at, n) in enumerate(TOK):
                    dve.wait_ge(xh_ready, L * NT + t + 1)
                    low = xl[:, t, :] if t < NT - 1 else xh[TS:2 * TS, t, :]
                    V.tensor_tensor(low.rearrange("p (k f) -> p f k", k=KC),
                                    tok[0:n, t, :].rearrange("p (f k) -> p f k", k=KC),
                                    xh[0:n, t, :].bitcast(F32).rearrange("p (k f) -> p f k", k=KC), ALU.subtract)\
                        .then_inc(xl_ready, 1)
                norm_back(L, V_G1, V_B1, Z_FILL1)

                dve.wait_ge(kv_stored, (L + 1) * 64)
                b3 = lambda x, k: x.rearrange("p (o k) -> p o k", o=1).to_broadcast((P, NT, k))
                V.tensor_copy(gsp[:, :, 8:12], b3(C["pads"], 4))
                V.tensor_copy(tr[:, :, 4:8], b3(C["pads"], 4))
                dve.wait_ge(score_ready, L + 1)
                link(V.tensor_tensor(rt[:, :, :], score[:, :, :], b3(ebias[:, :], NE), ALU.add), plain=True)
                for t in range(NT):
                    for g in range(NG):
                        last = V.max(m8[:, t, g, :], rt[:, t, g * EPG:(g + 1) * EPG])
                link(last)
                link(V.tensor_tensor(gsp[:, :, 0:NG], m8[:, :, :, 0], m8[:, :, :, 1], ALU.add), plain=True)
                for t in range(NT):
                    last = V.max(g8[:, t, :], gsp[:, t, 0:NG])
                link(last)
                link(V.tensor_copy(tr[:, :, 0:TOPG], g8[:, :, 0:TOPG]), plain=True)
                for t in range(NT):
                    last = V.match_replace(gs2[:, t, :], tr[:, t, :], gsp[:, t, :], MARK)
                link(last)
                link(V.tensor_scalar(gm[:, :, :], gs2[:, :, 0:NG], MARK, None, ALU.is_equal))
                r4 = lambda x: x.rearrange("p t (g e) -> p t g e", g=NG)
                gb = gm[:, :, :].rearrange("p t (g o) -> p t g o", o=1).to_broadcast((P, NT, NG, EPG))
                link(V.tensor_tensor(r4(rt[:, :, :]), r4(rt[:, :, :]), gb, ALU.mult))
                link(V.tensor_scalar(gm[:, :, :], gm[:, :, :], BIG, -BIG, ALU.mult, ALU.add))
                link(V.tensor_tensor(r4(rt[:, :, :]), r4(rt[:, :, :]), gb, ALU.add), plain=True)
                for t in range(NT):
                    last = V.max(t8[:, t, :], rt[:, t, :])
                link(last, plain=True)
                for t in range(NT):
                    last = V.match_replace(rt2[:, t, :], t8[:, t, :], rt[:, t, :], MARK)
                link(last)
                link(V.tensor_scalar(rt2[:, :, :], rt2[:, :, :], MARK, None, ALU.is_equal))
                valid = C["valid"].rearrange("p (t o) -> p t o", o=1)
                V.tensor_tensor(sel[:, :, :], rt2[:, :, :], valid.to_broadcast((P, NT, NE)), ALU.mult).then_inc(sel_ready, 1)
                dve.wait_ge(sel_ready, L + 1)
                link(V.tensor_tensor(gate[:, :, :], score[:, :, :], sel[:, :, :], ALU.mult))
                link(V.tensor_reduce(rs[:, 0:NT], gate[:, :, :], AX_X, ALU.add))
                link(V.tensor_tensor(rs[:, 0:NT], rs[:, 0:NT], C["blank"], ALU.add))
                link(V.reciprocal(rs[:, 0:NT], rs[:, 0:NT]))
                dve.wait_ge(sh_ready, L * 2 + 2)
                for m in range(ME):
                    dve.wait_ge(sh_silu, L * ME + m + 1)
                    V.tensor_tensor(hs[:, m, :], ps[:, 6 + m, 0:T], hs[:, m, :], ALU.mult).then_inc(sh_hid, 1)
                rb = rs[:, 0:NT].rearrange("p (t o) -> p t o", o=1).to_broadcast((P, NT, NE))
                V.scalar_tensor_tensor(gate[:, :, :], gate[:, :, :], ROUTED_SCALE, rb, ALU.mult, ALU.mult).then_inc(gate_ready, 1)
                dve.wait_ge(ranks, L + 1)
                link(V.scalar_tensor_tensor(rank[:, :, :], ps[:, 3, 0:NT * NE].rearrange("p (t e) -> p t e", t=NT), 1.0,
                                            sel[:, :, :], ALU.add, ALU.mult))
                link(V.tensor_scalar(rank[:, :, :], rank[:, :, :], -1.0, None, ALU.add))
                V.tensor_copy(rank[TS:2 * TS, NT - 1, :], rank[0:TS, NT - 1, :])
                link(V.tensor_reduce(rs[:, 4:5], ps[:, 3, NT * NE:(NT + 1) * NE], AX_X, ALU.max))
                link(V.tensor_scalar(rt[:, 0, 0:MAX_ROUNDS - 1], C["thr"], rs[:, 4:5], None, ALU.is_lt))
                link(V.tensor_reduce(rs[:, 5:6], rt[:, 0, 0:MAX_ROUNDS - 1], AX_X, ALU.add))
                link(V.tensor_copy(iota[:, :], C["iota"]))
                V.tensor_scalar(rounds[:, 0:1], rs[:, 5:6], 1.0, None, ALU.add).then_inc(rounds_set, 1)
                dve.wait_ge(rounds_set, L + 1)
                for c in range(KC):
                    bank = z_item(L, Z_SH2 + c)
                    V.scalar_tensor_tensor(ffT[:, c, :], xT[:, c, :], alpha, bank[:, 0:T], ALU.mult, ALU.add)\
                        .then_inc(z_free[c % 2], 1)
                for b in range(2):
                    dve.wait_ge(z_free[b], z_count(L, Z_SH2 + KC))

                def one_hot(n, i):
                    dve.wait_ge(ohT_full, FREE + n * 2)
                    shape = (P, NT, QUAD, CAP)
                    a = iota[:, :].rearrange("p (o e s) -> p o e s", o=1, e=QUAD).to_broadcast(shape)
                    b = rank[:, :, bass.ds(i * QUAD, QUAD)].rearrange("p t (e o) -> p t e o", o=1).to_broadcast(shape)
                    V.tensor_tensor(oh[:, :, :].rearrange("p t (e s) -> p t e s", e=QUAD), a, b, ALU.is_equal)\
                        .then_inc(oh_ready, 1)

                def hidden(n, u):
                    p = n * 2 + u
                    dve.wait_ge(silu_done, p + 1)
                    dve.wait_ge(hid_turned, FREE + p)
                    V.tensor_tensor(hid[:, :], ps[:, 2, DE:2 * DE], sil[:, :], ALU.mult).then_inc(hid_ready, 1)

                def keep_turned(n, u):
                    dve.wait_ge(ohT_full, FREE + n * 2 + (u + 1))
                    V.tensor_copy(gsl[0:CAP, u:u + 1], ps[0:CAP, 7, T:T + 1])
                    V.tensor_copy(gsl[CAP:P, u:u + 1], ps[CAP:P, 7, T + 1:T + 2])
                    V.tensor_copy(ohT[:, u, :], ps[:, 7, 0:T]).then_inc(ohT_ready, 1)

                def low_part(n, u):
                    p = n * 2 + u
                    for b in range(2):
                        dve.wait_ge(yh_ready, p * 2 + (b + 1))
                        x = slice(512 * b, 512 * b + 512)
                        V.scalar_tensor_tensor(yl[:, u, x], ps[:, 3 + b, :], gsl[:, u:u + 1], yh[:, u, x].bitcast(F32),
                                               ALU.mult, ALU.subtract).then_inc(yl_ready, 1)

                def add_output(n):
                    dve.wait_ge(c_added, FREE + n * KC)
                    for c in range(KC):
                        dve.wait_ge(c_full, FREE + n * KC + (c + 1))
                        V.tensor_tensor(ffT[:, c, :], ps[:, 5 + c % 2, 0:T], ffT[:, c, :], ALU.add).then_inc(c_added, 1)

                def quad(n, i, first=False, last=False):
                    hidden(n, 0)
                    if not first:
                        add_output(n - 1)
                    keep_turned(n, 0)
                    keep_turned(n, 1)
                    if not last:
                        one_hot(n + 1, i + 1)
                    low_part(n, 0)
                    hidden(n, 1)
                    low_part(n, 1)

                carry_wait(dve)
                nr = dve.value_load(rounds[0:1, 0:1], min_val=1, max_val=MAX_ROUNDS)
                with dve.Fori(0, nr) as r:
                    q = dve.snap(done)
                    one_hot(q, 0)
                    quad(q, 0, first=True)
                    with dve.Fori(1, NQUAD - 1) as i:
                        quad(q + i, i)
                    quad(q + (NQUAD - 1), NQUAD - 1, last=True)
                    add_output(q + (NQUAD - 1))
                    V.tensor_scalar(iota[:, :], iota[:, :], float(CAP), None, ALU.add).then_inc(next_round, NQUAD)
                    dve.wait_ge(next_round, q + NQUAD)
                    dve.reg_add(done, done, NQUAD)

                stats(L, 1, LN_EPS)
                norm_back(L, V_G2, V_B2, Z_FILL2)
            assert steps[0] == CH, steps[0]

            for t, (at, n) in enumerate(TOK):
                dve.wait_ge(tok_ps, 2 * depth * 2 * NT + 2 * t + 1)
                V.tensor_copy(tok[0:n, t, 0:512], ps[0:n, 2 + 2 * t, :]).then_inc(y_rows, 1)



def _constants():
    import numpy as np

    f = np.float32
    c = np.zeros((P, NCONST), f)
    put = lambda k, x: c.__setitem__((slice(None), slice(C_AT[k], C_AT[k] + CONSTS[k])), x)
    row, col = np.arange(P)[:, None], np.arange(P)[None, :]
    put("ident", row == col)
    put("upper", row < col)
    put("ones", 1.0)
    q, kw = row // CHUNK, np.arange(TP)[None, :] // CHUNK
    wide = np.where((kw <= q + 2) & (kw >= q), 0.0, -BIG)
    narrow = np.where(col // CHUNK <= q, 0.0, -BIG)
    put("mask", np.concatenate([wide, narrow], 1))
    half = HD // 2
    inv = np.power(f(10000.0), -np.arange(half, dtype=f) / f(half)).astype(f)
    pos = np.concatenate([np.arange(TP), PAST + np.arange(TS)]).astype(f)
    ang = (pos[None, :] * inv[np.arange(P) % half][:, None]).astype(f)
    put("cos", np.cos(ang))
    put("sin", np.where(row % HD < half, 1.0, -1.0) * np.sin(ang))
    put("iota", np.arange(QUAD * CAP)[None, :] % CAP)
    put("pads", np.array([[4e30, 3e30, 2e30, 1e30]]))
    put("thr", CAP * np.arange(1, MAX_ROUNDS)[None, :])
    rows = np.stack([np.arange(P) < n for _, n in TOK], 1)
    put("valid", rows)
    put("blank", ~rows)
    return c


def kernel(**inputs):
    import numpy as np
    import concourse.bacc as bacc
    from concourse.bass_utils import run_bass_kernel_spmd as run

    arrays = {k: np.ascontiguousarray(a) for k, a in inputs.items()}
    arrays["consts"] = _constants()
    depth = arrays["w_in"].shape[0]
    nc = bacc.Bacc("TRN2", target_bir_lowering=False, num_devices=1)
    inp = {k: nc.dram_tensor("in_" + k, a.shape, mybir.dt.from_np(a.dtype), kind="ExternalInput").ap() for k, a in arrays.items()}
    kv = lambda t: (depth, 1, t, NKV, HD)
    shapes = {"y_prompt": (1, TP, D), "y_sample": (1, TS, D), "k_prompt": kv(WIN), "v_prompt": kv(WIN), "h_prompt": (depth, 1, D),
              "conv_prompt": (depth, 1, CONV_W - 1, D), "k_sample": kv(TS), "v_sample": kv(TS), "h_sample": (depth, 1, D),
              "conv_sample": (depth, 1, CONV_W - 1, D)}
    out = {k: nc.dram_tensor("out_" + k, s, F32, kind="ExternalOutput").ap() for k, s in shapes.items()}
    build(nc, inp, out, depth, float((2 * depth) ** 0.25))
    r = run(nc, [{"in_" + k: a for k, a in arrays.items()}], core_ids=[0])
    return tuple(r.results[0]["out_" + k] for k in shapes)
```

```python
from contextlib import ExitStack

import concourse.bass as bass
from concourse import mybir

F32 = mybir.dt.float32
F32R = mybir.dt.float32r
I32 = mybir.dt.int32
ALU = mybir.AluOpType
ACT = mybir.ActivationFunctionType
AX_X = mybir.AxisListType.X

P = 128
D = 1024
KC = D // P
TP, TS = 256, 32
T = TP + TS
TOK = [(0, 128), (128, 128), (256, 32)]
NT = len(TOK)
HD = 64
NQ = D // HD
NKV = 2
CONV_W = 4
RG_C = 8.0
NE, TOPK, NG, TOPG = 64, 8, 8, 4
EPG = NE // NG
DE = 256
ME = DE // P
ROUTED_SCALE = 2.5
SCALE = HD ** -0.5
WIN = 128
PAST = 256
CHUNK = 64
LN_EPS = 1e-5
Q_OFF, K_OFF = D, 2 * D
V_OFF = K_OFF + NKV * HD
GR_OFF = V_OFF + NKV * HD
GA_OFF = GR_OFF + D

CAP = 64
QUAD = 4
NQUAD = NE // QUAD
MAX_ROUNDS = -(-T // CAP)

XC = (CONV_W - 1) + TP + (CONV_W - 1) + TS
US = TP + (CONV_W - 1)
U = US + TS

V_CW, V_CB, V_BA, V_BX, V_AP, V_G1, V_B1, V_G2, V_B2, V_H0, V_CS = 0, 4, 5, 6, 7, 8, 9, 10, 11, 12, 13
NV = 16

CONSTS = dict(ident=P, upper=P, ones=P, mask=3 * P, cos=T, sin=T, iota=QUAD * CAP, pads=4, thr=MAX_ROUNDS - 1, valid=NT, blank=NT)
C_AT, _n = {}, 0
for _k, _w in CONSTS.items():
    C_AT[_k] = _n
    _n += _w
NCONST = _n

BIG = 1.0e30
MARK = -3.0e38

Z_RNN, Z_Q, Z_K, Z_V, Z_LRU, Z_GATE, Z_OUT, Z_FILL1, Z_SH2, Z_FILL2, Z_N = 0, 8, 16, 17, 18, 34, 50, 58, 66, 74, 82
Z_HALF = Z_N // 2
Z_FIRST = KC // 2

PIECES = ([("in", 256 * j) for j in range(4)] + [("q", j) for j in range(4)] + [("in", K_OFF)]
          + [("in", GR_OFF + 256 * j) for j in range(8)]
          + [(n, 256 * j) for j in range(4) for n in ("br_rnn", "br_attn")]
          + [("out", 256 * j) for j in range(4)] + [("router", 0), ("s1", 0), ("s3", 0), ("s2", 0)])
ND = len(PIECES)
D_IN, D_Q, D_KV, D_G, D_BR, D_OUT, D_ROUTER = 0, 4, 8, 9, 17, 25, 29
RING = 3
SPLIT = [d for d in range(ND) if d != D_KV and d < D_ROUTER]
DMAS = {"q": 4, "br_attn": 2}
SLOT_INC = [sum(16 * DMAS.get(PIECES[d][0], 1) for d in range(s, ND, RING)) for s in range(RING)]

VECTOR_DMAS, CACHED_DMAS = 11, 6
EXPERTS_AFTER = (D_G, D_G + 2, D_G + 4, D_ROUTER + 2, D_ROUTER + 2, D_ROUTER + 2)
GATES_AHEAD = ((0, 1), (2, 3), (4,))
GATES_WITH = ((5, 6), (7,), (8,), (9, 10), (11,), (12, 13), (14,), (15,))
H_WITH = 2
CH = 133


FREE = 1


def piece_landed(L, d):
    return L * SLOT_INC[d % RING] + sum(16 * DMAS.get(PIECES[x][0], 1) for x in range(d % RING, d + 1, RING))


def z_count(L, i):
    return Z_FIRST + L * Z_HALF + i // 2


def build(nc, inp, out, depth, alpha):
    with ExitStack() as ctx:
        def sb(name, shape, dt=F32, scope=ctx):
            return scope.enter_context(nc.sbuf_tensor(name, shape, dt))

        def sem(name):
            return ctx.enter_context(nc.semaphore(name))

        def low_place(name, shape):
            with ExitStack() as scope:
                return sb(name, shape, F32R, scope)

        ps = ctx.enter_context(nc.psum_tensor("ps", [P, 8, 512], F32))

        cst = sb("cst", [P, NCONST])
        C = {k: cst[:, C_AT[k]:C_AT[k] + w] for k, w in CONSTS.items()}
        ident = C["ident"]
        parts_r = low_place("parts", [P, QUAD * 3 * KC * DE])
        experts = sb("experts", [P, QUAD, 3, KC * DE])
        dense_lo = low_place("dense_lo", [P, RING, KC * 256])
        dense = sb("dense", [P, RING, KC * 256])
        xT = sb("xT", [P, KC, T])
        prm_all = sb("prm_all", [P, depth, NV * KC])
        prm = sb("prm", [P, NV * KC])
        gperm_all = sb("gperm_all", [P, depth, 2, KC])
        gperm = sb("gperm", [P, 2, KC])
        ebias_all = sb("ebias_all", [P, depth, NE])
        ebias = sb("ebias", [P, NE])
        sink_all = sb("sink_all", [P, depth, NQ])
        kcT_all = sb("kcT_all", [P, depth, WIN])
        kcT = sb("kcT", [P, WIN])
        vc_all = sb("vc_all", [P, depth, NKV * HD])
        vc = sb("vc", [P, NKV * HD])
        sinkP = sb("sinkP", [P, KC, 2, 2])
        sinkS = sb("sinkS", [P, 2, 2])
        c8 = sb("c8", [P, 2, KC])
        stats_of = sb("stats_of", [P, NT, 2, 6])
        mv = sb("mv", [P, NT, 2])
        gate = sb("gate", [P, NT, NE])
        rank = sb("rank", [P, NT, NE])
        rounds = sb("rounds", [P, 2], I32)
        small = sb("small", [P, 64])
        st_rows = sb("st_rows", [P, P])
        k_rows = sb("k_rows", [P, 2, P])

        s1 = ExitStack()
        B1 = sb("B1", [P, KC, XC], scope=s1)
        B3 = sb("B3", [P, KC, XC], scope=s1)
        o_lo = low_place("o_lo", [P, KC, T])
        qT = sb("qT", [P, KC, T], scope=s1)
        s1a = ExitStack()
        wax = sb("wax", [P, 2, KC, P], scope=s1a)
        s1a.close()
        S = sb("S", [P, 2, 2, 3 * P], scope=s1)
        PTa = sb("PTa", [P, 2, 2, 3 * P], scope=s1)
        kT = sb("kT", [P, T], scope=s1)
        v = sb("v", [P, NT, NKV * HD], scope=s1)
        tmp = sb("tmp", [P, 2, U], scope=s1)
        st = sb("st", [P, 8, KC], scope=s1)
        ats = sb("ats", [P, 2, 5, 4], scope=s1)
        m_lo = low_place("m_lo", [P, KC, T])
        B4 = sb("B4", [P, KC, XC], scope=s1)
        h_lo = low_place("h_lo", [P, KC, T])
        B2 = sb("B2", [P, KC, XC], scope=s1)
        s1.close()
        B1f, B2f, B3f, B4f = (b[:, :, :].rearrange("p c t -> p (c t)") for b in (B1, B2, B3, B4))
        gr_s = B1f[:, 0:KC * T].rearrange("p (c t) -> p c t", c=KC)
        ga_s = B3f[:, 0:KC * T].rearrange("p (c t) -> p c t", c=KC)
        hT = B2f[:, 0:KC * T].rearrange("p (c t) -> p c t", c=KC)
        mT = B4f[:, 0:KC * T].rearrange("p (c t) -> p c t", c=KC)
        yP = hT
        u_, a_, gx_, gl_ = (f[:, 0:KC * U].rearrange("p (c t) -> p c t", c=KC) for f in (B2f, B2f, B3f, B4f))
        uF, aF, gxF, glF = (f[:, 0:KC * U] for f in (B2f, B2f, B3f, B4f))

        s2 = ExitStack()
        xh = sb("xh", [P, NT, D], F32R, scope=s2)
        xl = sb("xl", [P, NT - 1, D], F32R, scope=s2)
        s2a = ExitStack()
        tok = sb("tok", [P, NT, D], scope=s2a)
        s2a.close()
        xg = sb("xg", [P, KC, QUAD * CAP], scope=s2)
        oh = sb("oh", [P, NT, QUAD * CAP], F32R, scope=s2)
        ohT = sb("ohT", [P, 2, T], F32R, scope=s2)
        sil = sb("sil", [P, DE], scope=s2)
        hid = sb("hid", [P, DE], scope=s2)
        hidT = sb("hidT", [P, ME, 2 * CAP], scope=s2)
        s2b = ExitStack()
        rt = sb("rt", [P, NT, NE], scope=s2b)
        rt2 = sb("rt2", [P, NT, NE], scope=s2b)
        m8 = sb("m8", [P, NT, NG, 8], scope=s2b)
        gsp = sb("gsp", [P, NT, 12], scope=s2b)
        gs2 = sb("gs2", [P, NT, 12], scope=s2b)
        g8 = sb("g8", [P, NT, 8], scope=s2b)
        gm = sb("gm", [P, NT, NG], scope=s2b)
        t8 = sb("t8", [P, NT, 8], scope=s2b)
        sel = sb("sel", [P, NT, NE], scope=s2b)
        score = sb("score", [P, NT, NE], scope=s2b)
        tr = sb("tr", [P, NT, 8], scope=s2b)
        rs = sb("rs", [P, 8], scope=s2b)
        hs = sb("hs", [P, ME, T], scope=s2b)
        s2b.close()
        yh = sb("yh", [P, 2, D], F32R, scope=s2)
        yl = sb("yl", [P, 2, D], F32R, scope=s2)
        iota = sb("iota_w", [P, QUAD * CAP], scope=s2)
        gsl = sb("gsl", [P, 2], scope=s2)
        ffT = sb("ffT", [P, KC, T], scope=s2)
        s2.close()
        raw = B1f[:, 0:2 * depth * P].rearrange("p (k l c) -> p k l c", k=2, l=depth)


        parts = parts_r[:, 6 * KC * DE:12 * KC * DE]
        _w, _t = KC * 256, KC * T
        whi = parts[:, 0:2 * _w].rearrange("p (b x) -> p b x", b=2)
        x_hi, x_lo, h_hi = (parts[:, 2 * _w + j * _t:2 * _w + (j + 1) * _t].rearrange("p (c t) -> p c t", c=KC) for j in range(3))
        o_hi, m_hi = x_hi, x_lo
        as_f = lambda x: x.bitcast(F32)

        ident_in = sem("ident_in")
        consts_in = sem("consts_in")
        vectors_in = sem("vectors_in")
        cached_in = sem("cached_in")
        x_in = sem("x_in")
        rows_ready = sem("rows_ready")
        rows_kept = sem("rows_kept")
        whi_ready = sem("whi_ready")
        wlo_ready = sem("wlo_ready")
        x_hi_even = sem("x_hi_even")
        x_hi_odd = sem("x_hi_odd")
        x_lo_ready = sem("x_lo_ready")
        h_hi_ready = sem("h_hi_ready")
        o_hi_ready = sem("o_hi_ready")
        o_lo_ready = sem("o_lo_ready")
        m_hi_ready = sem("m_hi_ready")
        m_lo_ready = sem("m_lo_ready")
        dense_in = [sem(f"dense_in{s}") for s in range(RING)]
        w13_in = [sem(f"w13_in{e}") for e in range(QUAD)]
        w2_in = [sem(f"w2_in{e}") for e in range(QUAD)]
        wax_zero = sem("wax_zero")
        wax_in = sem("wax_in")
        z_ready = [sem(f"z_ready{b}") for b in range(2)]
        z_free = [sem(f"z_free{b}") for b in range(2)]
        neg_abs = sem("neg_abs")
        exp_abs = sem("exp_abs")
        stat_own = sem("stat_own")
        xc_used = sem("xc_used")
        own = sem("dve_own")
        act_own = sem("act_own")
        layer_prm = sem("layer_prm")
        xc_ready = sem("xc_ready")
        u_ready = sem("u_ready")
        q_ready = sem("q_ready")
        lru_gates = sem("lru_gates")
        gxu = sem("gxu")
        a_and_t = sem("a_and_t")
        m2_ready = sem("m2_ready")
        mult_ready = sem("mult_ready")
        h_scan = sem("h_scan")
        h_ready = sem("h_ready")
        st_ready = sem("st_ready")
        out_rows = sem("out_rows")
        out_kept = sem("out_kept")
        kv_stored = sem("kv_stored")
        states_stored = sem("states_stored")
        y_stored = sem("y_stored")
        s_scores = sem("s_scores")
        s_masked = sem("s_masked")
        s_max = sem("s_max")
        s_exp = sem("s_exp")
        s_norm = sem("s_norm")
        sam_pT = sem("sam_pT")
        s_pT = sem("s_pT")
        s_pT_kept = sem("s_pT_kept")
        s_o = sem("s_o")
        o_ready = sem("o_ready")
        gates_ready = sem("gates_ready")
        br_rnn_ready = sem("br_rnn_ready")
        br_ready = sem("br_ready")
        br_used = sem("br_used")

        tok_ps = sem("tok_ps")
        tok_act = sem("tok_act")
        tok_dve = sem("tok_dve")
        y_rows = sem("y_rows")
        var_ready = sem("var_ready")
        dev_ready = sem("dev_ready")
        norm_set = sem("norm_set")
        xh_ready = sem("xh_ready")
        xl_ready = sem("xl_ready")
        logits = sem("logits")
        score_clear = sem("score_clear")
        score_ready = sem("score_ready")
        sel_ready = sem("sel_ready")
        ranks = sem("ranks")
        rounds_set = sem("rounds_set")
        gate_ready = sem("gate_ready")
        sh_ready = sem("sh_ready")
        sh_silu = sem("sh_silu")
        sh_hid = sem("sh_hid")
        oh_ready = sem("oh_ready")
        xg_full = sem("xg_full")
        xg_kept = sem("xg_kept")
        w13_done = sem("w13_done")
        silu_done = sem("silu_done")
        hid_ready = sem("hid_ready")
        w2_done = sem("w2_done")
        hid_turned = sem("hid_turned")
        hidT_ready = sem("hidT_ready")
        yh_ready = sem("yh_ready")
        yl_ready = sem("yl_ready")
        ohT_full = sem("ohT_full")
        ohT_ready = sem("ohT_ready")
        c_full = sem("c_full")
        c_added = sem("c_added")
        next_round = sem("next_round")

        wait_carried = {e.engine: sem(f"wait_carried{i}") for i, e in enumerate((nc.sync, nc.gpsimd, nc.tensor, nc.scalar, nc.vector))}

        block = ctx.enter_context(nc.Block())

        def wait_piece_used(eng, L, d):
            kind, at = PIECES[d]
            if d < D_Q:
                i = Z_RNN + 2 * d + 1
            elif d < D_KV:
                i = Z_Q + 2 * (d - D_Q) + 1
            elif d == D_KV:
                i = Z_V
            elif d < D_BR:
                i = Z_GATE + 2 * (d - D_G) + 1
            elif d < D_OUT:
                eng.wait_ge(br_rnn_ready if kind == "br_rnn" else br_ready, L * KC + 2 * ((d - D_BR) // 2) + 2)
                return
            elif d < D_ROUTER:
                i = Z_OUT + 2 * (d - D_OUT) + 1
            elif kind == "router":
                eng.wait_ge(logits, L + 1)
                return
            else:
                eng.wait_ge(sh_ready, L * 2 + (1 if kind == "s1" else 2))
                return
            eng.wait_ge(z_ready[i % 2], z_count(L, i) + 1)

        def carry_wait(eng):
            eng.sem_inc(wait_carried[eng.engine], 1)

        @block.sync
        def _(sp):
            sp.dma_start(cst[:, 0:P], inp["consts"][:, 0:P]).then_inc(ident_in, 16)
            xp = inp["x_prompt"].rearrange("b (t p) d -> p (b t) d", p=P)
            sp.dma_start(tok[:, 0:2, :], xp).then_inc(x_in, 16)
            sp.dma_start(tok[0:TS, 2, :], inp["x_sample"].rearrange("b t d -> (b t) d")).then_inc(x_in, 16)
            sp.dma_start(cst[:, P:NCONST], inp["consts"][:, P:NCONST]).then_inc(consts_in, 16)

            def load_piece(L, d):
                kind, at = PIECES[d]
                slot = dense[:, d % RING, :]
                full = slot.rearrange("p (k c) -> p k c", k=KC)
                s = dense_in[d % RING]
                rows = lambda w: w[bass.ds(L, 1)].rearrange("l (k p) c -> p (l k) c", p=P)
                if d >= RING:
                    wait_piece_used(sp, L, d - RING)
                else:
                    sp.wait_ge(z_ready[1], Z_FIRST + L * Z_HALF - (Z_N - Z_SH2 - KC) // 2)
                if kind == "q":
                    for c in range(2):
                        for g in range(2):
                            x = Q_OFF + (g * KC + 2 * at + c) * HD
                            sp.dma_start(full[:, :, c * P + g * HD:c * P + g * HD + HD], rows(inp["w_in"])[:, :, x:x + HD])\
                                .then_inc(s, 16)
                elif kind == "br_attn":
                    w = inp["w_br_attn"][bass.ds(L, 1)].rearrange("l (g k p) c -> g p (l k) c", g=2, p=HD)
                    for g in range(2):
                        sp.dma_start(full[g * HD:g * HD + HD, :, :], w[g, :, :, at:at + 256]).then_inc(s, 16)
                elif kind == "router":
                    dst = slot[:, 0:KC * NE].rearrange("p (k c) -> p k c", k=KC)
                    sp.dma_start(dst, rows(inp["w_router"])).then_inc(s, 16)
                elif kind == "s2":
                    dst = slot.rearrange("p (m c) -> p m c", m=ME)
                    sp.dma_start(dst, rows(inp["ws2"])).then_inc(s, 16)
                else:
                    w = {"in": "w_in", "br_rnn": "w_br_rnn", "out": "w_out", "s1": "ws1", "s3": "ws3"}[kind]
                    sp.dma_start(full, rows(inp[w])[:, :, at:at + 256]).then_inc(s, 16)

            def load_w13(L, i, es):
                for e in es:
                    at = L * NE + i * QUAD + e
                    for j, w in enumerate(("w1", "w3")):
                        src = inp[w].rearrange("l e (p k) c -> (l e) p (k c)", k=KC)[bass.ds(at, 1)]
                        sp.dma_start(experts[:, e, j, :], src.rearrange("o p x -> p (o x)")).then_inc(w13_in[e], 16)

            def load_w2(L, i, u):
                for e in (2 * u, 2 * u + 1):
                    at = L * NE + i * QUAD + e
                    src = inp["w2"].rearrange("l e (m p) c -> (l e) p m c", p=P)[bass.ds(at, 1)]
                    dst = experts[:, e, 2, :].rearrange("p (m c) -> p m c", m=ME)
                    sp.dma_start(dst, src.rearrange("o p m c -> p (o m) c")).then_inc(w2_in[e], 16)

            done = sp.alloc_register("quads_done")
            sp.reg_mov(done, 0)
            with sp.Fori(0, depth) as L:
                for d in range(RING):
                    load_piece(L, d)
                q0 = sp.snap(done)
                for d in range(RING, ND):
                    load_piece(L, d)
                    if d == EXPERTS_AFTER[0]:
                        sp.wait_ge(w2_done, FREE + q0 * 4)
                    for x, after in enumerate(EXPERTS_AFTER):
                        if d == after:
                            u, part = divmod(x, 3)
                            load_w2(L, 0, u) if part == 2 else load_w13(L, 0, (2 * u + part,))
                sp.wait_ge(rounds_set, L + 1)
                carry_wait(sp)
                nr = sp.value_load(rounds[0:1, 0:1], min_val=1, max_val=MAX_ROUNDS)
                with sp.Fori(1, nr * NQUAD) as t:
                    for u in range(2):
                        sp.wait_ge(w13_done, FREE + (q0 + t) * 2 + (u - 1))
                        load_w13(L, t % NQUAD, (2 * u, 2 * u + 1))
                        sp.wait_ge(w2_done, FREE + (q0 + t) * 4 + (2 * u - 2))
                        load_w2(L, t % NQUAD, u)
                sp.reg_add(done, done, nr * NQUAD)

        @block.gpsimd
        def _(pool):
            pool.dma_start(raw[:, 1, :, :], inp["cache_k"].rearrange("l b t g d -> (b t) l (g d)")).then_inc(cached_in, 16)
            pool.dma_start(vc_all[:, :, :], inp["cache_v"].rearrange("l b t g d -> (b t) l (g d)")).then_inc(cached_in, 16)
            for j, name in enumerate(("ln1_g", "ln1_b")):
                pool.dma_start(gperm_all[:, :, j, :], inp[name].rearrange("l (p k) -> p l k", k=KC)).then_inc(cached_in, 16)
            wide = lambda w: w.rearrange("(o l) n -> o l n", o=1).to_broadcast((P, depth, w.shape[1]))
            pool.dma_start(ebias_all[:, :, :], wide(inp["e_bias"])).then_inc(cached_in, 16)
            pool.dma_start(sink_all[:, :, :], wide(inp["sinks"])).then_inc(cached_in, 16)
            with pool.Fori(0, depth) as L:
                def low_parts(f0, f1):
                    for f in range(f0, f1):
                        slot, low = dense[:, SPLIT[f] % RING, :], dense_lo[:, SPLIT[f] % RING, :]
                        for h in range(2):
                            x = slice(h * KC * P, (h + 1) * KC * P)
                            pool.wait_ge(whi_ready, (L * len(SPLIT) + f) * 2 + (h + 1))
                            nc.gpsimd.tensor_tensor(low[:, x], slot[:, x], as_f(whi[:, f % 2, x]), ALU.subtract)\
                                .then_inc(wlo_ready, 1)

                low_parts(0, 1)
                for b in range(2):
                    pool.wait_ge(z_free[b], Z_FIRST + L * Z_HALF)
                carry_wait(pool)
                nc.gpsimd.memset(wax[:, :, :, :], 0.0).then_inc(wax_zero, 1)
                pool.wait_ge(wax_zero, L + 1)
                carry_wait(pool)
                for j, w in enumerate(("w_x", "w_a")):
                    src = inp[w][bass.ds(L, 1)].rearrange("l (c g) i o -> g i (l c) o", g=2)
                    for g in range(2):
                        pool.dma_start(wax[g * HD:g * HD + HD, j, :, g * HD:g * HD + HD], src[g]).then_inc(wax_in, 16)
                low_parts(1, 9)
                pool.wait_ge(z_free[Z_V % 2], z_count(L, Z_V) + 1)
                carry_wait(pool)
                rows = lambda o: o[bass.ds(L, 1)].rearrange("l b t g d -> (l b t) (g d)")
                pool.dma_start(rows(out["v_prompt"]), v[:, 1, :]).then_inc(kv_stored, 16)
                pool.dma_start(rows(out["v_sample"]), v[0:TS, 2, :]).then_inc(kv_stored, 16)
                low_parts(9, 12)
                pool.wait_ge(out_kept, 2 * L + 1)
                carry_wait(pool)
                pool.dma_start(rows(out["k_prompt"]), k_rows[:, 0, :]).then_inc(kv_stored, 16)
                pool.dma_start(rows(out["k_sample"]), k_rows[0:TS, 1, :]).then_inc(kv_stored, 16)
                low_parts(12, len(SPLIT))
                pool.wait_ge(out_kept, 2 * L + 2)
                carry_wait(pool)
                hrow = lambda o: o[bass.ds(L, 1)].rearrange("l b (c p) -> (l b c) p", p=P)
                crow = lambda o: o[bass.ds(L, 1)].rearrange("l b j (c p) -> (l b j c) p", p=P)
                pool.dma_start(hrow(out["h_prompt"]), st_rows[0:KC, :]).then_inc(states_stored, 16)
                pool.dma_start(hrow(out["h_sample"]), st_rows[KC:2 * KC, :]).then_inc(states_stored, 16)
                pool.dma_start(crow(out["conv_prompt"]), st_rows[2 * KC:5 * KC, :]).then_inc(states_stored, 16)
                pool.dma_start(crow(out["conv_sample"]), st_rows[5 * KC:8 * KC, :]).then_inc(states_stored, 16)
                pool.wait_ge(kv_stored, (L + 1) * 64)
                pool.wait_ge(states_stored, (L + 1) * 64)
            pool.wait_ge(y_rows, 2 * NT)
            yp = out["y_prompt"].rearrange("b (t p) d -> p (b t) d", p=P)
            pool.dma_start(yp, tok[:, 0:2, :]).then_inc(y_stored, 16)
            pool.dma_start(out["y_sample"].rearrange("b t d -> (b t) d"), tok[0:TS, 2, :]).then_inc(y_stored, 16)
            pool.wait_ge(y_stored, 32)

        @block.tensor
        def _(pe):
            mm, transpose = nc.tensor.matmul, nc.tensor.transpose

            def bank_of(L, i):
                pe.wait_ge(z_free[i % 2], z_count(L, i))
                return ps[:, i % 2, :]

            def over_features(bank, d, col, rhs, n):
                w = dense[:, d % RING, :].rearrange("p (k c) -> p k c", k=KC)
                for k in range(KC):
                    last = mm(bank[:, 0:n], w[:, k, col:col + P], rhs(k), start=k == 0, stop=k == KC - 1)
                return last

            def over_parts(L, bank, d, col, hi, lo, ready=None):
                f = SPLIT.index(d)
                w_hi = whi[:, f % 2, :].rearrange("p (k c) -> p k c", k=KC)
                w_lo = dense_lo[:, d % RING, :].rearrange("p (k c) -> p k c", k=KC)
                for k in range(KC):
                    if col == 0 and k % 4 == 0:
                        pe.wait_ge(wlo_ready, (L * len(SPLIT) + f) * 2 + (k // 4 + 1))
                    if ready:
                        ready(k)
                    mm(bank[:, 0:T], w_hi[:, k, col:col + P], hi[:, k, :], start=k == 0, stop=False)
                    mm(bank[:, 0:T], w_hi[:, k, col:col + P], lo[:, k, :], start=False, stop=False)
                    last = mm(bank[:, 0:T], w_lo[:, k, col:col + P], hi[:, k, :], start=False, stop=k == KC - 1)
                return last

            def piece(L, d):
                pe.wait_ge(dense_in[d % RING], piece_landed(L, d))

            def fill_xT(wait):
                for c in range(KC):
                    wait(c)
                    for t, (at, n) in enumerate(TOK):
                        last = transpose(ps[:, c % 2, at:at + n], tok[0:n, t, c * P:c * P + P], ident[0:n, 0:n])
                    last.then_inc(z_ready[c % 2], 1)

            def to_tokens(src):
                for t, (at, n) in enumerate(TOK):
                    for h in range(2):
                        for c in range(4):
                            last = transpose(ps[0:n, 2 + 2 * t + h, c * P:c * P + P], src[:, 4 * h + c, at:at + n], ident)
                        last.then_inc(tok_ps, 1)

            for s in (w13_done, w2_done, c_full, ohT_full, hid_turned):
                pe.sem_inc(s, FREE)
            pe.wait_ge(ident_in, 16)
            pe.wait_ge(x_in, 32)
            fill_xT(lambda c: pe.wait_ge(z_free[c % 2], c // 2) if c >= 2 else None)
            pe.wait_ge(vectors_in, VECTOR_DMAS * 16)
            pe.wait_ge(cached_in, CACHED_DMAS * 16)
            for l in range(depth):
                transpose(ps[:, 2, l * P:l * P + P], raw[:, 0, l, :], ident)
                last = transpose(ps[:, 3, l * P:l * P + P], raw[:, 1, l, :], ident)
            last.then_inc(rows_ready, 1)
            pe.wait_ge(consts_in, 16)

            done = pe.alloc_register("quads_done")
            rounds_reg = pe.alloc_register("rounds")
            pe.reg_mov(done, 0)
            with pe.Fori(0, depth) as L:
                xk = lambda k: xT[:, k, :]
                for b in range(2):
                    pe.wait_ge(z_free[b], Z_FIRST + L * Z_HALF)

                for m in range(KC):
                    ready = (lambda k: pe.wait_ge(x_lo_ready, L * KC + k + 1)) if m == 0 else None
                    over_parts(L, bank_of(L, Z_RNN + m), D_IN + m // 2, m % 2 * P, x_hi, x_lo, ready).then_inc(z_ready[m % 2], 1)
                for c in range(KC):
                    over_parts(L, bank_of(L, Z_Q + c), D_Q + c // 2, c % 2 * P, x_hi, x_lo).then_inc(z_ready[c % 2], 1)
                piece(L, D_KV)
                over_features(bank_of(L, Z_K), D_KV, 0, xk, T).then_inc(z_ready[Z_K % 2], 1)
                bank = bank_of(L, Z_V)
                w = dense[:, D_KV % RING, :].rearrange("p (k c) -> p k c", k=KC)
                for t, (at, n) in enumerate(TOK):
                    for k in range(KC):
                        last = mm(bank[0:n, t * P:t * P + P], xT[:, k, at:at + n], w[:, k, P:2 * P], start=k == 0, stop=k == KC - 1)
                last.then_inc(z_ready[Z_V % 2], 1)
                pe.wait_ge(wax_in, (L + 1) * 64)
                for c in range(KC):
                    pe.wait_ge(u_ready, L * KC + c + 1)
                    for j in range(2):
                        bank = bank_of(L, Z_LRU + 2 * c + j)
                        mm(bank[:, 0:U], wax[:, j, c, :], u_[:, c, :], start=True, stop=True).then_inc(z_ready[j], 1)
                def gate_chunks(ms):
                    for m in ms:
                        over_parts(L, bank_of(L, Z_GATE + m), D_G + m // 2, m % 2 * P, x_hi, x_lo).then_inc(z_ready[m % 2], 1)

                def pair_scores(c):
                    if c == 0:
                        pe.wait_ge(s_exp, L * (KC + 1) + 1)
                    else:
                        pe.wait_ge(s_masked, L * KC + c)
                    for h in range(2):
                        lo, hi = h * HD, h * HD + HD
                        mm(ps[:, 2 + h, 0:TP], qT[lo:hi, c, P:TP], kT[lo:hi, 0:TP], start=True, stop=True)
                        last = mm(ps[:, 2 + h, TP:TP + P], qT[lo:hi, c, 0:P], kT[lo:hi, 0:P], start=True, stop=True)
                    last.then_inc(s_scores, 1)

                pe.wait_ge(q_ready, L * (KC + 1) + KC + 1)
                transpose(ps[:, 7, 0:P], kT[:, TP - WIN:TP], ident)
                transpose(ps[0:TS, 7, P:2 * P], kT[:, TP:T], ident).then_inc(out_rows, 1)

                for h in range(2):
                    lo, hi = h * HD, h * HD + HD
                    for a in range(2):
                        for i in range(4):
                            q = qT[lo:hi, 4 * a + i, TP:T]
                            o = ps[32 * i:32 * i + 32, 2 + h, a * 160:a * 160 + 160]
                            mm(o[:, 0:WIN], q, kcT[lo:hi, :], start=True, stop=True)
                            last = mm(o[:, WIN:WIN + TS], q, kT[lo:hi, TP:T], start=True, stop=True)
                last.then_inc(s_scores, 1)
                gate_chunks(GATES_AHEAD[0])
                pe.wait_ge(s_norm, L * (KC + 1) + 1)
                for h in range(2):
                    for a in range(2):
                        p = S[:, 0, h, a * 160:a * 160 + 160]
                        transpose(ps[:, 4 + h, a * P:a * P + P], p[:, 0:WIN], ident)
                        last = transpose(ps[0:TS, 4 + h, (2 + a) * P:(3 + a) * P], p[:, WIN:WIN + TS], ident)
                last.then_inc(s_pT, 1)
                pair_scores(0)
                gate_chunks(GATES_AHEAD[1])
                pe.wait_ge(z_free[Z_V % 2], z_count(L, Z_V) + 1)
                pe.wait_ge(s_pT_kept, L * (KC + 1) + 1)
                for h in range(2):
                    lo, hi = h * HD, h * HD + HD
                    pt = PTa[:, 0, :, :].rearrange("p h x -> p (h x)")[:, h * 256:h * 256 + 256]
                    ptn = PTa[:, 1, :, :].rearrange("p h x -> p (h x)")[:, h * 256:h * 256 + 256]
                    for a in range(2):
                        o = ps[lo:hi, 6, a * P:a * P + P]
                        mm(o, vc[:, lo:hi], pt[:, a * P:a * P + P], start=True, stop=False)
                        last = mm(o, v[0:TS, 2, lo:hi], ptn[0:TS, a * P:a * P + P], start=False, stop=True)
                last.then_inc(s_o, 1)

                gate_chunks(GATES_AHEAD[2])

                def pair_output(c):
                    n = L * (KC + 1) + c + 1
                    pe.wait_ge(s_pT_kept, n + 1)
                    pe.wait_ge(o_ready, n)
                    for h in range(2):
                        lo, hi = h * HD, h * HD + HD
                        pt = PTa[:, c % 2, h, :]
                        mm(ps[lo:hi, 6, P:2 * P], v[:, 0, lo:hi], pt[:, 0:P], start=True, stop=False)
                        mm(ps[lo:hi, 6, P:2 * P], v[:, 1, lo:hi], pt[:, P:2 * P], start=False, stop=True)
                        last = mm(ps[lo:hi, 6, 0:P], v[:, 0, lo:hi], pt[:, 2 * P:3 * P], start=True, stop=True)
                    last.then_inc(s_o, 1)

                for c in range(KC):
                    n = L * (KC + 1) + c + 1
                    if c == 0:
                        gate_chunks(GATES_WITH[c])
                    if c < KC - 1:
                        pair_scores(c + 1)
                    if c > 0:
                        gate_chunks(GATES_WITH[c][:1])
                        pair_output(c - 1)
                        gate_chunks(GATES_WITH[c][1:])
                    pe.wait_ge(s_norm, n + 1)
                    pe.wait_ge(s_pT_kept, n)
                    for h in range(2):
                        for k in range(3):
                            last = transpose(ps[:, 4 + h, k * P:k * P + P], S[:, c % 2, h, k * P:k * P + P], ident)
                    last.then_inc(s_pT, 1)
                pair_output(KC - 1)

                pe.wait_ge(st_ready, L + 1)
                pe.wait_ge(out_kept, 2 * L + 1)
                carry_wait(pe)
                transpose(ps[0:8 * KC, 7, 0:P], st[:, :, :].rearrange("p v c -> p (v c)"), ident).then_inc(out_rows, 1)

                pe.wait_ge(h_ready, L + 1)
                for j in range(KC // 2):
                    for i, (hi, lo, sig) in enumerate(((h_hi, h_lo, br_rnn_ready), (o_hi, o_lo, br_ready))):
                        if j == 0 and i == 1:
                            pe.wait_ge(o_lo_ready, L + 1)
                        for m in (2 * j, 2 * j + 1):
                            if m >= 2 and i == 0:
                                pe.wait_ge(br_used, L * KC + m - 1)
                            over_parts(L, ps[:, 2 + 2 * i + m % 2, :], D_BR + 2 * j + i, m % 2 * P, hi, lo).then_inc(sig, 1)
                for m in range(KC):
                    ready = (lambda k: pe.wait_ge(m_lo_ready, L * KC + k + 1)) if m == 0 else None
                    over_parts(L, bank_of(L, Z_OUT + m), D_OUT + m // 2, m % 2 * P, m_hi, m_lo, ready).then_inc(z_ready[m % 2], 1)
                for b in range(2):
                    pe.wait_ge(z_free[b], z_count(L, Z_OUT + KC))
                pe.wait_ge(out_kept, 2 * L + 2)
                to_tokens(yP)
                pe.wait_ge(tok_act, (2 * L + 1) * NT)
                pe.wait_ge(tok_dve, 2 * L + 1)
                fill_xT(lambda c: bank_of(L, Z_FILL1 + c))

                piece(L, D_ROUTER)
                for b in range(2):
                    pe.wait_ge(z_free[b], z_count(L, Z_FILL1 + KC))
                w = dense[:, D_ROUTER % RING, 0:KC * NE].rearrange("p (k c) -> p k c", k=KC)
                for t, (at, n) in enumerate(TOK):
                    for k in range(KC):
                        last = mm(ps[0:n, 2, t * NE:t * NE + NE], xT[:, k, at:at + n], w[:, k, :], start=k == 0, stop=k == KC - 1)
                last.then_inc(logits, 1)
                def shared_up(j):
                    piece(L, D_ROUTER + 1 + j)
                    for m in range(ME):
                        last = over_features(ps[:, 4 + 2 * j + m, :], D_ROUTER + 1 + j, m * P, xk, T)
                    last.then_inc(sh_ready, 1)

                shared_up(0)
                pe.wait_ge(sel_ready, L + 1)
                for t in range(NT):
                    o = ps[:, 3, t * NE:t * NE + NE]
                    for x in range(t):
                        mm(o, C["ones"], sel[:, x, :], start=x == 0, stop=False)
                    mm(o, C["upper"], sel[:, t, :], start=t == 0, stop=True)
                for t in range(NT):
                    last = mm(ps[:, 3, NT * NE:(NT + 1) * NE], C["ones"], sel[:, t, :], start=t == 0, stop=t == NT - 1)
                last.then_inc(ranks, 1)
                shared_up(1)

                def shared_down():
                    d = D_ROUTER + 3
                    piece(L, d)
                    pe.wait_ge(sh_hid, (L + 1) * 2)
                    w = dense[:, d % RING, :].rearrange("p (m c) -> p m c", m=ME)
                    for c in range(KC):
                        bank = bank_of(L, Z_SH2 + c)
                        for m in range(ME):
                            last = mm(bank[:, 0:T], w[:, m, c * P:c * P + P], hs[:, m, :], start=m == 0, stop=m == ME - 1)
                        last.then_inc(z_ready[c % 2], 1)
                    for b in range(2):
                        pe.wait_ge(z_free[b], z_count(L, Z_SH2 + KC))

                def gather(n, js=range(4)):
                    pe.wait_ge(oh_ready, n + 1)
                    for j in js:
                        if j >= 2:
                            pe.wait_ge(xg_kept, n * 4 + (j - 1))
                        for k in (2 * j, 2 * j + 1):
                            o = ps[:, j % 2, k % 2 * 256:k % 2 * 256 + 256]
                            x = slice(k * P, k * P + P)
                            if k == 0:
                                pe.wait_ge(xh_ready, (L + 1) * NT)
                                pe.wait_ge(xl_ready, (L + 1) * NT)
                            for t in range(NT - 1):
                                mm(o, xh[:, t, x], oh[:, t, :], start=t == 0, stop=False)
                                mm(o, xl[:, t, x], oh[:, t, :], start=False, stop=False)
                            last = mm(o, xh[0:2 * TS, NT - 1, x], oh[0:2 * TS, NT - 1, :], start=False, stop=True)
                        last.then_inc(xg_full, 1)

                def up(n, u):
                    pe.wait_ge(xg_kept, n * 4 + 4)
                    pe.wait_ge(hidT_ready, FREE + n * 2 + u)
                    for e in (2 * u, 2 * u + 1):
                        pe.wait_ge(w13_in[e], (n + 1) * 32)
                    for k in range(KC):
                        for e in (2 * u, 2 * u + 1):
                            last = mm(ps[e % 2 * CAP:(e % 2 + 1) * CAP, 2, :], xg[:, k, e * CAP:e * CAP + CAP],
                                      experts[:, e, 0:2, k * DE:k * DE + DE], start=k == 0, stop=k == KC - 1)
                    last.then_inc(w13_done, 1)

                def turn(n, u):
                    pe.wait_ge(hid_ready, FREE + n * 2 + u + 1)
                    for m in range(ME):
                        last = transpose(ps[:, 2, m * P:m * P + P], hid[:, m * P:m * P + P], ident)
                    last.then_inc(hid_turned, 1)

                def down(n, u):
                    pe.wait_ge(hidT_ready, FREE + n * 2 + u + 1)
                    pe.wait_ge(yl_ready, FREE + (n * 2 + u) * 2)
                    for e in (2 * u, 2 * u + 1):
                        pe.wait_ge(w2_in[e], (n + 1) * 16)
                    for b in range(2):
                        for m in range(ME):
                            for e in (2 * u, 2 * u + 1):
                                last = mm(ps[e % 2 * CAP:(e % 2 + 1) * CAP, 3 + b, :], hidT[:, m, e % 2 * CAP:(e % 2 + 1) * CAP],
                                          experts[:, e, 2, m * D + b * 512:m * D + b * 512 + 512], start=m == 0, stop=m == ME - 1)
                        last.then_inc(w2_done, 1)

                def slots_to_tokens(n, i, u):
                    pe.wait_ge(ohT_ready, FREE + n * 2 + u)
                    o = oh[:, :, u * P:u * P + P].bitcast(F32)
                    for t, (at, r) in enumerate(TOK):
                        transpose(ps[:, 7, at:at + r], o[0:r, t, :], ident[0:r, 0:r])
                    for t in range(NT):
                        g = gate[:, t, bass.ds(i * QUAD + 2 * u, 2)]
                        last = mm(ps[:, 7, T:T + 2], o[:, t, :], g, start=t == 0, stop=t == NT - 1)
                    last.then_inc(ohT_full, 1)

                def combine(n):
                    pe.wait_ge(ohT_ready, FREE + n * 2 + 2)
                    pe.wait_ge(yl_ready, FREE + n * 4 + 4)
                    for c in range(KC):
                        pe.wait_ge(c_added, FREE + n * KC + max(c - 1, 0))
                        o = ps[:, 5 + c % 2, 0:T]
                        for u in range(2):
                            mm(o, yh[:, u, c * P:c * P + P], ohT[:, u, :], start=u == 0, stop=False)
                            last = mm(o, yl[:, u, c * P:c * P + P], ohT[:, u, :], start=False, stop=u == 1)
                        last.then_inc(c_full, 1)

                def quad(n, i, first=False, last=False):
                    if not first:
                        up(n, 0)
                        combine(n - 1)
                    slots_to_tokens(n, i, 0)
                    turn(n, 0)
                    slots_to_tokens(n, i, 1)
                    down(n, 0)
                    up(n, 1)
                    if not last:
                        gather(n + 1, range(2))
                    turn(n, 1)
                    if not last:
                        gather(n + 1, range(2, 4))
                    down(n, 1)

                def round_of(q, meanwhile=None):
                    gather(q)
                    up(q, 0)
                    if meanwhile:
                        meanwhile()
                    quad(q, 0, first=True)
                    with pe.Fori(1, NQUAD - 1) as i:
                        quad(q + i, i)
                    quad(q + (NQUAD - 1), NQUAD - 1, last=True)
                    combine(q + (NQUAD - 1))
                    pe.reg_add(done, done, NQUAD)

                round_of(pe.snap(done), meanwhile=shared_down)
                pe.wait_ge(rounds_set, L + 1)
                carry_wait(pe)
                nr = pe.value_load(rounds[0:1, 0:1], min_val=1, max_val=MAX_ROUNDS)
                pe.reg_mov(rounds_reg, nr)
                with pe.If_ne(rounds_reg, 1), pe.Fori(1, nr):
                    round_of(pe.snap(done))

                pe.wait_ge(c_added, FREE + pe.snap(done) * KC)
                to_tokens(ffT)
                pe.wait_ge(tok_act, (2 * L + 2) * NT)
                pe.wait_ge(tok_dve, 2 * L + 2)
                fill_xT(lambda c: bank_of(L, Z_FILL2 + c))

            for b in range(2):
                pe.wait_ge(z_free[b], Z_FIRST + depth * Z_HALF)
            to_tokens(xT)

        @block.scalar
        def _(act):
            activation = nc.scalar.activation

            act.sem_inc(hidT_ready, FREE)
            def rows_of(w, at, n):
                act.dma_start(raw[at * KC:(at + n) * KC, 0, :, :], w).then_inc(vectors_in, 16)
            rows_of(inp["conv_w"].rearrange("l j (c p) -> (j c) l p", p=P), V_CW, CONV_W)
            for at, name in ((V_CB, "conv_b"), (V_BA, "b_a"), (V_BX, "b_x"), (V_AP, "a_param"), (V_G1, "ln1_g"),
                             (V_B1, "ln1_b"), (V_G2, "ln2_g"), (V_B2, "ln2_b")):
                rows_of(inp[name].rearrange("l (c p) -> c l p", p=P), at, 1)
            rows_of(inp["state_h"].rearrange("l b (c p) -> (b c) l p", p=P), V_H0, 1)
            rows_of(inp["state_conv"].rearrange("l b j (c p) -> (b j c) l p", p=P), V_CS, CONV_W - 1)

            def z_item(L, i):
                act.wait_ge(z_ready[i % 2], z_count(L, i) + 1)
                return ps[:, i % 2, :]

            for c in range(0, KC, 2):
                act.wait_ge(z_ready[0], c // 2 + 1)
                activation(x_hi[:, c, :], ps[:, 0, 0:T], ACT.Copy).then_inc(x_hi_even, 1)
                activation(xT[:, c, :], ps[:, 0, 0:T], ACT.Copy).then_inc(z_free[0], 1)

            def high_parts(L, f0, f1=None):
                for f in range(f0, f1 or f0 + 1):
                    d = SPLIT[f]
                    act.wait_ge(dense_in[d % RING], piece_landed(L, d))
                    if f >= 2:
                        wait_piece_used(act, L, SPLIT[f - 2])
                    for h in range(2):
                        x = slice(h * KC * P, (h + 1) * KC * P)
                        activation(whi[:, f % 2, x], dense[:, d % RING, x], ACT.Copy).then_inc(whi_ready, 1)

            def norm_rows(L, k):
                def root(t):
                    n = TOK[t][1]
                    act.wait_ge(var_ready, (2 * L + k) * NT + (t + 1))
                    activation(mv[0:n, t, 1:2], mv[0:n, t, 1:2], ACT.Sqrt).then_inc(dev_ready, 1)

                root(0)
                for t, (at, n) in enumerate(TOK):
                    if t < NT - 1:
                        root(t + 1)
                    act.wait_ge(norm_set, (2 * L + k) * NT + (t + 1))
                    for h in range(2) if t < NT - 1 else (1,):
                        last = activation(tok[0:n, t, 512 * h:512 * h + 512], ps[0:n, 2 + 2 * t + h, :], ACT.Identity,
                                          bias=mv[0:n, t, 0:1], scale=mv[0:n, t, 1:2])
                    last.then_inc(tok_act, 1)

            def norm_back(L, g, b, first, split=False):
                for c in range(0, KC, 2):
                    bank = z_item(L, first + c)
                    if split:
                        activation(x_hi[:, c, :], bank[:, 0:T], ACT.Identity, bias=prm[:, b * KC + c:b * KC + c + 1],
                                   scale=prm[:, g * KC + c:g * KC + c + 1]).then_inc(x_hi_even, 1)
                    activation(xT[:, c, :], bank[:, 0:T], ACT.Identity, bias=prm[:, b * KC + c:b * KC + c + 1],
                               scale=prm[:, g * KC + c:g * KC + c + 1]).then_inc(z_free[0], 1)

            done = act.alloc_register("quads_done")
            rounds_reg = act.alloc_register("rounds")
            layer_reg = act.alloc_register("layer")
            act.reg_mov(done, 0)
            high_parts(0, 0, 2)
            with act.Fori(0, depth) as L:
                act.wait_ge(neg_abs, L + 1)
                activation(small[:, 0:KC], small[:, 0:KC], ACT.Exp).then_inc(exp_abs, 1)
                act.wait_ge(rows_kept, 2)
                for m in range(KC):
                    bank = z_item(L, Z_RNN + m)
                    activation(B1[:, m, CONV_W - 1:CONV_W - 1 + TP], bank[:, 0:TP], ACT.Copy)
                    activation(B1[:, m, XC - TS:XC], bank[:, TP:T], ACT.Copy).then_inc(z_free[m % 2], 1)
                    if m % 2 == 1:
                        high_parts(L, m // 2 + 2)
                high_parts(L, 6, 9)
                bank = z_item(L, Z_V)
                activation(v[:, 0:2, :], bank[:, 0:2 * P].rearrange("p (t c) -> p t c", t=2), ACT.Copy)
                activation(v[0:TS, 2, :], bank[0:TS, 2 * P:3 * P], ACT.Copy).then_inc(z_free[Z_V % 2], 1)
                act.wait_ge(layer_prm, L + 1)
                for c in range(KC):
                    for j, (dst, b) in enumerate(((gx_, V_BX), (gl_, V_BA))):
                        bank = z_item(L, Z_LRU + 2 * c + j)
                        activation(dst[:, c, :], bank[:, 0:U], ACT.Sigmoid, bias=prm[:, b * KC + c:b * KC + c + 1])\
                            .then_inc(z_free[j], 1)
                high_parts(L, 9)
                def keep_gates(ms, high=True):
                    for m in ms:
                        bank = z_item(L, Z_GATE + m)
                        dst = gr_s[:, m, :] if m < KC else ga_s[:, m - KC, :]
                        activation(dst, bank[:, 0:T], ACT.Tanh, scale=0.5).then_inc(z_free[m % 2], 1)
                        if high and m % 2 == 1:
                            high_parts(L, SPLIT.index(D_G) + m // 2 + 2)

                act.wait_ge(s_max, L * (KC + 1) + 1)
                for h in range(2):
                    for a in range(2):
                        x = 2 * h + a
                        activation(S[:, 0, h, a * 160:a * 160 + 160], ps[:, 2 + h, a * 160:a * 160 + 160], ACT.Exp,
                                   bias=ats[:, 0, 1, x:x + 1], scale=SCALE, accum_out=ats[:, 0, 2, x:x + 1])
                activation(ats[:, 0, 4, :], ats[:, 0, 3, :], ACT.Exp).then_inc(s_exp, 1)
                act.wait_ge(gxu, L + 1)
                act.wait_ge(z_free[1], z_count(L, Z_LRU + 2 * KC))
                for c in range(KC):
                    activation(a_[:, c, :], gl_[:, c, :], ACT.Exp, scale=c8[:, 0, c:c + 1]).then_inc(act_own, 1)
                act.wait_ge(xc_used, L + 1)
                keep_gates(GATES_AHEAD[0])
                act.wait_ge(act_own, (L + 1) * KC)
                for c in range(KC):
                    activation(gl_[:, c, :], gl_[:, c, :], ACT.Tanh, scale=c8[:, 1, c:c + 1]).then_inc(a_and_t, 1)

                act.wait_ge(s_pT, L * (KC + 1) + 1)
                ptc = PTa[:, 0, :, :].rearrange("p h x -> p (h x)")
                ptn = PTa[0:TS, 1, :, :].rearrange("p h x -> p (h x)")
                for h in range(2):
                    activation(ptc[:, h * 256:h * 256 + 256], ps[:, 4 + h, 0:256], ACT.Copy)
                    last = activation(ptn[:, h * 256:h * 256 + 256], ps[0:TS, 4 + h, 256:512], ACT.Copy)
                last.then_inc(s_pT_kept, 1)
                keep_gates(GATES_AHEAD[1], high=False)
                act.wait_ge(m2_ready, (L + 1) * (KC // 2))
                activation(glF, glF, ACT.Sqrt).then_inc(mult_ready, 1)
                high_parts(L, SPLIT.index(D_G) + 3)
                keep_gates(GATES_AHEAD[2])

                def exponentials(c):
                    w = c % 2
                    act.wait_ge(s_max, L * (KC + 1) + c + 2)
                    for b, (lo, hi) in enumerate(((0, TP), (TP, TP + P))):
                        for h in range(2):
                            x = 2 * b + h
                            activation(S[:, w, h, lo:hi], S[:, w, h, lo:hi], ACT.Exp, bias=ats[:, w, 1, x:x + 1],
                                       scale=SCALE, accum_out=ats[:, w, 2, x:x + 1])
                    activation(ats[:, w, 4, :], ats[:, w, 3, :], ACT.Exp).then_inc(s_exp, 1)

                exponentials(0)
                for c in range(KC):
                    n = L * (KC + 1) + c + 1
                    w = c % 2
                    if c == H_WITH:
                        act.wait_ge(h_scan, L + 1)
                        activation(h_hi[:, :, 0:TP], gl_[:, :, 0:TP], ACT.Copy)
                        activation(h_hi[:, :, TP:T], gl_[:, :, US:U], ACT.Copy).then_inc(h_hi_ready, 1)
                    if c == 0:
                        keep_gates(GATES_WITH[c])
                    if c < KC - 1:
                        exponentials(c + 1)
                    if c > 0:
                        keep_gates(GATES_WITH[c])
                    act.wait_ge(s_pT, n + 1)
                    act.wait_ge(s_o, L * (KC + 1) + max(c, 1))
                    activation(PTa[:, w, 0, :], ps[:, 4, 0:3 * P], ACT.Copy)
                    activation(PTa[:, w, 1, :], ps[:, 5, 0:3 * P], ACT.Copy).then_inc(s_pT_kept, 1)

                act.wait_ge(o_ready, (L + 1) * (KC + 1))
                activation(o_hi[:, :, :], qT[:, :, :], ACT.Copy).then_inc(o_hi_ready, 1)
                f = SPLIT.index(D_BR)
                for j in range(KC // 2):
                    high_parts(L, f + 2 * j + 2, f + 2 * j + 4)
                    for m in (2 * j, 2 * j + 1):
                        act.wait_ge(br_used, L * KC + m + 1)
                        activation(m_hi[:, m, :], mT[:, m, :], ACT.Copy).then_inc(m_hi_ready, 1)
                high_parts(L, len(SPLIT) - 2, len(SPLIT))

                norm_rows(L, 0)
                norm_back(L, V_G1, V_B1, Z_FILL1)
                for t, (at, n) in enumerate(TOK):
                    act.wait_ge(tok_act, (2 * L) * NT + (t + 1))
                    if t == NT - 1:
                        act.wait_ge(tok_dve, 2 * L + 1)
                    activation(xh[0:n, t, :].rearrange("p (k f) -> p f k", k=KC),
                               tok[0:n, t, :].rearrange("p (f k) -> p f k", k=KC), ACT.Copy).then_inc(xh_ready, 1)
                act.wait_ge(logits, L + 1)
                act.wait_ge(score_clear, L + 1)
                activation(score[:, 0:2, :], ps[:, 2, 0:2 * NE].rearrange("p (t e) -> p t e", t=2), ACT.Sigmoid)
                activation(score[0:TS, 2, :], ps[0:TS, 2, 2 * NE:3 * NE], ACT.Sigmoid).then_inc(score_ready, 1)
                act.wait_ge(kv_stored, (L + 1) * 64)
                act.wait_ge(sh_ready, L * 2 + 1)
                for m in range(ME):
                    activation(hs[:, m, :], ps[:, 4 + m, 0:T], ACT.Silu).then_inc(sh_silu, 1)

                def keep_gathered(n, js=range(4)):
                    act.wait_ge(w13_done, FREE + n * 2)
                    for j in js:
                        act.wait_ge(xg_full, n * 4 + (j + 1))
                        for k in (2 * j, 2 * j + 1):
                            last = activation(xg[:, k, :], ps[:, j % 2, k % 2 * 256:k % 2 * 256 + 256], ACT.Identity,
                                              bias=gperm[:, 1, k:k + 1], scale=gperm[:, 0, k:k + 1])
                        last.then_inc(xg_kept, 1)

                def silu(n, u):
                    p = n * 2 + u
                    act.wait_ge(w13_done, FREE + p + 1)
                    act.wait_ge(hid_ready, FREE + p)
                    activation(sil[:, :], ps[:, 2, 0:DE], ACT.Silu).then_inc(silu_done, 1)

                def keep_hidden(n, u):
                    p = n * 2 + u
                    act.wait_ge(w2_done, FREE + p * 2)
                    act.wait_ge(hid_turned, FREE + p + 1)
                    activation(hidT[:, :, :].rearrange("p m s -> p (m s)"), ps[:, 2, 0:ME * P], ACT.Copy).then_inc(hidT_ready, 1)

                def high_part(n, u):
                    p = n * 2 + u
                    act.wait_ge(ohT_ready, FREE + p + 1)
                    act.wait_ge(c_full, FREE + n * KC)
                    for b in range(2):
                        act.wait_ge(w2_done, FREE + p * 2 + (b + 1))
                        activation(yh[:, u, 512 * b:512 * b + 512], ps[:, 3 + b, :], ACT.Identity, scale=gsl[:, u:u + 1])\
                            .then_inc(yh_ready, 1)

                def quad(n, last=False):
                    silu(n, 0)
                    keep_hidden(n, 0)
                    high_part(n, 0)
                    silu(n, 1)
                    if not last:
                        keep_gathered(n + 1, range(2))
                    keep_hidden(n, 1)
                    if not last:
                        keep_gathered(n + 1, range(2, 4))
                    high_part(n, 1)

                def round_of(q):
                    keep_gathered(q)
                    with act.Fori(0, NQUAD - 1) as i:
                        quad(q + i)
                    quad(q + (NQUAD - 1), last=True)
                    act.reg_add(done, done, NQUAD)

                round_of(act.snap(done))
                act.wait_ge(rounds_set, L + 1)
                carry_wait(act)
                nr = act.value_load(rounds[0:1, 0:1], min_val=1, max_val=MAX_ROUNDS)
                act.reg_mov(rounds_reg, nr)
                with act.If_ne(rounds_reg, 1), act.Fori(1, nr):
                    round_of(act.snap(done))

                act.wait_ge(w2_done, FREE + act.snap(done) * 4)
                act.reg_mov(layer_reg, L)
                with act.If_ne(layer_reg, depth - 1):
                    high_parts(L + 1, 0, 2)
                norm_rows(L, 1)
                norm_back(L, V_G2, V_B2, Z_FILL2, split=True)

            for t, (at, n) in enumerate(TOK):
                act.wait_ge(tok_ps, (2 * depth + 0) * 2 * NT + 2 * t + 2)
                activation(tok[0:n, t, 512:D], ps[0:n, 3 + 2 * t, :], ACT.Copy).then_inc(y_rows, 1)

        @block.vector
        def _(dve):
            V = nc.vector
            steps = [0]
            before = [0]

            def link(ins, plain=False):
                steps[0] += 1
                ins.then_inc(own, 1)
                dve.wait_ge(own, before[0] + steps[0])
                if plain:
                    carry_wait(dve)

            def z_item(L, i):
                dve.wait_ge(z_ready[i % 2], z_count(L, i) + 1)
                return ps[:, i % 2, :]

            for s in (hid_ready, yl_ready, ohT_ready, c_added):
                dve.sem_inc(s, FREE)
            def low_x(n, c):
                for c in (c - 1, c):
                    dve.wait_ge(x_hi_odd if c % 2 else x_hi_even, n * (KC // 2) + (c // 2 + 1))
                    dve.wait_ge(z_free[c % 2], Z_FIRST - KC // 2 + n * Z_HALF + (c // 2 + 1))
                    V.tensor_tensor(x_lo[:, c, :], xT[:, c, :], as_f(x_hi[:, c, :]), ALU.subtract).then_inc(x_lo_ready, 1)

            for c in range(1, KC, 2):
                dve.wait_ge(z_ready[1], c // 2 + 1)
                V.tensor_copy(x_hi[:, c, :], ps[:, 1, 0:T]).then_inc(x_hi_odd, 1)
                V.tensor_copy(xT[:, c, :], ps[:, 1, 0:T]).then_inc(z_free[1], 1)
                low_x(0, c)


            dve.wait_ge(rows_ready, 1)
            V.tensor_copy(prm_all[:, :, :], ps[:, 2, 0:depth * P].rearrange("p (l c) -> p l c", l=depth)).then_inc(rows_kept, 1)
            V.tensor_copy(kcT_all[:, :, :], ps[:, 3, 0:depth * P].rearrange("p (l c) -> p l c", l=depth)).then_inc(rows_kept, 1)
            dve.wait_ge(rows_kept, 2)
            dve.wait_ge(consts_in, 16)

            def stats(L, k, eps):
                count = [(2 * L + k) * 4 * NT]

                def stat(ins, plain=False):
                    count[0] += 1
                    ins.then_inc(stat_own, 1)
                    dve.wait_ge(stat_own, count[0])
                    if plain:
                        carry_wait(dve)

                def moments(t, n):
                    for h in range(2):
                        dve.wait_ge(tok_ps, (2 * L + k) * 2 * NT + (2 * t + h + 1))
                        stat(V.bn_stats(stats_of[0:n, t, h, :], ps[0:n, 2 + 2 * t + h, :]), plain=h == 1)
                    stat(V.bn_aggr(mv[0:n, t, :], stats_of[0:n, t, :, :]))
                    V.tensor_scalar(mv[0:n, t, 1:2], mv[0:n, t, 1:2], eps, None, ALU.add).then_inc(var_ready, 1)

                def deviation(t, n):
                    dve.wait_ge(dev_ready, (2 * L + k) * NT + (t + 1))
                    stat(V.reciprocal(mv[0:n, t, 1:2], mv[0:n, t, 1:2]))
                    V.scalar_tensor_tensor(mv[0:n, t, 0:1], mv[0:n, t, 0:1], -1.0, mv[0:n, t, 1:2], ALU.mult, ALU.mult)\
                        .then_inc(norm_set, 1)

                for t, (at, n) in enumerate(TOK):
                    moments(t, n)
                    if t > 0:
                        deviation(t - 1, TOK[t - 1][1])
                t, n = NT - 1, TOK[-1][1]
                deviation(t, n)
                dve.wait_ge(norm_set, (2 * L + k + 1) * NT)
                V.tensor_scalar(tok[0:n, t, 0:512], ps[0:n, 2 + 2 * t, :], mv[0:n, t, 1:2], mv[0:n, t, 0:1],
                                ALU.mult, ALU.add).then_inc(tok_dve, 1)

            def norm_back(L, g, b, first, split=False):
                for c in range(1, KC, 2):
                    bank = z_item(L, first + c)
                    if split:
                        V.tensor_scalar(x_hi[:, c, :], bank[:, 0:T], prm[:, g * KC + c:g * KC + c + 1],
                                        prm[:, b * KC + c:b * KC + c + 1], ALU.mult, ALU.add).then_inc(x_hi_odd, 1)
                    V.tensor_scalar(xT[:, c, :], bank[:, 0:T], prm[:, g * KC + c:g * KC + c + 1],
                                    prm[:, b * KC + c:b * KC + c + 1], ALU.mult, ALU.add).then_inc(z_free[1], 1)
                    if split:
                        low_x(L + 1, c)

            done = dve.alloc_register("quads_done")
            rounds_reg = dve.alloc_register("rounds")
            dve.reg_mov(done, 0)
            with dve.Fori(0, depth) as L:
                before[0] = L * CH
                for b in range(2):
                    dve.wait_ge(z_free[b], Z_FIRST + L * Z_HALF)
                dve.wait_ge(cached_in, CACHED_DMAS * 16)
                V.tensor_copy(prm[:, :], prm_all[:, bass.ds(L, 1), :].rearrange("p o c -> p (o c)"))
                V.tensor_copy(gperm[:, :, :], gperm_all[:, bass.ds(L, 1), :, :].rearrange("p o j k -> p (o j) k"))
                V.tensor_copy(ebias[:, :], ebias_all[:, bass.ds(L, 1), :].rearrange("p o c -> p (o c)"))
                V.tensor_copy(kcT[:, :], kcT_all[:, bass.ds(L, 1), :].rearrange("p o c -> p (o c)"))
                V.tensor_copy(vc[:, :], vc_all[:, bass.ds(L, 1), :].rearrange("p o c -> p (o c)"))
                sk = sink_all[:, bass.ds(L, 1), :].rearrange("p o (h c) -> p (o c) h", h=2)
                V.tensor_copy(sinkP[:, :, 0, :], sk)
                link(V.tensor_copy(sinkP[:, :, 1, :], sk))
                for i in range(4):
                    x = slice(32 * i, 32 * i + 32)
                    last = V.tensor_copy(sinkS[x, :, :], sinkP[x, i:KC:4, 0, :].rearrange("p a h -> p h a"))
                link(last)
                ap = prm[:, V_AP * KC:V_AP * KC + KC]
                e, s_, s2_, p_ = (small[:, 8 * j:8 * j + 8] for j in range(4))
                link(V.tensor_scalar(e, ap, -1.0, None, ALU.mult))
                V.tensor_tensor(e, e, ap, ALU.min).then_inc(neg_abs, 1)
                dve.wait_ge(exp_abs, L + 1)
                link(V.tensor_scalar(s2_, e, 2.0, None, ALU.add))
                link(V.reciprocal(s2_, s2_))
                link(V.tensor_tensor(s_, e, s2_, ALU.mult))
                link(V.tensor_tensor(s2_, s_, s_, ALU.mult))
                link(V.tensor_scalar(p_, s2_, 1.0 / 17, 1.0 / 15, ALU.mult, ALU.add))
                for k in (13, 11, 9, 7, 5, 3, 1):
                    link(V.tensor_tensor(p_, p_, s2_, ALU.mult))
                    link(V.tensor_scalar(p_, p_, 1.0 / k, None, ALU.add))
                link(V.scalar_tensor_tensor(p_, p_, 2.0, s_, ALU.mult, ALU.mult))
                link(V.tensor_scalar(s_, ap, -1.0, 0.0, ALU.mult, ALU.max))
                link(V.tensor_tensor(p_, p_, s_, ALU.add))
                V.tensor_scalar(c8[:, 0, :], p_, -RG_C, None, ALU.mult)
                V.tensor_scalar(c8[:, 1, :], p_, RG_C, None, ALU.mult).then_inc(layer_prm, 1)

                V.memset(B1[:, :, 0:CONV_W - 1], 0.0)
                cs = prm[:, V_CS * KC:(V_CS + CONV_W - 1) * KC].rearrange("p (j c) -> p c j", c=KC)
                link(V.tensor_copy(B1[:, :, CONV_W - 1 + TP:US + CONV_W - 1], cs))
                for c in range(KC):
                    dve.wait_ge(z_free[c % 2], z_count(L, Z_RNN + c) + 1)
                    w = lambda j: prm[:, (V_CW + j) * KC + c:(V_CW + j) * KC + c + 1]
                    link(V.tensor_scalar(u_[:, c, :], B1[:, c, 0:U], w(0), prm[:, V_CB * KC + c:V_CB * KC + c + 1],
                                         ALU.mult, ALU.add))
                    for j in range(1, CONV_W):
                        last = V.scalar_tensor_tensor(u_[:, c, :], B1[:, c, j:j + U], w(j), u_[:, c, :], ALU.mult, ALU.add)
                        if j < CONV_W - 1:
                            link(last)
                    last.then_inc(u_ready, 1)
                V.tensor_copy(st[:, 2:5, :], B1[:, :, TP:TP + 3].rearrange("p c j -> p j c"))
                V.tensor_copy(st[:, 5:8, :], B1[:, :, XC - 3:XC].rearrange("p c j -> p j c")).then_inc(xc_used, 1)

                rot = tmp[:, :, :].rearrange("p a t -> p (a t)")[:, 0:T]
                for c in range(KC + 1):
                    i = Z_Q + c
                    dst = qT[:, c, :] if c < KC else kT[:, :]
                    bank = z_item(L, i)
                    V.tensor_tensor(dst, bank[:, 0:T], C["cos"], ALU.mult)
                    for x in range(4):
                        a, b = 32 * x, 32 * (x ^ 1)
                        last = V.tensor_tensor(rot[a:a + 32, :], bank[b:b + 32, 0:T], C["sin"][b:b + 32, :], ALU.mult)
                    last.then_inc(z_free[i % 2], 1)
                    dve.wait_ge(z_free[i % 2], z_count(L, i) + 1)
                    V.tensor_tensor(dst, dst, rot, ALU.add).then_inc(q_ready, 1)
                    dve.wait_ge(q_ready, L * (KC + 1) + c + 1)
                dve.wait_ge(out_rows, 2 * L + 1)
                V.tensor_copy(k_rows[:, 0, :], ps[:, 7, 0:P])
                V.tensor_copy(k_rows[0:TS, 1, :], ps[0:TS, 7, P:2 * P]).then_inc(out_kept, 1)

                def soften(w, sinks, n):
                    m, nm, dif = ats[:, w, 0, :], ats[:, w, 1, :], ats[:, w, 3, :]
                    link(V.scalar_tensor_tensor(m, m, SCALE, sinks, ALU.mult, ALU.max))
                    link(V.tensor_scalar(nm, m, -1.0, None, ALU.mult))
                    V.tensor_tensor(dif, sinks, nm, ALU.add).then_inc(s_max, 1)

                def normalise(w, parts, n):
                    dve.wait_ge(s_exp, n)
                    den, rd = ats[:, w, 2, :], ats[:, w, 0, :]
                    link(V.tensor_tensor(den, den, ats[:, w, 4, :], ALU.add))
                    link(V.reciprocal(rd, den))
                    for x, s in enumerate(parts):
                        last = V.tensor_scalar(s, s, rd[:, x:x + 1], None, ALU.mult)
                    last.then_inc(s_norm, 1)

                n = L * (KC + 1) + 1
                dve.wait_ge(s_scores, n)
                for h in range(2):
                    last = V.tensor_reduce(ats[:, 0, 0, 2 * h:2 * h + 2], ps[:, 2 + h, 0:320].rearrange("p (a s) -> p a s", a=2),
                                           AX_X, ALU.max)
                link(last)
                soften(0, sinkS[:, :, :].rearrange("p h a -> p (h a)"), n)
                for b in range(2):
                    dve.wait_ge(z_free[b], z_count(L, Z_LRU + 2 * KC))
                V.tensor_tensor(gxF, gxF, uF, ALU.mult).then_inc(gxu, 1)
                normalise(0, [S[:, 0, h, a * 160:a * 160 + 160] for h in range(2) for a in range(2)], n)
                for c in range(0, KC, 2):
                    dve.wait_ge(a_and_t, L * KC + c + 2)
                    link(V.tensor_tensor(tmp[:, :, :], a_[:, c:c + 2, :], a_[:, c:c + 2, :], ALU.mult))
                    V.scalar_tensor_tensor(gl_[:, c:c + 2, :], tmp[:, :, :], 1.0, gl_[:, c:c + 2, :], ALU.add, ALU.mult)\
                        .then_inc(m2_ready, 1)
                    dve.wait_ge(m2_ready, L * (KC // 2) + c // 2 + 1)
                def mask_and_max(c):
                    w = c % 2
                    dve.wait_ge(s_scores, L * (KC + 1) + c + 2)
                    dve.wait_ge(s_pT, L * (KC + 1) + max(c, 1))
                    for h in range(2):
                        last = V.tensor_tensor(S[:, w, h, :], ps[:, 2 + h, 0:3 * P], C["mask"], ALU.add)
                    last.then_inc(s_masked, 1)
                    dve.wait_ge(s_masked, L * KC + c + 1)
                    V.tensor_reduce(ats[:, w, 0, 0:2], S[:, w, :, 0:TP], AX_X, ALU.max)
                    link(V.tensor_reduce(ats[:, w, 0, 2:4], S[:, w, :, TP:TP + P], AX_X, ALU.max))
                    soften(w, sinkP[:, c, :, :].rearrange("p b h -> p (b h)"), n)

                mask_and_max(0)
                dve.wait_ge(mult_ready, L + 1)
                link(V.memset(gl_[:, :, 0:1], 1.0))
                V.memset(a_[:, :, 0:1], 0.0)
                V.memset(a_[:, :, US - 1:US], 0.0)
                link(V.tensor_tensor(gxF, gxF, glF, ALU.mult))
                h0 = prm[:, V_H0 * KC:V_H0 * KC + KC].rearrange("p (c o) -> p c o", o=1)
                link(V.tensor_copy(gx_[:, :, US - 1:US], h0))
                V.tensor_tensor_scan(glF, aF, gxF, 0.0, ALU.mult, ALU.add).then_inc(h_scan, 1)
                dve.wait_ge(h_scan, L + 1)
                V.tensor_copy(st[:, 0, :], gl_[:, :, TP - 1])
                V.tensor_copy(st[:, 1, :], gl_[:, :, U - 1]).then_inc(st_ready, 1)

                def keep_output(c):
                    dve.wait_ge(s_o, L * (KC + 1) + c + 2)
                    V.tensor_copy(qT[:, c, 0:TP], ps[:, 6, 0:TP]).then_inc(o_ready, 1)

                dve.wait_ge(s_o, L * (KC + 1) + 1)
                V.tensor_copy(qT[:, :, TP:T], ps[:, 6, 0:KC * TS].rearrange("p (c t) -> p c t", c=KC)).then_inc(o_ready, 1)
                for c in range(KC):
                    w = c % 2
                    if 0 < c < KC - 1:
                        mask_and_max(c + 1)
                    if c == H_WITH + 1:
                        dve.wait_ge(h_hi_ready, L + 1)
                        V.tensor_tensor(h_lo[:, :, 0:TP], gl_[:, :, 0:TP], as_f(h_hi[:, :, 0:TP]), ALU.subtract)
                        V.tensor_tensor(h_lo[:, :, TP:T], gl_[:, :, US:U], as_f(h_hi[:, :, TP:T]), ALU.subtract).then_inc(h_ready, 1)
                    normalise(w, [S[:, w, h, lo:hi] for lo, hi in ((0, TP), (TP, TP + P)) for h in range(2)],
                              L * (KC + 1) + c + 2)
                    if c == 0:
                        mask_and_max(1)
                    if c > 0:
                        keep_output(c - 1)
                keep_output(KC - 1)
                dve.wait_ge(o_hi_ready, L + 1)
                V.tensor_tensor(o_lo[:, :, :], qT[:, :, :], as_f(o_hi[:, :, :]), ALU.subtract).then_inc(o_lo_ready, 1)
                dve.wait_ge(out_rows, 2 * L + 2)
                V.tensor_copy(st_rows[0:8 * KC, :], ps[0:8 * KC, 7, 0:P]).then_inc(out_kept, 1)

                dve.wait_ge(z_free[0], z_count(L, Z_OUT))
                dve.wait_ge(z_free[1], z_count(L, Z_OUT))
                def low_merged(m):
                    dve.wait_ge(m_hi_ready, L * KC + m + 1)
                    V.tensor_tensor(m_lo[:, m, :], mT[:, m, :], as_f(m_hi[:, m, :]), ALU.subtract).then_inc(m_lo_ready, 1)

                for m in range(KC):
                    dve.wait_ge(br_rnn_ready, L * KC + m + 1)
                    V.scalar_tensor_tensor(gr_s[:, m, :], gr_s[:, m, :], 1.0, ps[:, 2 + m % 2, 0:T], ALU.add, ALU.mult)
                    dve.wait_ge(br_ready, L * KC + m + 1)
                    link(V.scalar_tensor_tensor(ga_s[:, m, :], ga_s[:, m, :], 1.0, ps[:, 4 + m % 2, 0:T], ALU.add, ALU.mult))
                    V.tensor_tensor(mT[:, m, :], gr_s[:, m, :], ga_s[:, m, :], ALU.add).then_inc(br_used, 1)
                    if m > 0:
                        low_merged(m - 1)
                low_merged(KC - 1)
                for m in range(KC):
                    bank = z_item(L, Z_OUT + m)
                    V.scalar_tensor_tensor(yP[:, m, :], xT[:, m, :], 2.0 * alpha, bank[:, 0:T], ALU.mult, ALU.add)\
                        .then_inc(z_free[m % 2], 1)

                stats(L, 0, 4.0 * LN_EPS)
                V.memset(score[:, 2, :], 0.0).then_inc(score_clear, 1)
                norm_back(L, V_G1, V_B1, Z_FILL1)

                for t, (at, n) in enumerate(TOK):
                    dve.wait_ge(xh_ready, L * NT + t + 1)
                    low = xl[:, t, :] if t < NT - 1 else xh[TS:2 * TS, t, :]
                    V.tensor_tensor(low.rearrange("p (k f) -> p f k", k=KC),
                                    tok[0:n, t, :].rearrange("p (f k) -> p f k", k=KC),
                                    xh[0:n, t, :].bitcast(F32).rearrange("p (k f) -> p f k", k=KC), ALU.subtract)\
                        .then_inc(xl_ready, 1)

                dve.wait_ge(kv_stored, (L + 1) * 64)
                b3 = lambda x, k: x.rearrange("p (o k) -> p o k", o=1).to_broadcast((P, NT, k))
                V.tensor_copy(gsp[:, :, 8:12], b3(C["pads"], 4))
                V.tensor_copy(tr[:, :, 4:8], b3(C["pads"], 4))
                dve.wait_ge(score_ready, L + 1)
                link(V.tensor_tensor(rt[:, :, :], score[:, :, :], b3(ebias[:, :], NE), ALU.add), plain=True)
                for t in range(NT):
                    for g in range(NG):
                        last = V.max(m8[:, t, g, :], rt[:, t, g * EPG:(g + 1) * EPG])
                link(last)
                link(V.tensor_tensor(gsp[:, :, 0:NG], m8[:, :, :, 0], m8[:, :, :, 1], ALU.add), plain=True)
                for t in range(NT):
                    last = V.max(g8[:, t, :], gsp[:, t, 0:NG])
                link(last)
                link(V.tensor_copy(tr[:, :, 0:TOPG], g8[:, :, 0:TOPG]), plain=True)
                for t in range(NT):
                    last = V.match_replace(gs2[:, t, :], tr[:, t, :], gsp[:, t, :], MARK)
                link(last)
                link(V.tensor_scalar(gm[:, :, :], gs2[:, :, 0:NG], MARK, None, ALU.is_equal))
                r4 = lambda x: x.rearrange("p t (g e) -> p t g e", g=NG)
                gb = gm[:, :, :].rearrange("p t (g o) -> p t g o", o=1).to_broadcast((P, NT, NG, EPG))
                link(V.tensor_tensor(r4(rt[:, :, :]), r4(rt[:, :, :]), gb, ALU.mult))
                link(V.tensor_scalar(gm[:, :, :], gm[:, :, :], BIG, -BIG, ALU.mult, ALU.add))
                link(V.tensor_tensor(r4(rt[:, :, :]), r4(rt[:, :, :]), gb, ALU.add), plain=True)
                for t in range(NT):
                    last = V.max(t8[:, t, :], rt[:, t, :])
                link(last, plain=True)
                for t in range(NT):
                    last = V.match_replace(rt2[:, t, :], t8[:, t, :], rt[:, t, :], MARK)
                link(last)
                link(V.tensor_scalar(rt2[:, :, :], rt2[:, :, :], MARK, None, ALU.is_equal))
                valid = C["valid"].rearrange("p (t o) -> p t o", o=1)
                V.tensor_tensor(sel[:, :, :], rt2[:, :, :], valid.to_broadcast((P, NT, NE)), ALU.mult).then_inc(sel_ready, 1)
                dve.wait_ge(sel_ready, L + 1)
                link(V.tensor_tensor(gate[:, :, :], score[:, :, :], sel[:, :, :], ALU.mult))
                link(V.tensor_reduce(rs[:, 0:NT], gate[:, :, :], AX_X, ALU.add))
                link(V.tensor_tensor(rs[:, 0:NT], rs[:, 0:NT], C["blank"], ALU.add))
                link(V.reciprocal(rs[:, 0:NT], rs[:, 0:NT]))
                rb = rs[:, 0:NT].rearrange("p (t o) -> p t o", o=1).to_broadcast((P, NT, NE))
                V.scalar_tensor_tensor(gate[:, :, :], gate[:, :, :], ROUTED_SCALE, rb, ALU.mult, ALU.mult).then_inc(gate_ready, 1)
                dve.wait_ge(ranks, L + 1)
                link(V.scalar_tensor_tensor(rank[:, :, :], ps[:, 3, 0:NT * NE].rearrange("p (t e) -> p t e", t=NT), 1.0,
                                            sel[:, :, :], ALU.add, ALU.mult))
                link(V.tensor_scalar(rank[:, :, :], rank[:, :, :], -1.0, None, ALU.add))
                V.tensor_copy(rank[TS:2 * TS, NT - 1, :], rank[0:TS, NT - 1, :])
                link(V.tensor_copy(iota[:, :], C["iota"]))

                def one_hot(n, i):
                    dve.wait_ge(ohT_full, FREE + n * 2)
                    shape = (P, NT, QUAD, CAP)
                    a = iota[:, :].rearrange("p (o e s) -> p o e s", o=1, e=QUAD).to_broadcast(shape)
                    b = rank[:, :, bass.ds(i * QUAD, QUAD)].rearrange("p t (e o) -> p t e o", o=1).to_broadcast(shape)
                    V.tensor_tensor(oh[:, :, :].rearrange("p t (e s) -> p t e s", e=QUAD), a, b, ALU.is_equal)\
                        .then_inc(oh_ready, 1)

                def hidden(n, u):
                    p = n * 2 + u
                    dve.wait_ge(silu_done, p + 1)
                    dve.wait_ge(hid_turned, FREE + p)
                    V.tensor_tensor(hid[:, :], ps[:, 2, DE:2 * DE], sil[:, :], ALU.mult).then_inc(hid_ready, 1)

                def keep_turned(n, u):
                    dve.wait_ge(ohT_full, FREE + n * 2 + (u + 1))
                    V.tensor_copy(gsl[0:CAP, u:u + 1], ps[0:CAP, 7, T:T + 1])
                    V.tensor_copy(gsl[CAP:P, u:u + 1], ps[CAP:P, 7, T + 1:T + 2])
                    V.tensor_copy(ohT[:, u, :], ps[:, 7, 0:T]).then_inc(ohT_ready, 1)

                def low_part(n, u):
                    p = n * 2 + u
                    for b in range(2):
                        dve.wait_ge(yh_ready, p * 2 + (b + 1))
                        x = slice(512 * b, 512 * b + 512)
                        V.scalar_tensor_tensor(yl[:, u, x], ps[:, 3 + b, :], gsl[:, u:u + 1], yh[:, u, x].bitcast(F32),
                                               ALU.mult, ALU.subtract).then_inc(yl_ready, 1)

                def add_output(n):
                    dve.wait_ge(c_added, FREE + n * KC)
                    for c in range(KC):
                        dve.wait_ge(c_full, FREE + n * KC + (c + 1))
                        V.tensor_tensor(ffT[:, c, :], ps[:, 5 + c % 2, 0:T], ffT[:, c, :], ALU.add).then_inc(c_added, 1)

                def quad(n, i, first=False, last=False, hidden0=True):
                    if hidden0:
                        hidden(n, 0)
                    if not first:
                        add_output(n - 1)
                    keep_turned(n, 0)
                    keep_turned(n, 1)
                    if not last:
                        one_hot(n + 1, i + 1)
                    low_part(n, 0)
                    hidden(n, 1)
                    low_part(n, 1)

                def meanwhile():
                    link(V.tensor_reduce(rs[:, 4:5], ps[:, 3, NT * NE:(NT + 1) * NE], AX_X, ALU.max))
                    link(V.tensor_scalar(rt[:, 0, 0:MAX_ROUNDS - 1], C["thr"], rs[:, 4:5], None, ALU.is_lt))
                    link(V.tensor_reduce(rs[:, 5:6], rt[:, 0, 0:MAX_ROUNDS - 1], AX_X, ALU.add))
                    V.tensor_scalar(rounds[:, 0:1], rs[:, 5:6], 1.0, None, ALU.add).then_inc(rounds_set, 1)
                    dve.wait_ge(rounds_set, L + 1)
                    dve.wait_ge(sh_ready, L * 2 + 2)
                    for m in range(ME):
                        dve.wait_ge(sh_silu, L * ME + m + 1)
                        V.tensor_tensor(hs[:, m, :], ps[:, 6 + m, 0:T], hs[:, m, :], ALU.mult).then_inc(sh_hid, 1)
                    hidden(q, 0)
                    for c in range(KC):
                        bank = z_item(L, Z_SH2 + c)
                        V.scalar_tensor_tensor(ffT[:, c, :], xT[:, c, :], alpha, bank[:, 0:T], ALU.mult, ALU.add)\
                            .then_inc(z_free[c % 2], 1)
                    for b in range(2):
                        dve.wait_ge(z_free[b], z_count(L, Z_SH2 + KC))

                def round_of(q, first=False):
                    one_hot(q, 0)
                    if first:
                        meanwhile()
                    quad(q, 0, first=True, hidden0=not first)
                    with dve.Fori(1, NQUAD - 1) as i:
                        quad(q + i, i)
                    quad(q + (NQUAD - 1), NQUAD - 1, last=True)
                    add_output(q + (NQUAD - 1))
                    V.tensor_scalar(iota[:, :], iota[:, :], float(CAP), None, ALU.add).then_inc(next_round, NQUAD)
                    dve.wait_ge(next_round, q + NQUAD)
                    dve.reg_add(done, done, NQUAD)

                q = dve.snap(done)
                round_of(q, first=True)
                dve.wait_ge(rounds_set, L + 1)
                carry_wait(dve)
                nr = dve.value_load(rounds[0:1, 0:1], min_val=1, max_val=MAX_ROUNDS)
                dve.reg_mov(rounds_reg, nr)
                with dve.If_ne(rounds_reg, 1), dve.Fori(1, nr):
                    round_of(dve.snap(done))

                stats(L, 1, LN_EPS)
                norm_back(L, V_G2, V_B2, Z_FILL2, split=True)
            assert steps[0] == CH, steps[0]

            for t, (at, n) in enumerate(TOK):
                dve.wait_ge(tok_ps, 2 * depth * 2 * NT + 2 * t + 1)
                V.tensor_copy(tok[0:n, t, 0:512], ps[0:n, 2 + 2 * t, :]).then_inc(y_rows, 1)



def _constants():
    import numpy as np

    f = np.float32
    c = np.zeros((P, NCONST), f)
    put = lambda k, x: c.__setitem__((slice(None), slice(C_AT[k], C_AT[k] + CONSTS[k])), x)
    row, col = np.arange(P)[:, None], np.arange(P)[None, :]
    put("ident", row == col)
    put("upper", row < col)
    put("ones", 1.0)
    q, kw = row // CHUNK, np.arange(TP)[None, :] // CHUNK
    wide = np.where((kw <= q + 2) & (kw >= q), 0.0, -BIG)
    narrow = np.where(col // CHUNK <= q, 0.0, -BIG)
    put("mask", np.concatenate([wide, narrow], 1))
    half = HD // 2
    inv = np.power(f(10000.0), -np.arange(half, dtype=f) / f(half)).astype(f)
    pos = np.concatenate([np.arange(TP), PAST + np.arange(TS)]).astype(f)
    ang = (pos[None, :] * inv[np.arange(P) % half][:, None]).astype(f)
    put("cos", np.cos(ang))
    put("sin", np.where(row % HD < half, 1.0, -1.0) * np.sin(ang))
    put("iota", np.arange(QUAD * CAP)[None, :] % CAP)
    put("pads", np.array([[4e30, 3e30, 2e30, 1e30]]))
    put("thr", CAP * np.arange(1, MAX_ROUNDS)[None, :])
    rows = np.stack([np.arange(P) < n for _, n in TOK], 1)
    put("valid", rows)
    put("blank", ~rows)
    return c


def kernel(**inputs):
    import numpy as np
    import concourse.bacc as bacc
    from concourse.bass_utils import run_bass_kernel_spmd as run

    arrays = {k: np.ascontiguousarray(a) for k, a in inputs.items()}
    arrays["consts"] = _constants()
    depth = arrays["w_in"].shape[0]
    nc = bacc.Bacc("TRN2", target_bir_lowering=False, num_devices=1)
    inp = {k: nc.dram_tensor("in_" + k, a.shape, mybir.dt.from_np(a.dtype), kind="ExternalInput").ap() for k, a in arrays.items()}
    kv = lambda t: (depth, 1, t, NKV, HD)
    shapes = {"y_prompt": (1, TP, D), "y_sample": (1, TS, D), "k_prompt": kv(WIN), "v_prompt": kv(WIN), "h_prompt": (depth, 1, D),
              "conv_prompt": (depth, 1, CONV_W - 1, D), "k_sample": kv(TS), "v_sample": kv(TS), "h_sample": (depth, 1, D),
              "conv_sample": (depth, 1, CONV_W - 1, D)}
    out = {k: nc.dram_tensor("out_" + k, s, F32, kind="ExternalOutput").ap() for k, s in shapes.items()}
    build(nc, inp, out, depth, float((2 * depth) ** 0.25))
    r = run(nc, [{"in_" + k: a for k, a in arrays.items()}], core_ids=[0])
    return tuple(r.results[0]["out_" + k] for k in shapes)
```
